# Optimizing a Trainium2 kernel written in Bass

```python
import math
import jax, jax.numpy as jnp
from jax import lax
import numpy as np

D_MODEL = 1024
BATCH = 1
SEQ = 256
DEPTH = 2

HEAD_DIM = 64
HEADS_PER_GROUP = 8
DILATION_GROUPS = ((128, 1), (512, 4), (2048, 16))
N_GROUPS = len(DILATION_GROUPS)
ATTN_WIDTH = N_GROUPS * HEADS_PER_GROUP * HEAD_DIM
ATTN_OUT_WIDTH = HEADS_PER_GROUP * HEAD_DIM
CONV_CH = D_MODEL
CONV_WIDTH = 31
D_FF = ((8 * D_MODEL // 3 + 255) // 256) * 256
IN_WIDTH = 3 * ATTN_WIDTH + 2 * CONV_CH + 2 * D_MODEL
ROPE_THETA = 10000.0
Q_BLOCK = 128
EPS = 1e-6
NEG = -1e30


def rmsnorm(x, g):
    xf = x.astype(jnp.float32)
    y = xf * lax.rsqrt(jnp.mean(xf * xf, axis=-1, keepdims=True) + EPS)
    return (y * g.astype(jnp.float32)).astype(x.dtype)

def swiglu_ffn(h, w_up, w_down):
    a, b = jnp.split(h @ w_up, 2, axis=-1)
    return (jax.nn.silu(a) * b) @ w_down

def rope_tables(seq):
    pos = jnp.arange(seq, dtype=jnp.float32)
    inv = ROPE_THETA ** (-jnp.arange(0, HEAD_DIM, 2, dtype=jnp.float32) / HEAD_DIM)
    ang = pos[:, None] * inv[None, :]
    return jnp.cos(ang), jnp.sin(ang)

def apply_rope(t, cos, sin):
    tf = t.astype(jnp.float32)
    t1, t2 = jnp.split(tf, 2, axis=-1)
    c = cos[:, None, None, :]
    s = sin[:, None, None, :]
    return jnp.concatenate([t1 * c - t2 * s, t1 * s + t2 * c], axis=-1).astype(t.dtype)

def dilated_window_attn(q, k, v, dil, w_sub):
    B, S, H, Dh = q.shape
    L = S // dil
    qb_size = min(Q_BLOCK, L)
    nb = -(-L // qb_size)
    Lp = nb * qb_size
    kb_size = qb_size + 2 * w_sub

    def to_sub(t):
        return t.reshape(B, L, dil, H, Dh).transpose(0, 2, 1, 3, 4)

    qs, ks, vs = to_sub(q), to_sub(k), to_sub(v)
    qs = jnp.pad(qs, ((0, 0), (0, 0), (0, Lp - L), (0, 0), (0, 0)))
    kpad = ((0, 0), (0, 0), (w_sub, w_sub + Lp - L), (0, 0), (0, 0))
    ks = jnp.pad(ks, kpad)
    vs = jnp.pad(vs, kpad)

    qblk = qs.reshape(B, dil, nb, qb_size, H, Dh)
    key_idx = jnp.arange(nb)[:, None] * qb_size + jnp.arange(kb_size)[None, :]
    kblk = ks[:, :, key_idx]
    vblk = vs[:, :, key_idx]

    scores = jnp.einsum('brnqhd,brnkhd->brnhqk', qblk, kblk,
                        preferred_element_type=jnp.float32) * (1.0 / math.sqrt(Dh))
    qpos = jnp.arange(nb)[:, None] * qb_size + jnp.arange(qb_size)[None, :]
    kpos = key_idx - w_sub
    valid = (jnp.abs(qpos[:, :, None] - kpos[:, None, :]) <= w_sub) \
        & (kpos[:, None, :] >= 0) & (kpos[:, None, :] < L)
    scores = jnp.where(valid[None, None, :, None], scores, NEG)

    m = jnp.max(scores, axis=-1, keepdims=True)
    p = jnp.exp(scores - m)
    denom = jnp.sum(p, axis=-1)
    out = jnp.einsum('brnhqk,brnkhd->brnqhd', p, vblk.astype(jnp.float32))
    out = out / jnp.moveaxis(denom, -1, -2)[..., None]
    lse = jnp.moveaxis(m[..., 0] + jnp.log(denom), -1, -2)

    out = out.reshape(B, dil, Lp, H, Dh)[:, :, :L].transpose(0, 2, 1, 3, 4).reshape(B, S, H, Dh)
    lse = lse.reshape(B, dil, Lp, H)[:, :, :L].transpose(0, 2, 1, 3).reshape(B, S, H)
    return out.astype(v.dtype), lse

def conv_module(glu_in, conv_w, conv_b, ln_g, ln_b, w_proj, b_proj):
    a, g = jnp.split(glu_in, 2, axis=-1)
    u = a * jax.nn.sigmoid(g)
    u = lax.conv_general_dilated(
        u, conv_w[:, None, :].astype(u.dtype), window_strides=(1,),
        padding=[(CONV_WIDTH // 2, CONV_WIDTH // 2)],
        dimension_numbers=('NWC', 'WIO', 'NWC'),
        feature_group_count=CONV_CH) + conv_b
    uf = u.astype(jnp.float32)
    mu = jnp.mean(uf, axis=-1, keepdims=True)
    var = jnp.mean(jnp.square(uf - mu), axis=-1, keepdims=True)
    u = ((uf - mu) * lax.rsqrt(var + EPS) * ln_g.astype(jnp.float32)
         + ln_b.astype(jnp.float32)).astype(u.dtype)
    return jax.nn.silu(u) @ w_proj + b_proj

def mixer(h, w_in, b_in, q_norm, k_norm, w_attn_proj, conv_w, conv_b, conv_ln_g,
          conv_ln_b, w_conv_proj, b_conv_proj, w_out, cos, sin):
    B, S, _ = h.shape
    z = h @ w_in + b_in
    q, k, v, glu_in, gates = jnp.split(
        z, [ATTN_WIDTH, 2 * ATTN_WIDTH, 3 * ATTN_WIDTH, 3 * ATTN_WIDTH + 2 * CONV_CH], axis=-1)
    shp = (B, S, N_GROUPS, HEADS_PER_GROUP, HEAD_DIM)
    q = apply_rope(rmsnorm(q.reshape(shp), q_norm[:, None, :]), cos, sin)
    k = apply_rope(rmsnorm(k.reshape(shp), k_norm[:, None, :]), cos, sin)
    v = v.reshape(shp)

    outs, lses = [], []
    for g, (window, dil) in enumerate(DILATION_GROUPS):
        o, l = dilated_window_attn(q[:, :, g], k[:, :, g], v[:, :, g], dil, window // (2 * dil))
        outs.append(o)
        lses.append(l)
    wts = jax.nn.softmax(jnp.stack(lses, axis=0), axis=0)
    y_attn = jnp.sum(wts[..., None] * jnp.stack(outs, axis=0).astype(jnp.float32), axis=0)
    y_attn = y_attn.astype(h.dtype).reshape(B, S, ATTN_OUT_WIDTH) @ w_attn_proj

    y_conv = conv_module(glu_in, conv_w, conv_b, conv_ln_g, conv_ln_b, w_conv_proj, b_conv_proj)

    g_attn, g_conv = jnp.split(jax.nn.sigmoid(gates), 2, axis=-1)
    return (g_attn * y_attn + g_conv * y_conv) @ w_out

def first_inputs(seed: int = 0) -> dict:
    key = jax.random.key(seed)
    ks = jax.random.split(key, 24)
    f32 = jnp.float32
    L = DEPTH

    def w(k, shape, fan_in):
        return jax.random.normal(k, shape, f32) * (fan_in ** -0.5)

    def gain(k, shape):
        return 1.0 + 0.02 * jax.random.normal(k, shape, f32)

    def bias(k, shape):
        return 0.02 * jax.random.normal(k, shape, f32)

    return {
        "x": jax.random.normal(ks[0], (BATCH, SEQ, D_MODEL), f32),
        "ffn1_norm": gain(ks[1], (L, D_MODEL)),
        "ffn1_w_up": w(ks[2], (L, D_MODEL, 2 * D_FF), D_MODEL),
        "ffn1_w_down": w(ks[3], (L, D_FF, D_MODEL), D_FF),
        "mix_norm": gain(ks[4], (L, D_MODEL)),
        "w_in": w(ks[5], (L, D_MODEL, IN_WIDTH), D_MODEL),
        "b_in": bias(ks[6], (L, IN_WIDTH)),
        "q_norm": gain(ks[7], (L, N_GROUPS, HEAD_DIM)),
        "k_norm": gain(ks[8], (L, N_GROUPS, HEAD_DIM)),
        "w_attn_proj": w(ks[9], (L, ATTN_OUT_WIDTH, D_MODEL), ATTN_OUT_WIDTH),
        "conv_w": w(ks[10], (L, CONV_WIDTH, CONV_CH), CONV_WIDTH),
        "conv_b": bias(ks[11], (L, CONV_CH)),
        "conv_ln_g": gain(ks[12], (L, CONV_CH)),
        "conv_ln_b": bias(ks[13], (L, CONV_CH)),
        "w_conv_proj": w(ks[14], (L, CONV_CH, D_MODEL), CONV_CH),
        "b_conv_proj": bias(ks[15], (L, D_MODEL)),
        "w_out": w(ks[16], (L, D_MODEL, D_MODEL), D_MODEL),
        "ffn2_norm": gain(ks[17], (L, D_MODEL)),
        "ffn2_w_up": w(ks[18], (L, D_MODEL, 2 * D_FF), D_MODEL),
        "ffn2_w_down": w(ks[19], (L, D_FF, D_MODEL), D_FF),
        "final_norm": gain(ks[20], (L, D_MODEL)),
    }

def first_block(x, ffn1_norm, ffn1_w_up, ffn1_w_down, mix_norm, w_in, b_in, q_norm, k_norm,
              w_attn_proj, conv_w, conv_b, conv_ln_g, conv_ln_b, w_conv_proj, b_conv_proj,
              w_out, ffn2_norm, ffn2_w_up, ffn2_w_down, final_norm):
    cos, sin = rope_tables(x.shape[1])
    for l in range(DEPTH):
        x = x + 0.5 * swiglu_ffn(rmsnorm(x, ffn1_norm[l]), ffn1_w_up[l], ffn1_w_down[l])
        x = x + mixer(rmsnorm(x, mix_norm[l]), w_in[l], b_in[l], q_norm[l], k_norm[l],
                      w_attn_proj[l], conv_w[l], conv_b[l], conv_ln_g[l], conv_ln_b[l],
                      w_conv_proj[l], b_conv_proj[l], w_out[l], cos, sin)
        x = x + 0.5 * swiglu_ffn(rmsnorm(x, ffn2_norm[l]), ffn2_w_up[l], ffn2_w_down[l])
        x = rmsnorm(x, final_norm[l])
    return x


RNN_WIDTH = 1024
RNN_BLOCKS = 16
RNN_CONV = 4
LRU_C = 8.0
NSA_HEADS = 16
NSA_KV_HEADS = 4
GQA_REP = NSA_HEADS // NSA_KV_HEADS
CMP_BLOCK = 32
CMP_STRIDE = 16
CMP_HIDDEN = 128
SLC_BLOCK = 64
SLC_TOPK = 4
WINDOW = 256
Q_CHUNK = 64
FORCE_BONUS = 1.0e4
ROPE_THETA_2 = 500000.0
ROPE_DIM = HEAD_DIM // 4
SC_WIDTH = D_MODEL
SC_CONV = 3
D_FF_2 = 2816
FFN_CONV = 3
NEG_2 = -1e30

AB_SPLITS = (RNN_WIDTH, RNN_WIDTH, NSA_HEADS * HEAD_DIM) + (NSA_KV_HEADS * HEAD_DIM,) * 6 + (3 * NSA_HEADS,)
AB_IN = sum(AB_SPLITS)
AB_MIX = RNN_WIDTH + NSA_HEADS * HEAD_DIM


def rms_norm(x, g):
    xf = x.astype(jnp.float32)
    y = xf * lax.rsqrt(jnp.mean(xf * xf, axis=-1, keepdims=True) + EPS)
    return (y * g.astype(jnp.float32)).astype(x.dtype)

def causal_dwconv(x, w, b):
    K, C = w.shape
    y = lax.conv_general_dilated(x, w[:, None, :].astype(x.dtype), window_strides=(1,),
                                 padding=[(K - 1, 0)], dimension_numbers=('NWC', 'WIO', 'NWC'),
                                 feature_group_count=C)
    return y + b.astype(x.dtype)

def rope_partial(x, pos):
    half = ROPE_DIM // 2
    inv = jnp.power(jnp.float32(ROPE_THETA_2), -jnp.arange(half, dtype=jnp.float32) / half)
    ang = pos.astype(jnp.float32)[:, None] * inv[None, :]
    cos = jnp.cos(ang)[None, :, None, :]
    sin = jnp.sin(ang)[None, :, None, :]
    x1 = x[..., :half].astype(jnp.float32)
    x2 = x[..., half:ROPE_DIM].astype(jnp.float32)
    rot = jnp.concatenate([x1 * cos - x2 * sin, x2 * cos + x1 * sin], axis=-1).astype(x.dtype)
    return jnp.concatenate([rot, x[..., ROPE_DIM:]], axis=-1)

def rg_lru(x, w_r, b_r, w_i, b_i, lam):
    Bsz, T, W = x.shape
    xb = x.reshape(Bsz, T, RNN_BLOCKS, W // RNN_BLOCKS)
    r = jax.nn.sigmoid(jnp.einsum('btnc,ncd->btnd', xb, w_r).reshape(Bsz, T, W) + b_r)
    i = jax.nn.sigmoid(jnp.einsum('btnc,ncd->btnd', xb, w_i).reshape(Bsz, T, W) + b_i)
    log_a = -LRU_C * r.astype(jnp.float32) * jax.nn.softplus(-lam.astype(jnp.float32))
    a = jnp.exp(log_a)
    u = jnp.sqrt(-jnp.expm1(2.0 * log_a)) * (i * x).astype(jnp.float32)

    def combine(left, right):
        a1, b1 = left
        a2, b2 = right
        return a1 * a2, a2 * b1 + b2

    _, h = lax.associative_scan(combine, (a, u), axis=1)
    return h.astype(x.dtype)

def compress(t, pe, w1, w2):
    Bsz, T, G, hd = t.shape
    n_cmp = (T - CMP_BLOCK) // CMP_STRIDE + 1
    idx = np.arange(n_cmp)[:, None] * CMP_STRIDE + np.arange(CMP_BLOCK)[None, :]
    blk = t[:, idx] + pe[:, None, :].astype(t.dtype)
    blk = blk.transpose(0, 1, 3, 2, 4).reshape(Bsz, n_cmp, G, CMP_BLOCK * hd)
    return jax.nn.gelu(blk @ w1) @ w2, idx[:, -1]

def nsa(q, kc, vc, ks, vs, kw, vw, gate_logits, pe_k, pe_v, wk1, wk2, wv1, wv2):
    Bsz, T = q.shape[:2]
    G, R, hd = NSA_KV_HEADS, GQA_REP, HEAD_DIM
    scale = HEAD_DIM ** -0.5
    pos = jnp.arange(T)
    q_rot = rope_partial(q, pos)
    ks = rope_partial(ks, pos)
    kw = rope_partial(kw, pos)
    k_cmp, cmp_end = compress(kc, pe_k, wk1, wk2)
    v_cmp, _ = compress(vc, pe_v, wv1, wv2)
    n_cmp = k_cmp.shape[1]
    cmp_end = jnp.asarray(cmp_end)
    n_slc = T // SLC_BLOCK
    k_sel = min(SLC_TOPK, n_slc)
    cs = np.arange(n_cmp) * CMP_STRIDE
    js = np.arange(n_slc) * SLC_BLOCK
    overlap = jnp.asarray(((cs[:, None] < js[None, :] + SLC_BLOCK) &
                           (cs[:, None] + CMP_BLOCK > js[None, :])).astype(np.float32))
    ksb = ks.reshape(Bsz, n_slc, SLC_BLOCK, G, hd).transpose(0, 3, 1, 2, 4)
    vsb = vs.reshape(Bsz, n_slc, SLC_BLOCK, G, hd).transpose(0, 3, 1, 2, 4)
    kwp = jnp.pad(kw, ((0, 0), (WINDOW, 0), (0, 0), (0, 0)))
    vwp = jnp.pad(vw, ((0, 0), (WINDOW, 0), (0, 0), (0, 0)))
    bi = jnp.arange(Bsz)[:, None, None, None]
    gi = jnp.arange(G)[None, :, None, None]
    blk_ids = jnp.arange(n_slc)
    f32 = jnp.float32

    def chunk(args):
        qn, qr, gt, s = args
        t = s + jnp.arange(Q_CHUNK)
        qn5 = qn.reshape(Bsz, Q_CHUNK, G, R, hd)
        qr5 = qr.reshape(Bsz, Q_CHUNK, G, R, hd)
        sc = jnp.einsum('bqgrd,bngd->bgrqn', qn5, k_cmp, preferred_element_type=f32) * scale
        mask_c = cmp_end[None, :] <= t[:, None]
        p_c = jnp.where(mask_c, jax.nn.softmax(jnp.where(mask_c, sc, NEG_2), axis=-1), 0.0)
        o_c = jnp.einsum('bgrqn,bngd->bqgrd', p_c.astype(v_cmp.dtype), v_cmp, preferred_element_type=f32)
        imp = jnp.einsum('bgrqn,nj->bgqj', p_c, overlap)
        forced = (blk_ids[None, :] == 0) | (blk_ids[None, :] == (t // SLC_BLOCK)[:, None])
        imp = jnp.where(forced, imp + FORCE_BONUS, imp)
        imp = jnp.where(blk_ids[None, :] * SLC_BLOCK <= t[:, None], imp, NEG_2)
        _, sel = lax.top_k(imp, k_sel)
        kg = ksb[bi, gi, sel]
        vg = vsb[bi, gi, sel]
        ss = jnp.einsum('bqgrd,bgqkld->bgrqkl', qr5, kg, preferred_element_type=f32) * scale
        tok = sel[..., None] * SLC_BLOCK + jnp.arange(SLC_BLOCK)
        mask_s = (tok <= t[None, None, :, None, None])[:, :, None]
        ss = jnp.where(mask_s, ss, NEG_2)
        p_s = jax.nn.softmax(ss.reshape(ss.shape[:4] + (k_sel * SLC_BLOCK,)), axis=-1).reshape(ss.shape)
        o_s = jnp.einsum('bgrqkl,bgqkld->bqgrd', p_s.astype(vg.dtype), vg, preferred_element_type=f32)
        kwin = lax.dynamic_slice_in_dim(kwp, s, WINDOW + Q_CHUNK, axis=1)
        vwin = lax.dynamic_slice_in_dim(vwp, s, WINDOW + Q_CHUNK, axis=1)
        j = s - WINDOW + jnp.arange(WINDOW + Q_CHUNK)
        mask_w = (j[None, :] <= t[:, None]) & (j[None, :] > t[:, None] - WINDOW) & (j[None, :] >= 0)
        sw = jnp.einsum('bqgrd,bjgd->bgrqj', qr5, kwin, preferred_element_type=f32) * scale
        p_w = jax.nn.softmax(jnp.where(mask_w, sw, NEG_2), axis=-1)
        o_w = jnp.einsum('bgrqj,bjgd->bqgrd', p_w.astype(vwin.dtype), vwin, preferred_element_type=f32)
        g = jax.nn.sigmoid(gt.astype(f32)).reshape(Bsz, Q_CHUNK, G, R, 3)
        o = g[..., 0:1] * o_c + g[..., 1:2] * o_s + g[..., 2:3] * o_w
        return o.reshape(Bsz, Q_CHUNK, NSA_HEADS * hd).astype(q.dtype)

    n_chunk = T // Q_CHUNK
    to_chunks = lambda a: a.reshape((Bsz, n_chunk, Q_CHUNK) + a.shape[2:]).swapaxes(0, 1)
    starts = jnp.arange(n_chunk) * Q_CHUNK
    out = lax.map(chunk, (to_chunks(q), to_chunks(q_rot), to_chunks(gate_logits), starts))
    return out.swapaxes(0, 1).reshape(Bsz, T, NSA_HEADS * hd)

def mixer_ab(h, w_in, conv_w, conv_b, w_r, b_r, w_i, b_i, lam, pe_k, pe_v, wk1, wk2, wv1, wv2, w_out):
    Bsz, T, _ = h.shape
    splits = np.cumsum(AB_SPLITS)[:-1].tolist()
    xr, gr, q, kc, vc, ks, vs, kw, vw, gl = jnp.split(h @ w_in, splits, axis=-1)
    y_rnn = rg_lru(causal_dwconv(xr, conv_w, conv_b), w_r, b_r, w_i, b_i, lam) * jax.nn.gelu(gr)
    kv = lambda a: a.reshape(Bsz, T, NSA_KV_HEADS, HEAD_DIM)
    y_att = nsa(q.reshape(Bsz, T, NSA_HEADS, HEAD_DIM), kv(kc), kv(vc), kv(ks), kv(vs), kv(kw), kv(vw),
                gl.reshape(Bsz, T, NSA_HEADS, 3), pe_k, pe_v, wk1, wk2, wv1, wv2)
    return jnp.concatenate([y_rnn, y_att], axis=-1) @ w_out

def mixer_c(h, w_in, conv_w, conv_b, w_out):
    bg, cg, v = jnp.split(h @ w_in, 3, axis=-1)
    return (bg * causal_dwconv(cg * v, conv_w, conv_b)) @ w_out

def conv_ffn(h, w_gate, w_up, conv_w, conv_b, w_down):
    g = causal_dwconv(h @ w_gate, conv_w, conv_b)
    return (jax.nn.silu(g) * (h @ w_up)) @ w_down

def second_inputs(seed: int = 0) -> dict:
    key = jax.random.key(seed)
    keys = iter(jax.random.split(key, 48))
    NE = (DEPTH + 1) // 2
    NO = DEPTH // 2
    f32 = jnp.float32

    def w(shape, fan_in, scale=1.0):
        return jax.random.normal(next(keys), shape, f32) * (scale * fan_in ** -0.5)

    def small(shape):
        return 0.02 * jax.random.normal(next(keys), shape, f32)

    def gain(shape):
        return 1.0 + small(shape)

    x = jax.random.normal(next(keys), (BATCH, SEQ, D_MODEL), f32)
    c = jax.random.normal(next(keys), (BATCH, D_MODEL), f32)
    a_target = jax.random.uniform(next(keys), (NE, RNN_WIDTH), f32, 0.9, 0.999)
    s = a_target ** (1.0 / LRU_C)
    lam = jnp.log(s) - jnp.log1p(-s)
    bw = RNN_WIDTH // RNN_BLOCKS
    return {
        'x': x,
        'c': c,
        'mod_w': w((DEPTH, D_MODEL, 6 * D_MODEL), D_MODEL, 0.5),
        'mod_b': small((DEPTH, 6 * D_MODEL)),
        'norm_mix_pre': gain((DEPTH, D_MODEL)),
        'norm_mix_post': gain((DEPTH, D_MODEL)),
        'norm_ffn_pre': gain((DEPTH, D_MODEL)),
        'norm_ffn_post': gain((DEPTH, D_MODEL)),
        'ab_w_in': w((NE, D_MODEL, AB_IN), D_MODEL),
        'ab_conv_w': w((NE, RNN_CONV, RNN_WIDTH), RNN_CONV),
        'ab_conv_b': small((NE, RNN_WIDTH)),
        'lru_w_r': w((NE, RNN_BLOCKS, bw, bw), bw),
        'lru_b_r': small((NE, RNN_WIDTH)),
        'lru_w_i': w((NE, RNN_BLOCKS, bw, bw), bw),
        'lru_b_i': small((NE, RNN_WIDTH)),
        'lru_lam': lam,
        'cmp_pe_k': small((NE, CMP_BLOCK, HEAD_DIM)),
        'cmp_pe_v': small((NE, CMP_BLOCK, HEAD_DIM)),
        'cmp_wk1': w((NE, CMP_BLOCK * HEAD_DIM, CMP_HIDDEN), CMP_BLOCK * HEAD_DIM),
        'cmp_wk2': w((NE, CMP_HIDDEN, HEAD_DIM), CMP_HIDDEN),
        'cmp_wv1': w((NE, CMP_BLOCK * HEAD_DIM, CMP_HIDDEN), CMP_BLOCK * HEAD_DIM),
        'cmp_wv2': w((NE, CMP_HIDDEN, HEAD_DIM), CMP_HIDDEN),
        'ab_w_out': w((NE, AB_MIX, D_MODEL), AB_MIX),
        'sc_w_in': w((NO, D_MODEL, 3 * SC_WIDTH), D_MODEL),
        'sc_conv_w': w((NO, SC_CONV, SC_WIDTH), SC_CONV),
        'sc_conv_b': small((NO, SC_WIDTH)),
        'sc_w_out': w((NO, SC_WIDTH, D_MODEL), SC_WIDTH),
        'ffn_w_gate': w((DEPTH, D_MODEL, D_FF_2), D_MODEL),
        'ffn_w_up': w((DEPTH, D_MODEL, D_FF_2), D_MODEL),
        'ffn_conv_w': w((DEPTH, FFN_CONV, D_FF_2), FFN_CONV),
        'ffn_conv_b': small((DEPTH, D_FF_2)),
        'ffn_w_down': w((DEPTH, D_FF_2, D_MODEL), D_FF_2),
    }

def second_block(x, c, mod_w, mod_b, norm_mix_pre, norm_mix_post, norm_ffn_pre, norm_ffn_post,
              ab_w_in, ab_conv_w, ab_conv_b, lru_w_r, lru_b_r, lru_w_i, lru_b_i, lru_lam,
              cmp_pe_k, cmp_pe_v, cmp_wk1, cmp_wk2, cmp_wv1, cmp_wv2, ab_w_out,
              sc_w_in, sc_conv_w, sc_conv_b, sc_w_out,
              ffn_w_gate, ffn_w_up, ffn_conv_w, ffn_conv_b, ffn_w_down):
    c_act = jax.nn.silu(c)
    for i in range(DEPTH):
        mod = c_act @ mod_w[i] + mod_b[i]
        sh_m, sc_m, g_m, sh_f, sc_f, g_f = jnp.split(mod[:, None, :], 6, axis=-1)
        h = rms_norm(x, norm_mix_pre[i]) * (1.0 + sc_m) + sh_m
        if i % 2 == 0:
            e = i // 2
            y = mixer_ab(h, ab_w_in[e], ab_conv_w[e], ab_conv_b[e], lru_w_r[e], lru_b_r[e],
                         lru_w_i[e], lru_b_i[e], lru_lam[e], cmp_pe_k[e], cmp_pe_v[e],
                         cmp_wk1[e], cmp_wk2[e], cmp_wv1[e], cmp_wv2[e], ab_w_out[e])
        else:
            o = i // 2
            y = mixer_c(h, sc_w_in[o], sc_conv_w[o], sc_conv_b[o], sc_w_out[o])
        x = x + (1.0 + g_m) * rms_norm(y, norm_mix_post[i])
        h = rms_norm(x, norm_ffn_pre[i]) * (1.0 + sc_f) + sh_f
        y = conv_ffn(h, ffn_w_gate[i], ffn_w_up[i], ffn_conv_w[i], ffn_conv_b[i], ffn_w_down[i])
        x = x + (1.0 + g_f) * rms_norm(y, norm_ffn_post[i])
    return x


def setup_inputs(seed=0):
    out = dict(first_inputs(seed))
    for name, value in second_inputs(seed + 1).items():
        if name != "x":
            out[name + "_2"] = value
    return out


def reference(
    x, ffn1_norm, ffn1_w_up, ffn1_w_down, mix_norm, w_in, b_in, q_norm, k_norm, w_attn_proj,
    conv_w, conv_b, conv_ln_g, conv_ln_b, w_conv_proj, b_conv_proj, w_out, ffn2_norm, ffn2_w_up,
    ffn2_w_down, final_norm, c_2, mod_w_2, mod_b_2, norm_mix_pre_2, norm_mix_post_2,
    norm_ffn_pre_2, norm_ffn_post_2, ab_w_in_2, ab_conv_w_2, ab_conv_b_2, lru_w_r_2, lru_b_r_2,
    lru_w_i_2, lru_b_i_2, lru_lam_2, cmp_pe_k_2, cmp_pe_v_2, cmp_wk1_2, cmp_wk2_2, cmp_wv1_2,
    cmp_wv2_2, ab_w_out_2, sc_w_in_2, sc_conv_w_2, sc_conv_b_2, sc_w_out_2, ffn_w_gate_2,
    ffn_w_up_2, ffn_conv_w_2, ffn_conv_b_2, ffn_w_down_2,
):
    x = first_block(
        x, ffn1_norm, ffn1_w_up, ffn1_w_down, mix_norm, w_in, b_in, q_norm, k_norm, w_attn_proj,
        conv_w, conv_b, conv_ln_g, conv_ln_b, w_conv_proj, b_conv_proj, w_out, ffn2_norm,
        ffn2_w_up, ffn2_w_down, final_norm,
    )
    return second_block(
        x, c_2, mod_w_2, mod_b_2, norm_mix_pre_2, norm_mix_post_2, norm_ffn_pre_2,
        norm_ffn_post_2, ab_w_in_2, ab_conv_w_2, ab_conv_b_2, lru_w_r_2, lru_b_r_2, lru_w_i_2,
        lru_b_i_2, lru_lam_2, cmp_pe_k_2, cmp_pe_v_2, cmp_wk1_2, cmp_wk2_2, cmp_wv1_2,
        cmp_wv2_2, ab_w_out_2, sc_w_in_2, sc_conv_w_2, sc_conv_b_2, sc_w_out_2, ffn_w_gate_2,
        ffn_w_up_2, ffn_conv_w_2, ffn_conv_b_2, ffn_w_down_2,
    )


_drawn_inputs = setup_inputs


def setup_inputs(seed=0):
    import zlib

    import numpy as np

    out = dict(_drawn_inputs(seed))
    spreads = {}
    factors = {'ffn1_norm': 2.679,
     'mix_norm': 3.199,
     'q_norm': 8.0,
     'k_norm': 8.0,
     'conv_ln_g': 2.694,
     'ffn2_norm': 3.201,
     'norm_ffn_post_2': 3.105,
     'lru_b_r_2': 8.0,
     'lru_b_i_2': 8.0,
     'cmp_pe_k_2': 45.493,
     'cmp_pe_v_2': 8.0,
     'sc_conv_b_2': 6.031,
     'ffn_conv_b_2': 3.492}
    for name, (base, spread) in spreads.items():
        noise = np.random.default_rng([zlib.crc32(name.encode()), seed]).standard_normal(out[name].shape)
        drawn = base * np.exp(spread * noise) if base else spread * noise
        out[name] = __import__('jax').numpy.asarray(drawn.astype(out[name].dtype))
    for name, factor in factors.items():
        out[name] = (out[name] * factor).astype(out[name].dtype)
    return out
```

```python
import math
from contextlib import ExitStack

import numpy as np
import concourse.bass as bass
from concourse import mybir

ALU = mybir.AluOpType
ACT = mybir.ActivationFunctionType
F32 = mybir.dt.float32
X_AXIS = mybir.AxisListType.X

P = 128
D_MODEL = 1024
SEQ = 256
DEPTH = 2
KT = D_MODEL // P
TT = SEQ // P
D_FF = 2816
FT = D_FF // P
HD = 64
GROUPS = 3
GH = 8
GT = GH * HD // P
QT = GROUPS * GT
CONV_TAPS = 31
CONV_PAD = CONV_TAPS // 2
EPS = 1e-6
NEG = -1e30
NSA_HEADS = 16
NSA_KV = 4
NSA_REP = NSA_HEADS // NSA_KV
NSA_TILES = NSA_HEADS * HD // P
RNN_TAPS = 4
SHORT_TAPS = 3
CMP_BLOCK = 32
CMP_STRIDE = 16
N_CMP = (SEQ - CMP_BLOCK) // CMP_STRIDE + 1
CMP_ROOM = 32
SCALE = 1.0 / math.sqrt(HD)
MOD_PARTS = 6

RING = 6
TILE = KT * P

ONLY_FIRST = False



class Count:

    def __init__(self):
        self.count, self.now, self.per, self.before = {}, None, {}, {}

    def next(self, sem, k=1):
        self.count[sem.name] = n = self.count.get(sem.name, 0) + k
        return n if self.now is None else self.now * self.per[sem.name] + n

    def last(self, sem):
        return self.count[sem.name]

    def skip(self, sem, k):
        self.count[sem.name] = self.count.get(sem.name, 0) + k

    def turn(self, i, per):
        self.now, self.per = i, {sem.name: k for sem, k in per}
        self.before = {name: self.count.get(name, 0) for name in self.per}

    def turned(self, number):
        for name, k in self.per.items():
            asked = self.count.get(name, 0) - self.before[name]
            assert asked == k, (name, asked, k)
            self.count[name] = self.before[name] + k * number
        self.now = None


def vector_columns():
    at, n = {}, 0
    for l in range(DEPTH):
        for name, width in (("ffn1_norm", KT), ("mix_norm", KT), ("ffn2_norm", KT), ("final_norm", KT),
                            ("b_in", 2 * QT + 4 * KT), ("q_gain", GROUPS), ("q_gain_swapped", GROUPS),
                            ("k_gain", GROUPS), ("k_gain_swapped", GROUPS), ("conv_w", KT * CONV_TAPS),
                            ("conv_b", KT), ("conv_ln_g", KT), ("conv_ln_b", KT), ("b_conv_proj", KT),
                            ("mod_b", MOD_PARTS * KT), ("mix_pre", KT), ("mix_post", KT), ("ffn_pre", KT),
                            ("ffn_post", KT), ("ffn_conv_w", FT * SHORT_TAPS), ("ffn_conv_b", FT)):
            at[name, l] = n
            n += width
    for name, width in (("c", KT), ("rnn_conv_w", KT * RNN_TAPS), ("rnn_conv_b", KT), ("b_r", KT), ("b_i", KT),
                        ("lam", KT), ("sc_conv_w", KT * SHORT_TAPS), ("sc_conv_b", KT), ("pe_k", CMP_BLOCK // 2),
                        ("pe_v", CMP_BLOCK // 2), ("wk2", P), ("wv2", HD)):
        at[name, 0] = n
        n += width
    return at, n


VEC, N_VEC = vector_columns()

TABLES, N_TAB = {}, 0
for _name, _width in (("identity", P), ("mean_all", P), ("mean_head", P), ("rot", P), ("rot16", P),
                      ("dup0", P), ("dup1", P), ("rotdup0", P), ("rotdup1", P),
                      ("cos", SEQ), ("sin", SEQ), ("cos16", SEQ), ("sin16", SEQ),
                      ("mask0", 4 * P), ("mask1", 4 * P), ("causal0", P), ("causal1", 2 * P),
                      ("cmp0", N_CMP), ("cmp1", N_CMP), ("seen0", 1), ("seen1", 1),
                      ("own_rep", NSA_REP), ("one", 1), ("eps", 1)):
    TABLES[_name] = (N_TAB, _width)
    N_TAB += _width


def shape_tables():
    t = {}
    eye = np.eye(P, dtype=np.float64)
    t["identity"] = eye
    t["mean_all"] = np.full((P, P), 1.0 / D_MODEL)
    head = np.kron(np.eye(P // HD), np.ones((HD, HD)))
    t["mean_head"] = head / HD

    def rotation(half):
        r = np.zeros((HD, HD))
        for d in range(half):
            r[d + half, d] = -1.0
            r[d, d + half] = 1.0
        return r

    rot, rot16 = rotation(HD // 2), rotation(HD // 8)
    t["rot"] = np.kron(np.eye(2), rot)
    t["rot16"] = np.kron(np.eye(2), rot16)
    for par in range(2):
        pick = np.zeros((2, 1))
        pick[par] = 1.0
        t[f"dup{par}"] = np.kron(pick, np.concatenate([np.eye(HD)] * 2, 1))
        t[f"rotdup{par}"] = np.kron(pick, np.concatenate([rot16] * 2, 1))
    pos = np.arange(SEQ, dtype=np.float32)
    inv = np.float32(10000.0) ** (-np.arange(0, HD, 2, dtype=np.float32) / np.float32(HD))
    ang = (pos[:, None] * inv[None, :]).astype(np.float32).astype(np.float64)
    t["cos"] = np.tile(np.cos(ang).T, (4, 1))
    t["sin"] = np.tile(np.sin(ang).T, (4, 1))
    half = HD // 8
    inv = np.power(np.float32(500000.0), -np.arange(half, dtype=np.float32) / np.float32(half))
    ang = (pos[:, None] * inv[None, :]).astype(np.float32).astype(np.float64)
    c, s = np.ones((HD, SEQ)), np.zeros((HD, SEQ))
    c[:2 * half] = np.tile(np.cos(ang).T, (2, 1))
    s[:2 * half] = np.tile(np.sin(ang).T, (2, 1))
    t["cos16"], t["sin16"] = np.tile(c, (2, 1)), np.tile(s, (2, 1))
    tok = np.arange(SEQ)
    order = tok.reshape(SEQ // 4, 2, 2).transpose(1, 0, 2).reshape(-1)
    for q in range(TT):
        i = order[q * P:(q + 1) * P][:, None]
        own = order[q * P:(q + 1) * P][None, :]
        blocks = []
        for (window, dil), keys in zip(((128, 1), (512, 4), (2048, 16)), (order[None, :], own, own)):
            ok = ((i - keys) % dil == 0) & (np.abs(i - keys) // dil <= window // (2 * dil))
            blocks.append(np.where(ok, 0.0, NEG))
        t[f"mask{q}"] = np.concatenate(blocks, 1)
        i = q * P + np.arange(P)[:, None]
        t[f"causal{q}"] = np.where(np.arange((q + 1) * P)[None, :] <= i, 0.0, NEG)
        end = np.arange(N_CMP)[None, :] * CMP_STRIDE + CMP_BLOCK - 1
        t[f"cmp{q}"] = np.where(end <= i, 0.0, NEG)
        t[f"seen{q}"] = (i >= CMP_BLOCK - 1).astype(np.float64)
    t["own_rep"] = np.kron(np.eye(NSA_REP), np.ones((CMP_ROOM, 1)))
    t["one"] = np.ones((P, 1))
    t["eps"] = np.full((P, 1), EPS)
    return np.concatenate([t[n] for n in TABLES], 1).astype(np.float32)



def build(nc, x_in, weights, vecs_in, tables_in, bv_in, mod_in, out):
    with ExitStack() as ctx:
        def sb(name, *shape):
            return ctx.enter_context(nc.sbuf_tensor(name, [P, *shape], F32))

        def sem(name):
            return ctx.enter_context(nc.semaphore(name))

        x = sb("x", KT, SEQ)
        h = sb("h", KT, SEQ)
        work = sb("work", KT, SEQ)
        work_row = work[:, :, :].rearrange("p k t -> p (k t)")
        rinv = sb("rinv", SEQ)
        ring = sb("ring", RING, TILE)
        vecs = sb("vecs", N_VEC)
        tabs = sb("tabs", N_TAB)
        gate_a = sb("gate_a", 2, SEQ)
        hid = sb("hid", 2, SEQ)
        fpad = sb("fpad", 2, SHORT_TAPS - 1 + SEQ)
        mod_acc = sb("mod_acc", MOD_PARTS * D_MODEL)
        mod_w = sb("mod_w_buf", 2, TILE)
        mod_t = sb("mod_t", TILE)
        modv = sb("modv", DEPTH, MOD_PARTS, KT)
        c_act = sb("c_act", KT)
        decay = sb("decay", KT)
        tiny = sb("tiny", 8, KT)
        nmax = sb("nmax", 2 * TT * NSA_HEADS)
        rsum = sb("rsum", 2 * TT * NSA_HEADS)
        rrec = sb("rrec", 2 * TT * NSA_HEADS)
        ARENA = 22400
        arena = sb("arena", ARENA)
        used = [0]

        def take(*shape):
            n = int(np.prod(shape))
            ap = arena[:, used[0]:used[0] + n]
            used[0] += n
            assert used[0] <= ARENA, used[0]
            if len(shape) == 2:
                return ap.rearrange("p (a b) -> p a b", a=shape[0])
            if len(shape) == 3:
                return ap.rearrange("p (a b c) -> p a b c", a=shape[0], b=shape[1])
            return ap

        upad = take(KT, SEQ + 2 * CONV_PAD)
        conv = take(KT, SEQ)
        qf = take(QT, SEQ)
        kf = take(QT, SEQ)
        vt = take(TT, QT * P)
        gates = take(2 * KT, SEQ)
        z_buf = take(2, 2 * SEQ)
        sq_buf = take(2, 2 * SEQ)
        root_buf = take(2, 2 * SEQ)
        hperm = gates[:, 0:KT, :]
        v_bias = work_row[:, 0:QT * P]
        probs, scores_s, probs_t = sq_buf, root_buf, z_buf
        y_tm = arena[:, 0:TT * GH * HD].rearrange("p (a b) -> p a b", a=TT)
        ya = qf[:, 0:GT, :]

        used[0] = 0
        zk = take(2, 2 * SEQ)
        kcs = take(2, NSA_KV, SEQ)
        xpad = take(KT, RNN_TAPS - 1 + SEQ)
        xc = take(KT, SEQ)
        qn = take(NSA_TILES, SEQ)
        qr = take(NSA_TILES, SEQ)
        kr = take(2, NSA_KV, SEQ)
        gg = take(KT, SEQ)
        vsw = take(2, TT, NSA_KV * HD)
        glog = take(TT, 3 * NSA_HEADS)
        it = take(KT, SEQ)
        th = take(KT, SEQ)
        hk = take(NSA_KV * N_CMP)
        hv = take(NSA_KV * N_CMP)
        hb = take(2)
        hrep = take(NSA_KV, NSA_REP, CMP_ROOM)
        kcmp = take(NSA_KV * N_CMP)
        v4 = take(NSA_KV, NSA_REP, HD)
        xpad_row = xpad.rearrange("p a b -> p (a b)")
        xc_row = xc.rearrange("p a b -> p (a b)")
        den = xpad_row[:, 0:KT * SEQ].rearrange("p (a b) -> p a b", a=KT)
        s2 = xpad_row[:, 0:1024].rearrange("p (a b) -> p a b", a=2)
        p2 = xpad_row[:, 1024:2048].rearrange("p (a b) -> p a b", a=2)
        pt2 = xc_row[:, 0:1024].rearrange("p (a b) -> p a b", a=2)
        pc = xc_row[:, 1024:1536].rearrange("p (a b) -> p a b", a=NSA_HEADS)
        otmp = xc_row[:, 1536:2048]
        pct = work_row[:, 0:512]
        scc = work_row[:, 512:512 + NSA_HEADS * N_CMP].rearrange("p (a b) -> p a b", a=NSA_HEADS)
        rtmp = work_row[:, 1024:2048].rearrange("p (a b) -> p a b", a=2)
        y2t = it.rearrange("p a b -> p (a b)").rearrange("p (a b) -> p a b", a=TT)
        yfm = gg
        yrnn = th
        vpad, vconv = xpad, xc

        bank = [ctx.enter_context(nc.psum_tensor(f"bank{i}", [P, 512], F32)) for i in range(8)]
        UP = 4

        def half(b, k):
            return bank[b][:, k * SEQ:(k + 1) * SEQ]

        def two(ap):
            return ap.rearrange("p (a b) -> p a b", a=2)

        def tab(name):
            at, width = TABLES[name]
            return tabs[:, at:at + width]

        def vec(name, l, k=0, width=1):
            at = VEC[name, l] + k
            return vecs[:, at:at + width]

        def rows(ap, n):
            return ap[:, None, :].broadcast_to([P, n, ap.shape[-1]])

        def cols(ap, n):
            return ap[:, :, None].broadcast_to([P, ap.shape[1], n])

        loaded = sem("inputs_loaded")
        w_full = [sem(f"weight_tile_full{i}") for i in range(RING)]
        w_used = sem("weight_tiles_used")
        pair_full = sem("pair_in_psum")
        pair_free = [sem(f"pair_bank_free{i}") for i in range(2)]
        dve_link = sem("dve_result_written")
        act_link = sem("act_result_written")
        pool_link = sem("pool_result_written")
        sq_ready = sem("squares_ready")
        stat_full = sem("mean_square_in_psum")
        root_ready = sem("root_ready")
        scaled = sem("tile_scaled_by_rinv")
        h_ready = sem("normed_tile_ready")
        x_ready = sem("x_tiles_updated")
        y_pair = sem("mixer_output_pair_taken")
        y_down = sem("ffn_output_bank_taken")
        gate_ready = sem("activated_gate_ready")
        gate_copied = sem("gate_tile_copied")
        gate_convolved = sem("gate_tile_convolved")
        hid_ready = sem("hidden_tile_ready")
        down_full = sem("down_bank_full")
        v_bias_full = sem("v_bias_loaded")
        hperm_ready = sem("h_by_residue_ready")
        hm_full = sem("head_mean_in_psum")
        hm_root = sem("head_root_ready")
        rot_full = sem("rotated_in_psum")
        rot_free = sem("rotation_bank_free")
        qk_ready = sem("q_or_k_pair_ready")
        conv_link = sem("conv_tap_added")
        conv_ready = sem("convolution_ready")
        cmean_full = sem("conv_mean_in_psum")
        centred = sem("conv_centred")
        csq_ready = sem("conv_squares_ready")
        cvar_full = sem("conv_variance_in_psum")
        croot = sem("conv_root_ready")
        cnorm = sem("conv_normed")
        csilu = sem("conv_activated")
        sc_full = sem("scores_in_psum")
        sc_free = sem("scores_taken")
        smax = sem("score_maximum_ready")
        p_ready = sem("probabilities_ready")
        pt_full = sem("probabilities_turned_in_psum")
        pt_ready = sem("probabilities_turned_ready")
        o_full = sem("head_output_in_psum")
        o_free = sem("head_output_taken")
        ytm_ready = sem("attention_rows_ready")
        yt_full = sem("attention_turned_in_psum")
        ya_ready = sem("attention_turned_ready")
        gmix_ready = sem("gated_mix_ready")
        res_pair = sem("residual_pair_added")
        lam_ready = sem("lam_magnitude_ready")
        lam_exp = sem("lam_exponential_ready")
        decay_ready = sem("decay_ready")
        c_ready = sem("c_activated")
        mod_w_full = [sem(f"mod_weight_full{i}") for i in range(2)]
        mod_acc_ready = sem("mod_products_ready")
        mod_col_full = sem("mod_columns_in_psum")
        mod_ready = sem("mod_vectors_ready")
        kdup_full = sem("doubled_kv_in_psum")
        kcs_ready = sem("doubled_kv_ready")
        xc_ready = sem("recurrence_input_ready")
        qrot_full = sem("nsa_q_rotated_in_psum")
        qrot_free = sem("nsa_q_rotation_taken")
        kr_full = sem("nsa_k_rotated_in_psum")
        kr_ready = sem("nsa_k_ready")
        th_ready = sem("decay_tanh_ready")
        amp_ready = sem("input_amplitude_ready")
        rnn_ready = sem("recurrence_ready")
        hk_ready = sem("compressed_k_hidden_ready")
        hv_ready = sem("compressed_v_hidden_ready")
        hrep_ready = sem("compressed_v_hidden_repeated")
        cmp_full = sem("compressed_kv_in_psum")
        cmp_ready = sem("compressed_kv_ready")
        cs_full = sem("compressed_scores_in_psum")
        cs_ready = sem("compressed_scores_ready")
        cp_ready = sem("compressed_probabilities_ready")
        cpt_full = sem("compressed_probabilities_turned_in_psum")
        cpt_ready = sem("compressed_probabilities_turned_ready")
        co_full = sem("compressed_output_in_psum")
        co_free = sem("compressed_output_taken")
        y2_ready = sem("nsa_rows_ready")
        yfm_full = sem("nsa_turned_in_psum")
        yfm_ready = sem("nsa_turned_ready")
        bgv_ready = sem("short_conv_gated")
        out_ready = sem("output_ready")
        out_done = sem("output_stored")

        block = ctx.enter_context(nc.Block())
        N_TILES = weights.shape[0]
        units = TT * GH
        nsa_units = TT * NSA_HEADS

        @block.sync
        def _(sp):
            w = Count()
            sp.dma_start(tabs[:, :], tables_in).then_inc(loaded, 16)
            sp.dma_start(vecs[:, :], vecs_in).then_inc(loaded, 16)
            sp.dma_start(x[:, :, :], x_in).then_inc(loaded, 16)
            for n in range(RING):
                sp.dma_start(ring[:, n, :], weights[n]).then_inc(w_full[n], 16)
            whole = N_TILES // RING
            with sp.Fori(1, whole) as i:
                for n in range(RING):
                    sp.wait_ge(w_used, i * RING + (n + 1 - RING))
                    tile = weights[bass.ds(i * RING + n, 1)].rearrange("a p w -> (a p) w")
                    sp.dma_start(ring[:, n, :], tile).then_inc(w_full[n], 16)
            for n in range(whole * RING, N_TILES):
                sp.wait_ge(w_used, n + 1 - RING)
                sp.dma_start(ring[:, n % RING, :], weights[n]).then_inc(w_full[n % RING], 16)
            sp.wait_ge(out_ready, w.next(out_ready, 4 if ONLY_FIRST else 1))
            sp.dma_start(out, x[:, :, :]).then_inc(out_done, 16)
            sp.wait_ge(out_done, w.next(out_done, 16))

        @block.gpsimd
        def _(pool):
            w = Count()
            pool.wait_ge(c_ready, w.next(c_ready))
            col_tiles = MOD_PARTS * D_MODEL // TILE
            for k in range(2):
                pool.dma_start(mod_w[:, k, :], mod_in[k]).then_inc(mod_w_full[k], 16)

            def product(n, m, first, refill):
                acc = mod_acc[:, m * TILE:(m + 1) * TILE]
                pool.wait_ge(mod_w_full[m % 2], w.next(mod_w_full[m % 2], 16))
                k = n
                if first:
                    nc.gpsimd.tensor_scalar(acc, mod_w[:, m % 2, :], c_act[:, 0:1], None, ALU.mult).then_inc(pool_link, 1)
                    pool.wait_ge(pool_link, w.next(pool_link))
                else:
                    nc.gpsimd.tensor_scalar(mod_t[:, :], mod_w[:, m % 2, :], k, None, ALU.mult).then_inc(pool_link, 1)
                    pool.wait_ge(pool_link, w.next(pool_link))
                if refill is not None:
                    pool.dma_start(mod_w[:, m % 2, :], refill).then_inc(mod_w_full[m % 2], 16)
                if not first:
                    nc.gpsimd.tensor_tensor(acc, acc, mod_t[:, :], ALU.add).then_inc(pool_link, 1)
                    pool.wait_ge(pool_link, w.next(pool_link))

            for l in range(DEPTH):
                base = l * KT * col_tiles
                for kt in range(KT):
                    for m in range(col_tiles):
                        n = base + kt * col_tiles + m
                        refill = mod_in[n + 2] if n + 2 < DEPTH * KT * col_tiles else None
                        product(c_act[:, kt:kt + 1], m, kt == 0, refill)
                nc.gpsimd.memset(mod_t[:, 0:1], 0.0).then_inc(mod_acc_ready, 1)
                pool.wait_ge(mod_col_full, w.next(mod_col_full))

        @block.tensor
        def _(pe):
            w = Count()
            state = {"tile": 0, "pair": 0, "release": False}
            owed = [None, None]
            pe.wait_ge(loaded, w.next(loaded, 48))

            def mm(o, lhs, rhs, start=True, stop=True, sig=None, share=False):
                ins = pe.matmul(o, lhs, rhs, start=start, stop=stop, skip_group_check=share)
                if sig is not None:
                    ins.then_inc(sig, 1)
                elif state["release"]:
                    ins.then_inc(w_used, 1)
                    state["release"] = False
                return ins

            def slot():
                n = state["tile"] % RING
                pe.wait_ge(w_full[n], w.next(w_full[n], 16))
                state["tile"] += 1
                return n

            def slot_done():
                assert not state["release"]
                state["release"] = True

            def blk(n, k, width=P):
                return ring[:, n, k * P:k * P + width]

            def pair_bank(frees="pair"):
                k = state["pair"] % 2
                if owed[k] is not None:
                    pe.wait_ge(owed[k], w.next(owed[k]))
                owed[k] = pair_free[k] if frees == "pair" else frees
                state["pair"] += 1
                return UP + k

            def column(o, src, each=False, sig=None):
                n = slot()
                for kt in range(KT):
                    if each:
                        pe.wait_ge(h_ready, w.next(h_ready))
                    mm(o, blk(n, kt), src[:, kt, :], kt == 0, kt == KT - 1, sig if kt == KT - 1 else None)
                slot_done()

            def column_pair(src, each=False, frees="pair"):
                b = pair_bank(frees)
                column(half(b, 0), src, each)
                column(half(b, 1), src, sig=pair_full)

            def mean_squares():
                for kt in range(KT):
                    pe.wait_ge(sq_ready, w.next(sq_ready))
                    mm(half(6, 0), tab("mean_all"), work[:, kt, :], kt == 0, kt == KT - 1,
                       stat_full if kt == KT - 1 else None)

            def ffn():
                def down(j, par, last=False):
                    n = slot()
                    pe.wait_ge(hid_ready, w.next(hid_ready))
                    for m in range(KT):
                        mm(half(m // 2, m % 2), blk(n, m), hid[:, par, :], j == 0 and m % 2 == 0, last,
                           down_full if last and m % 2 else None, share=True)
                    slot_done()

                column_pair(h, True, None)
                column_pair(h, False, None)
                down(0, 0)
                t0, p0 = state["tile"], state["pair"]
                with pe.Fori(0, (FT - 2) // 2) as i:
                    w.turn(i, [(s, 16) for s in w_full] + [(hid_ready, 2)])
                    for s in range(2):
                        column_pair(h, False, None)
                        down(1, (1 + s) % 2)
                w.turned((FT - 2) // 2)
                state["tile"], state["pair"] = t0 + 3 * (FT - 2), p0 + FT - 2
                down(FT - 1, (FT - 1) % 2, last=True)

            def token_pair(src, width, tiles):
                b = pair_bank()
                for c in range(tiles):
                    n = slot()
                    for tt in range(TT):
                        at = tt * SEQ + c * P
                        for kt in range(KT):
                            last = c == tiles - 1 and tt == TT - 1 and kt == KT - 1
                            mm(bank[b][:, at:at + width], src[:, kt, tt * P:(tt + 1) * P], blk(n, kt, width),
                               kt == 0, kt == KT - 1, pair_full if last else None)
                    slot_done()

            def turn(o, src, sig=None):
                ins = pe.transpose(o, src, tab("identity"))
                if sig is not None:
                    ins.then_inc(sig, 1)

            def first_mixer():
                for m in range(KT):
                    column_pair(h, m == 0)

                def qk_stats(i):
                    if i >= 1:
                        pe.wait_ge(hm_root, w.next(hm_root))
                        pe.wait_ge(rot_free, w.next(rot_free))
                    mm(bank[6][:, :], tab("mean_head"), sq_buf[:, i % 2, :], sig=hm_full)
                    mm(bank[7][:, :], tab("rot"), z_buf[:, i % 2, :], sig=rot_full)

                for i in range(QT):
                    column_pair(h)
                    if i >= 2:
                        qk_stats(i - 2)
                pe.wait_ge(hperm_ready, w.next(hperm_ready))
                for i in range(QT // 2):
                    token_pair(hperm, P, 2)
                    if i < 2:
                        qk_stats(QT - 2 + i)
                for i in range(KT):
                    column_pair(h)
                    if i == 3:
                        pe.wait_ge(conv_ready, w.next(conv_ready))
                        for kt in range(KT):
                            mm(half(6, 0), tab("mean_all"), conv[:, kt, :], kt == 0, kt == KT - 1,
                               cmean_full if kt == KT - 1 else None)
                    if i == 6:
                        pe.wait_ge(csq_ready, w.next(csq_ready))
                        for kt in range(KT):
                            mm(half(6, 1), tab("mean_all"), work[:, kt, :], kt == 0, kt == KT - 1,
                               cvar_full if kt == KT - 1 else None)
                pe.wait_ge(croot, w.next(croot))
                pe.wait_ge(qk_ready, w.next(qk_ready, QT))
                w.skip(hm_root, 1)
                w.skip(rot_free, 1)

                def scores(u):
                    hd, qt = u // TT, u % TT
                    p0 = HD * (hd % 2)
                    if u >= 2:
                        pe.wait_ge(sc_free, w.next(sc_free))
                    for g in range(GROUPS):
                        k0, k1 = (0, SEQ) if g == 0 else (qt * P, (qt + 1) * P)
                        at = 0 if g == 0 else SEQ + (g - 1) * P
                        mm(bank[u % 2][:, at:at + k1 - k0],
                           qf[p0:p0 + HD, g * GT + hd // 2, qt * P:(qt + 1) * P],
                           kf[p0:p0 + HD, g * GT + hd // 2, k0:k1], sig=sc_full if g == GROUPS - 1 else None)

                def turns(u):
                    pe.wait_ge(p_ready, w.next(p_ready))
                    for b in range(4):
                        turn(bank[2 + u % 2][:, b * P:(b + 1) * P], probs[:, u % 2, b * P:(b + 1) * P],
                             pt_full if b == 3 else None)

                def values(u):
                    hd, qt = u // TT, u % TT
                    pe.wait_ge(pt_ready, w.next(pt_ready))
                    for b, (tt, g) in enumerate(((0, 0), (1, 0), (qt, 1), (qt, 2))):
                        mm(bank[6 + qt][:, hd * HD:(hd + 1) * HD], probs_t[:, u % 2, b * P:(b + 1) * P],
                           vt[:, tt, (g * GH + hd) * HD:(g * GH + hd + 1) * HD], b == 0, b == 3,
                           o_full if b == 3 else None)

                for u in range(units + 2):
                    if u < units:
                        scores(u)
                    if 1 <= u <= units:
                        turns(u - 1)
                    if u >= 2:
                        values(u - 2)
                pe.wait_ge(sc_free, w.next(sc_free, 2))
                pe.wait_ge(ytm_ready, w.next(ytm_ready))
                for qt in range(TT):
                    for b in range(GT):
                        turn(bank[2 + qt][:, b * P:(b + 1) * P], y_tm[:, qt, b * P:(b + 1) * P],
                             yt_full if (qt, b) == (TT - 1, GT - 1) else None)
                pe.wait_ge(ya_ready, w.next(ya_ready))
                for i in range(KT // 2):
                    b = pair_bank()
                    n = slot()
                    for c in range(2):
                        for kt in range(GT):
                            mm(half(b, c), blk(n, c * GT + kt), ya[:, kt, :], kt == 0, kt == GT - 1,
                               pair_full if (c, kt) == (1, GT - 1) else None)
                    slot_done()
                pe.wait_ge(csilu, w.next(csilu))
                for i in range(KT // 2):
                    column_pair(conv)
                pe.wait_ge(gmix_ready, w.next(gmix_ready))
                for i in range(KT // 2):
                    column_pair(h, False, res_pair)

            def mod_columns():
                pe.wait_ge(mod_acc_ready, w.next(mod_acc_ready))
                n = MOD_PARTS * KT
                for c in range(n):
                    mm(bank[7][:, c:c + 1], mod_acc[:, c * P:(c + 1) * P], tab("one"),
                       sig=mod_col_full if c == n - 1 else None)

            def recurrent_nsa_mixer():
                column_pair(h, True)
                column_pair(h)
                column_pair(h)
                column_pair(h)
                for kind in range(2):
                    for g in range(NSA_KV):
                        mm(half(2 * kind + g // 2, g % 2), tab(f"dup{g % 2}"),
                           zk[:, kind, (g // 2) * SEQ:(g // 2 + 1) * SEQ],
                           sig=kdup_full if g == NSA_KV - 1 else None)
                column_pair(h)
                column_pair(h)

                def q_rotated(i):
                    if i >= 2:
                        pe.wait_ge(qrot_free, w.next(qrot_free))
                    mm(bank[6 + i % 2][:, :], tab("rot16"), qn[:, 2 * i:2 * i + 2, :].rearrange("p a b -> p (a b)"),
                       sig=qrot_full)

                def k_rotated(kind):
                    for g in range(NSA_KV):
                        src = zk[:, kind, (g // 2) * SEQ:(g // 2 + 1) * SEQ]
                        mm(half(g // 2, g % 2), tab(f"dup{g % 2}"), src)
                        mm(half(2 + g // 2, g % 2), tab(f"rotdup{g % 2}"), src,
                           sig=kr_full if g == NSA_KV - 1 else None)

                for i in range(4):
                    column_pair(h)
                    if i >= 2:
                        q_rotated(i - 2)
                for i in range(2):
                    column_pair(h)
                    q_rotated(2 + i)
                pe.wait_ge(kcs_ready, w.next(kcs_ready))
                for i in range(4):
                    column_pair(h)
                    if i == 1:
                        k_rotated(0)
                    if i == 3:
                        pe.wait_ge(kr_ready, w.next(kr_ready))
                        k_rotated(1)
                for i in range(2):
                    token_pair(h, P, 2)
                token_pair(h, 3 * NSA_HEADS, 1)
                pe.wait_ge(xc_ready, w.next(xc_ready))
                r_slot = slot()
                state["tile"] += 1
                i_slot = (r_slot + 1) % RING
                pe.wait_ge(w_full[i_slot], w.next(w_full[i_slot], 16))
                for m in range(KT):
                    b = pair_bank()
                    mm(half(b, 0), blk(r_slot, m), xc[:, m, :])
                    mm(half(b, 1), blk(i_slot, m), xc[:, m, :], sig=pair_full)
                slot_done()
                b = pair_bank(hv_ready)
                for kind in range(2):
                    for t in range(2):
                        n = slot()
                        for k in range(KT):
                            j = t * KT + k
                            last = t == 1 and k == KT - 1
                            mm(bank[b][:, kind * SEQ:kind * SEQ + NSA_KV * N_CMP], blk(n, k),
                               kcs[:, kind, :, 2 * j:2 * j + CMP_STRIDE * (N_CMP - 1) + 1:CMP_STRIDE],
                               j == 0, last, share=True)
                            if kind == 0 and t == 0 and k == 0:
                                slot_done()
                            mm(bank[b][:, kind * SEQ + P:kind * SEQ + P + 1], blk(n, k),
                               vec("pe_k" if kind == 0 else "pe_v", 0, j), False, last, share=True,
                               sig=pair_full if kind == 1 and last else None)
                        slot_done()
                pe.wait_ge(hk_ready, w.next(hk_ready))
                mm(bank[6][:, 0:NSA_KV * N_CMP], vec("wk2", 0, 0, P), hk)
                pe.wait_ge(hrep_ready, w.next(hrep_ready))
                for g in range(NSA_KV):
                    mm(bank[6][:, HD + g * HD:HD + (g + 1) * HD], hrep[:, g].rearrange("p a b -> p (a b)"),
                       vec("wv2", 0, 0, HD), sig=cmp_full if g == NSA_KV - 1 else None)
                pe.wait_ge(cmp_ready, w.next(cmp_ready))
                pe.wait_ge(kr_ready, w.next(kr_ready))
                pe.wait_ge(rnn_ready, w.next(rnn_ready))

                def q_half(src, hd, qt):
                    p0 = HD * (hd % 2)
                    return src[p0:p0 + HD, hd // 2, qt * P:(qt + 1) * P]

                for qt in range(TT):
                    for par in range(2):
                        for k in range(NSA_HEADS // 2):
                            hd = 2 * k + par
                            g, p0 = hd // NSA_REP, HD * par
                            mm(bank[par][:, k * CMP_ROOM:k * CMP_ROOM + N_CMP], q_half(qn, hd, qt),
                               kcmp[p0:p0 + HD, g * N_CMP:(g + 1) * N_CMP],
                               sig=cs_full if (par, k) == (1, NSA_HEADS // 2 - 1) else None)
                    pe.wait_ge(cp_ready, w.next(cp_ready))
                    for g in range(NSA_KV):
                        turn(bank[2][:, g * P:(g + 1) * P],
                             pc[:, NSA_REP * g:NSA_REP * (g + 1), :].rearrange("p a b -> p (a b)"),
                             cpt_full if g == NSA_KV - 1 else None)
                    pe.wait_ge(cpt_ready, w.next(cpt_ready))
                    if qt:
                        pe.wait_ge(co_free, w.next(co_free))
                    for g in range(NSA_KV):
                        mm(half(6 + g // 2, g % 2), pct[:, g * P:(g + 1) * P],
                           v4[:, g].rearrange("p a b -> p (a b)"), sig=co_full if g == NSA_KV - 1 else None)
                pe.wait_ge(co_free, w.next(co_free))

                def scores(u):
                    qt, hd = u // NSA_HEADS, u % NSA_HEADS
                    length, p0 = (qt + 1) * P, HD * (hd % 2)
                    if u >= 2:
                        pe.wait_ge(sc_free, w.next(sc_free))
                    for br in range(2):
                        mm(bank[u % 2][:, br * length:(br + 1) * length], q_half(qr, hd, qt),
                           kr[p0:p0 + HD, br, hd // NSA_REP, 0:length], sig=sc_full if br else None)

                def turns(u):
                    n = 2 * (u // NSA_HEADS + 1)
                    pe.wait_ge(p_ready, w.next(p_ready))
                    for b in range(n):
                        turn(bank[2 + u % 2][:, b * P:(b + 1) * P], p2[:, u % 2, b * P:(b + 1) * P],
                             pt_full if b == n - 1 else None)

                def values(u):
                    qt, hd = u // NSA_HEADS, u % NSA_HEADS
                    g, r = hd // NSA_REP, hd % NSA_REP
                    lot = u // NSA_REP
                    pe.wait_ge(pt_ready, w.next(pt_ready))
                    if r == 0 and lot >= 2:
                        pe.wait_ge(o_free, w.next(o_free))
                    for br in range(2):
                        for kt in range(qt + 1):
                            at = (r * 2 + br) * HD
                            mm(bank[6 + lot % 2][:, at:at + HD],
                               pt2[:, u % 2, (br * (qt + 1) + kt) * P:(br * (qt + 1) + kt + 1) * P],
                               vsw[:, br, kt, g * HD:(g + 1) * HD], kt == 0, kt == qt,
                               o_full if br and kt == qt else None)

                for u in range(nsa_units + 2):
                    if u < nsa_units:
                        scores(u)
                    if 1 <= u <= nsa_units:
                        turns(u - 1)
                    if u >= 2:
                        values(u - 2)
                pe.wait_ge(sc_free, w.next(sc_free, 2))
                pe.wait_ge(y2_ready, w.next(y2_ready))
                for b in range(4):
                    for k in range(4):
                        qt, f = b // 2, (b % 2) * 4 + k
                        turn(bank[b][:, k * P:(k + 1) * P], y2t[:, qt, f * P:(f + 1) * P],
                             yfm_full if k == 3 else None)
                pe.wait_ge(yfm_ready, w.next(yfm_ready))
                for i in range(KT // 2):
                    b = pair_bank(y_pair)
                    for c in range(2):
                        for t, src in enumerate((yrnn, yfm)):
                            n = slot()
                            for kt in range(KT):
                                mm(half(b, c), blk(n, kt), src[:, kt, :], t == 0 and kt == 0, t == 1 and kt == KT - 1,
                                   pair_full if (c, t, kt) == (1, 1, KT - 1) else None)
                            slot_done()

            def short_conv_mixer():
                for m in range(KT):
                    column_pair(h, m == 0)
                for i in range(KT // 2):
                    column_pair(h)
                pe.wait_ge(bgv_ready, w.next(bgv_ready))
                for i in range(KT // 2):
                    column_pair(vconv, False, y_pair)

            for l in range(DEPTH):
                mean_squares()
                ffn()
                mean_squares()
                first_mixer()
                mean_squares()
                ffn()
                mod_columns()
                mean_squares()
            if not ONLY_FIRST:
                for l in range(DEPTH):
                    mean_squares()
                    recurrent_nsa_mixer() if l == 0 else short_conv_mixer()
                    mean_squares()
                    mean_squares()
                    ffn()
                    mean_squares()
            assert state["tile"] == N_TILES, (state["tile"], N_TILES)

        @block.scalar
        def _(act):
            w = Count()
            state = {"pair": 0}
            act.wait_ge(loaded, w.next(loaded, 48))
            act_f = nc.scalar.activation
            act_f(c_act[:, :], vec("c", 0, 0, KT), ACT.Silu).then_inc(c_ready, 1)
            act.wait_ge(lam_ready, w.next(lam_ready))
            act_f(tiny[:, 1, :], tiny[:, 0, :], ACT.Exp, scale=-1.0).then_inc(lam_exp, 1)

            def next_pair():
                act.wait_ge(pair_full, w.next(pair_full))
                b = UP + state["pair"] % 2
                state["pair"] += 1
                return b, pair_free[b - UP]

            def squares(src, ready):
                for kt in range(KT):
                    if kt % 2 == 0 and ready is not None:
                        act.wait_ge(ready, w.next(ready))
                    act_f(work[:, kt, :], src[:, kt, :], ACT.Square).then_inc(sq_ready, 1)
                act.wait_ge(stat_full, w.next(stat_full))
                act_f(rinv[:, :], half(6, 0), ACT.Sqrt, bias=tab("eps")).then_inc(root_ready, 1)

            def norm(ready, gain, shift, dst, done):
                squares(x, ready)
                for kt in range(KT):
                    act.wait_ge(scaled, w.next(scaled))
                    ins = act_f(dst[:, kt, :], work[:, kt, :], ACT.Identity, scale=gain[:, kt:kt + 1],
                                bias=shift[:, kt:kt + 1] if shift is not None else 0.0)
                    if done is h_ready or kt % 2:
                        ins.then_inc(done, 1)
                if done is h_ready:
                    w.skip(h_ready, KT)

            def ffn():
                def step(par):
                    b, _ = next_pair()
                    act_f(gate_a[:, par, :], half(b, 0), ACT.Silu).then_inc(gate_ready, 1)

                p0 = state["pair"]
                with act.Fori(0, FT // 2) as i:
                    w.turn(i, [(pair_full, 2)])
                    step(0)
                    step(1)
                w.turned(FT // 2)
                state["pair"] = p0 + FT

            def conv_ffn():
                def step(par):
                    b, _ = next_pair()
                    act_f(fpad[:, par, SHORT_TAPS - 1:], half(b, 0), ACT.Copy).then_inc(gate_copied, 1)
                    act.wait_ge(gate_convolved, w.next(gate_convolved))
                    act_f(gate_a[:, par, :], gate_a[:, par, :], ACT.Silu).then_inc(gate_ready, 1)

                p0 = state["pair"]
                with act.Fori(0, FT // 2) as i:
                    w.turn(i, [(pair_full, 2), (gate_convolved, 2)])
                    step(0)
                    step(1)
                w.turned(FT // 2)
                state["pair"] = p0 + FT

            def heads(count, exponentials, turned, n_turned):
                for u in range(count + 1):
                    if u < count:
                        act.wait_ge(smax, w.next(smax))
                        exponentials(u)
                    if u >= 1:
                        act.wait_ge(pt_full, w.next(pt_full))
                        n = n_turned(u - 1)
                        act_f(turned[:, (u - 1) % 2, 0:n], bank[2 + (u - 1) % 2][:, 0:n], ACT.Copy).then_inc(pt_ready, 1)

            def first_mixer(l):
                norm(res_x, vec("mix_norm", l, 0, KT), None, h, h_ready)
                act.wait_ge(h_ready, w.last(h_ready))
                act.dma_start(v_bias, bv_in[l]).then_inc(v_bias_full, 16)
                for r in range(2):
                    ins = act_f(hperm[:, :, r * P:(r + 1) * P].rearrange("p k (a l) -> p k a l", l=2),
                                h[:, :, :].rearrange("p k (a r l) -> p r k a l", r=2, l=2)[:, r], ACT.Copy)
                ins.then_inc(hperm_ready, 1)
                for m in range(KT):
                    b, _ = next_pair()
                    act_f(gate_a[:, m % 2, :], half(b, 1), ACT.Sigmoid,
                          bias=vec("b_in", l, KT + m)).then_inc(gate_ready, 1)

                def head_root(i):
                    act.wait_ge(hm_full, w.next(hm_full))
                    act_f(root_buf[:, i % 2, :], bank[6][:, :], ACT.Sqrt, bias=tab("eps")).then_inc(hm_root, 1)

                for i in range(QT):
                    if i >= 2:
                        head_root(i - 2)
                    b, free = next_pair()
                    if i >= 2:
                        act.wait_ge(qk_ready, w.next(qk_ready))
                    for c in range(2):
                        bias = vec("b_in", l, 2 * KT + 2 * i + c)
                        act_f(z_buf[:, i % 2, c * SEQ:(c + 1) * SEQ], half(b, c), ACT.Identity, bias=bias)
                        ins = act_f(sq_buf[:, i % 2, c * SEQ:(c + 1) * SEQ], half(b, c), ACT.Square, bias=bias)
                    ins.then_inc(free, 1)
                w.skip(qk_ready, 2)
                head_root(QT - 2)
                head_root(QT - 1)
                skip_pairs(QT // 2)
                for i in range(KT):
                    b, free = next_pair()
                    for c in range(2):
                        ins = act_f(gates[:, 2 * i + c, :], half(b, c), ACT.Sigmoid,
                                    bias=vec("b_in", l, 2 * KT + 2 * QT + 2 * i + c))
                    ins.then_inc(free, 1)
                    if i == 4:
                        act.wait_ge(centred, w.next(centred))
                        act_f(work[:, :, :], conv, ACT.Square).then_inc(csq_ready, 1)
                    if i == 6:
                        act.wait_ge(cvar_full, w.next(cvar_full))
                        act_f(rinv[:, :], half(6, 1), ACT.Sqrt, bias=tab("eps")).then_inc(croot, 1)
                act.wait_ge(cnorm, w.next(cnorm))
                for kt in range(KT):
                    ins = act_f(conv[:, kt, :], conv[:, kt, :], ACT.Silu, scale=vec("conv_ln_g", l, kt),
                                bias=vec("conv_ln_b", l, kt))
                ins.then_inc(csilu, 1)

                def exponential(u):
                    act_f(probs[:, u % 2, :], scores_s[:, u % 2, :], ACT.Exp, bias=nmax[:, u:u + 1],
                          accum_out=rsum[:, u:u + 1]).then_inc(p_ready, 1)

                heads(units, exponential, probs_t, lambda u: 4 * P)
                skip_pairs(3 * KT // 2)

            def recurrent_nsa_mixer():
                for kind in range(2):
                    b, free = next_pair()
                    act_f(zk[:, kind, :], bank[b][:, :], ACT.Copy).then_inc(free, 1)
                skip_pairs(KT // 2)
                for i in range(4):
                    b, free = next_pair()
                    act_f(qn[:, 2 * i:2 * i + 2, :], two(bank[b][:, :]), ACT.Copy).then_inc(free, 1)
                for kind in range(2):
                    b, free = next_pair()
                    act_f(zk[:, kind, :], bank[b][:, :], ACT.Copy).then_inc(free, 1)
                for i in range(4):
                    b, free = next_pair()
                    act_f(gg[:, 2 * i:2 * i + 2, :], two(bank[b][:, :]), ACT.Gelu_apprx_tanh).then_inc(free, 1)
                for kind in range(2):
                    b, free = next_pair()
                    act_f(vsw[:, kind, :, :], two(bank[b][:, :]), ACT.Copy).then_inc(free, 1)
                b, free = next_pair()
                act_f(glog, two(bank[b][:, :])[:, :, 0:3 * NSA_HEADS], ACT.Sigmoid).then_inc(free, 1)
                for m in range(KT):
                    b, free = next_pair()
                    act_f(th[:, m, :], half(b, 0), ACT.Sigmoid, bias=vec("b_r", 0, m)).then_inc(act_link, 1)
                    act_f(it[:, m, :], half(b, 1), ACT.Sigmoid, bias=vec("b_i", 0, m)).then_inc(free, 1)
                act.wait_ge(act_link, w.next(act_link, KT))
                act.wait_ge(decay_ready, w.next(decay_ready))
                for m in range(KT):
                    ins = act_f(th[:, m, :], th[:, m, :], ACT.Tanh, scale=decay[:, m:m + 1])
                ins.then_inc(th_ready, 1)
                act.wait_ge(th_ready, w.next(th_ready))
                act.wait_ge(kr_ready, w.next(kr_ready, 2))
                act_f(work[:, :, :], th, ACT.Sqrt, scale=-4.0).then_inc(amp_ready, 1)
                b, _ = next_pair()
                for kind in range(2):
                    at = kind * SEQ + P
                    ins = act_f(hb[:, kind:kind + 1], bank[b][:, at:at + 1], ACT.Copy)
                ins.then_inc(act_link, 1)
                act.wait_ge(act_link, w.next(act_link))
                n = NSA_KV * N_CMP
                act_f(hk, bank[b][:, 0:n], ACT.Gelu_apprx_tanh, bias=hb[:, 0:1]).then_inc(hk_ready, 1)
                act_f(hv, bank[b][:, SEQ:SEQ + n], ACT.Gelu_apprx_tanh, bias=hb[:, 1:2]).then_inc(hv_ready, 1)
                for qt in range(TT):
                    act.wait_ge(cs_ready, w.next(cs_ready))
                    act_f(pc[:, :, 0:N_CMP], scc, ACT.Exp).then_inc(cp_ready, 1)
                    act.wait_ge(cpt_full, w.next(cpt_full))
                    act_f(pct, bank[2][:, :], ACT.Copy).then_inc(cpt_ready, 1)

                def exponentials(u):
                    length = (u // NSA_HEADS + 1) * P
                    for br in range(2):
                        k = 2 * u + br
                        ins = act_f(p2[:, u % 2, br * length:(br + 1) * length],
                                    s2[:, u % 2, br * length:(br + 1) * length], ACT.Exp, bias=nmax[:, k:k + 1],
                                    accum_out=rsum[:, k:k + 1])
                    ins.then_inc(p_ready, 1)

                heads(nsa_units, exponentials, pt2, lambda u: 2 * (u // NSA_HEADS + 1) * P)
                for b in range(4):
                    act.wait_ge(yfm_full, w.next(yfm_full))
                    ins = act_f(yfm[:, 4 * (b % 2):4 * (b % 2) + 4, (b // 2) * P:(b // 2 + 1) * P],
                                bank[b][:, :].rearrange("p (k t) -> p k t", k=4), ACT.Copy)
                ins.then_inc(yfm_ready, 1)
                skip_pairs(KT // 2)

            def short_conv_mixer():
                for m in range(KT):
                    b, _ = next_pair()
                    act_f(gate_a[:, m % 2, :], half(b, 0), ACT.Copy).then_inc(gate_copied, 1)
                skip_pairs(KT)

            def skip_pairs(n):
                w.skip(pair_full, n)
                state["pair"] += n

            res_x = x_ready
            for l in range(DEPTH):
                norm(None if l == 0 else x_ready, vec("ffn1_norm", l, 0, KT), None, h, h_ready)
                ffn()
                first_mixer(l)
                norm(res_pair, vec("ffn2_norm", l, 0, KT), None, h, h_ready)
                ffn()
                norm(x_ready, vec("final_norm", l, 0, KT), None, x, out_ready if ONLY_FIRST and l else x_ready)
            if not ONLY_FIRST:
                act.wait_ge(mod_ready, w.next(mod_ready, DEPTH))
                for l in range(DEPTH):
                    norm(x_ready, modv[:, l, 1, :], modv[:, l, 0, :], h, h_ready)
                    recurrent_nsa_mixer() if l == 0 else short_conv_mixer()
                    squares(h, y_pair)
                    norm(x_ready, modv[:, l, 4, :], modv[:, l, 3, :], h, h_ready)
                    conv_ffn()
                    squares(h, y_down)

        @block.vector
        def _(dve):
            w = Count()
            state = {"pair": 0, "conv": 0}
            v = nc.vector
            dve.wait_ge(loaded, w.next(loaded, 48))

            lam = vec("lam", 0, 0, KT)
            v.scalar_tensor_tensor(tiny[:, 0, :], lam, -1.0, lam, ALU.mult, ALU.max).then_inc(lam_ready, 1)
            v.tensor_scalar(tiny[:, 5, :], lam, -1.0, 0.0, ALU.mult, ALU.max).then_inc(dve_link, 1)
            dve.wait_ge(dve_link, w.next(dve_link))
            dve.wait_ge(lam_exp, w.next(lam_exp))
            e, s, q, r = tiny[:, 1, :], tiny[:, 2, :], tiny[:, 3, :], tiny[:, 4, :]
            v.tensor_scalar(s, e, 2.0, None, ALU.add).then_inc(dve_link, 1)
            dve.wait_ge(dve_link, w.next(dve_link))
            v.reciprocal(s, s).then_inc(dve_link, 1)
            dve.wait_ge(dve_link, w.next(dve_link))
            v.tensor_tensor(s, s, e, ALU.mult).then_inc(dve_link, 1)
            dve.wait_ge(dve_link, w.next(dve_link))
            v.tensor_tensor(q, s, s, ALU.mult).then_inc(dve_link, 1)
            dve.wait_ge(dve_link, w.next(dve_link))
            v.tensor_scalar(r, q, 1.0 / 17, None, ALU.mult).then_inc(dve_link, 1)
            dve.wait_ge(dve_link, w.next(dve_link))
            for odd in range(15, 1, -2):
                v.scalar_tensor_tensor(r, r, 1.0 / odd, q, ALU.add, ALU.mult).then_inc(dve_link, 1)
                dve.wait_ge(dve_link, w.next(dve_link))
            v.scalar_tensor_tensor(r, r, 1.0, s, ALU.add, ALU.mult).then_inc(dve_link, 1)
            dve.wait_ge(dve_link, w.next(dve_link))
            v.scalar_tensor_tensor(r, r, 2.0, tiny[:, 5, :], ALU.mult, ALU.add).then_inc(dve_link, 1)
            dve.wait_ge(dve_link, w.next(dve_link))
            v.tensor_scalar(decay[:, :], r, -4.0, None, ALU.mult).then_inc(decay_ready, 1)
            v.memset(fpad[:, :, 0:SHORT_TAPS - 1], 0.0).then_inc(dve_link, 1)
            dve.wait_ge(dve_link, w.next(dve_link))

            def next_pair(wait=True):
                if wait:
                    dve.wait_ge(pair_full, w.next(pair_full))
                else:
                    w.skip(pair_full, 1)
                b = UP + state["pair"] % 2
                state["pair"] += 1
                return b, pair_free[b - UP]

            def skip_pairs(n):
                w.skip(pair_full, n)
                state["pair"] += n

            def scale_tiles():
                dve.wait_ge(root_ready, w.next(root_ready))
                v.reciprocal(rinv[:, :], rinv[:, :]).then_inc(dve_link, 1)
                dve.wait_ge(dve_link, w.next(dve_link))
                for kt in range(KT):
                    v.tensor_tensor(work[:, kt, :], x[:, kt, :], rinv[:, :], ALU.mult).then_inc(scaled, 1)

            def add_normed(gain, done):
                dve.wait_ge(root_ready, w.next(root_ready))
                v.reciprocal(rinv[:, :], rinv[:, :]).then_inc(dve_link, 1)
                dve.wait_ge(dve_link, w.next(dve_link))
                for kt in range(KT):
                    ins = v.scalar_tensor_tensor(work[:, kt, :], h[:, kt, :], gain[:, kt:kt + 1], rinv[:, :],
                                                 ALU.mult, ALU.mult)
                ins.then_inc(dve_link, 1)
                dve.wait_ge(dve_link, w.next(dve_link))
                for kt in range(0, KT, 2):
                    ins = v.tensor_tensor(x[:, kt:kt + 2, :], x[:, kt:kt + 2, :], work[:, kt:kt + 2, :], ALU.add)
                    if done is x_ready or kt == KT - 2:
                        ins.then_inc(done, 1)

            def hidden(par, b):
                dve.wait_ge(gate_ready, w.next(gate_ready))
                v.tensor_tensor(hid[:, par, :], gate_a[:, par, :], half(b, 1), ALU.mult).then_inc(hid_ready, 1)

            def ffn():
                assert state["pair"] % 2 == 0
                with dve.Fori(0, FT // 2) as i:
                    w.turn(i, [(gate_ready, 2)])
                    hidden(0, UP)
                    hidden(1, UP + 1)
                w.turned(FT // 2)
                skip_pairs(FT)
                for b in range(4):
                    dve.wait_ge(down_full, w.next(down_full))
                    v.scalar_tensor_tensor(x[:, 2 * b:2 * b + 2, :], two(bank[b][:, :]), 0.5, x[:, 2 * b:2 * b + 2, :],
                                           ALU.mult, ALU.add).then_inc(x_ready, 1)

            def conv_ffn(l):
                assert state["pair"] % 2 == 0
                at_w, at_b = VEC["ffn_conv_w", l], VEC["ffn_conv_b", l]
                with dve.Fori(0, FT // 2) as i:
                    w.turn(i, [(gate_copied, 2), (dve_link, 2 * (SHORT_TAPS - 1)), (gate_ready, 2)])
                    for par in range(2):
                        dve.wait_ge(gate_copied, w.next(gate_copied))
                        g = gate_a[:, par, :]
                        for k in range(SHORT_TAPS):
                            tap = vecs[:, bass.ds(i * 2 * SHORT_TAPS + (at_w + par * SHORT_TAPS + k), 1)]
                            src = fpad[:, par, k:k + SEQ]
                            if k == 0:
                                bias = vecs[:, bass.ds(i * 2 + (at_b + par), 1)]
                                ins = v.tensor_scalar(g, src, tap, bias, ALU.mult, ALU.add)
                            else:
                                ins = v.scalar_tensor_tensor(g, src, tap, g, ALU.mult, ALU.add)
                            if k < SHORT_TAPS - 1:
                                ins.then_inc(dve_link, 1)
                                dve.wait_ge(dve_link, w.next(dve_link))
                        ins.then_inc(gate_convolved, 1)
                        hidden(par, UP + par)
                w.turned(FT // 2)
                skip_pairs(FT)
                for b in range(4):
                    dve.wait_ge(down_full, w.next(down_full))
                    v.tensor_copy(h[:, 2 * b:2 * b + 2, :], two(bank[b][:, :])).then_inc(y_down, 1)

            def depthwise(taps, src, dst, weight, bias):
                for m0 in range(0, KT, 2):
                    for k in range(taps):
                        for m in (m0, m0 + 1):
                            if state["conv"] % (2 * taps) >= 2:
                                dve.wait_ge(conv_link, w.next(conv_link))
                            state["conv"] += 1
                            tap = weight(m, k)
                            if k == 0:
                                ins = v.tensor_scalar(dst[:, m, :], src[:, m, k:k + SEQ], tap, bias(m),
                                                      ALU.mult, ALU.add)
                            else:
                                ins = v.scalar_tensor_tensor(dst[:, m, :], src[:, m, k:k + SEQ], tap, dst[:, m, :],
                                                             ALU.mult, ALU.add)
                            ins.then_inc(conv_link, 1)
                            yield ins
                    dve.wait_ge(conv_link, w.next(conv_link, 2))

            def first_mixer(l):
                scale_tiles()
                v.memset(upad[:, :, 0:CONV_PAD], 0.0)
                v.memset(upad[:, :, CONV_PAD + SEQ:], 0.0).then_inc(dve_link, 1)
                dve.wait_ge(dve_link, w.next(dve_link))
                for m in range(KT):
                    b, free = next_pair(False)
                    dve.wait_ge(gate_ready, w.next(gate_ready))
                    v.scalar_tensor_tensor(upad[:, m, CONV_PAD:CONV_PAD + SEQ], half(b, 0), vec("b_in", l, m),
                                           gate_a[:, m % 2, :], ALU.add, ALU.mult).then_inc(free, 1)
                v.memset(tiny[:, 7, :], 0.0).then_inc(dve_link, 1)
                dve.wait_ge(dve_link, w.next(dve_link))
                steps = depthwise(CONV_TAPS, upad, conv, lambda m, k: vec("conv_w", l, m * CONV_TAPS + k),
                                  lambda m: vec("conv_b", l, m))

                def some_taps(n):
                    for _ in range(n):
                        next(steps, None)

                def q_or_k(i):
                    gain, dst = ("q", qf) if i < QT // 2 else ("k", kf)
                    g, t0 = (2 * i % QT) // GT, 2 * i % QT
                    z, t2, root = z_buf[:, i % 2, :], sq_buf[:, i % 2, :], root_buf[:, i % 2, :]
                    dve.wait_ge(hm_root, w.next(hm_root))
                    v.reciprocal(root, root)
                    dve.wait_ge(rot_full, w.next(rot_full))
                    v.scalar_tensor_tensor(two(t2), two(bank[7][:, :]), vec(gain + "_gain_swapped", l, g),
                                           rows(tab("sin"), 2), ALU.mult, ALU.mult).then_inc(rot_free, 1)
                    v.scalar_tensor_tensor(two(z), two(z), vec(gain + "_gain", l, g), rows(tab("cos"), 2),
                                           ALU.mult, ALU.mult).then_inc(dve_link, 1)
                    dve.wait_ge(dve_link, w.next(dve_link))
                    v.tensor_tensor(z, z, t2, ALU.add).then_inc(dve_link, 1)
                    dve.wait_ge(dve_link, w.next(dve_link))
                    for c in range(2):
                        def by_residue(ap):
                            return ap[:, c * SEQ:(c + 1) * SEQ].rearrange("p (a h l) -> p h a l", h=2, l=2)
                        ins = v.tensor_tensor(dst[:, t0 + c, :].rearrange("p (h a l) -> p h a l", h=2, l=2),
                                              by_residue(z), by_residue(root), ALU.mult)
                    ins.then_inc(qk_ready, 1)

                some_taps(12)
                for i in range(QT):
                    q_or_k(i)
                    some_taps(14)
                dve.wait_ge(v_bias_full, w.next(v_bias_full, 16))
                for i in range(QT // 2):
                    if i == 0:
                        skip_pairs(QT)
                    b, free = next_pair()
                    v.tensor_tensor(vt[:, :, i * SEQ:(i + 1) * SEQ], two(bank[b][:, :]),
                                    rows(v_bias[:, i * SEQ:(i + 1) * SEQ], TT), ALU.add).then_inc(free, 1)
                    some_taps(14)
                some_taps(KT * CONV_TAPS)
                v.memset(tiny[:, 7, :], 0.0).then_inc(conv_ready, 1)
                skip_pairs(KT)
                dve.wait_ge(cmean_full, w.next(cmean_full))
                v.tensor_tensor(conv, conv, half(6, 0)[:, None, :].broadcast_to([P, KT, SEQ]), ALU.subtract
                                ).then_inc(centred, 1)
                dve.wait_ge(croot, w.next(croot))
                v.reciprocal(rinv[:, :], rinv[:, :]).then_inc(dve_link, 1)
                dve.wait_ge(dve_link, w.next(dve_link))
                v.tensor_tensor(conv, conv, rows(rinv[:, :], KT), ALU.mult).then_inc(cnorm, 1)

                for u in range(units):
                    dve.wait_ge(sc_full, w.next(sc_full))
                    v.scalar_tensor_tensor(scores_s[:, u % 2, :], bank[u % 2][:, :], SCALE, tab(f"mask{u % TT}"),
                                           ALU.mult, ALU.add).then_inc(sc_free, 1)
                    dve.wait_ge(sc_free, w.next(sc_free))
                    v.tensor_reduce(nmax[:, u:u + 1], scores_s[:, u % 2, :], X_AXIS, ALU.max, negate=True
                                    ).then_inc(smax, 1)
                dve.wait_ge(o_full, w.next(o_full, units))
                v.reciprocal(rrec[:, 0:units], rsum[:, 0:units]).then_inc(dve_link, 1)
                dve.wait_ge(dve_link, w.next(dve_link))
                for qt in range(TT):
                    share = rrec[:, 0:units].rearrange("p (h t) -> p t h", t=TT)[:, qt]
                    ins = v.tensor_tensor(y_tm[:, qt, :].rearrange("p (h d) -> p h d", h=GH),
                                          bank[6 + qt][:, :].rearrange("p (h d) -> p h d", h=GH),
                                          cols(share, HD), ALU.mult)
                ins.then_inc(ytm_ready, 1)
                dve.wait_ge(yt_full, w.next(yt_full))
                for qt in range(TT):
                    ins = v.tensor_copy(ya.rearrange("p k (a h l) -> p h k a l", h=2, l=2)[:, qt],
                                        bank[2 + qt][:, :].rearrange("p (k a l) -> p k a l", k=GT, l=2))
                ins.then_inc(ya_ready, 1)
                for i in range(KT // 2):
                    b, free = next_pair()
                    v.tensor_tensor(h[:, 2 * i:2 * i + 2, :], two(bank[b][:, :]), gates[:, 2 * i:2 * i + 2, :],
                                    ALU.mult).then_inc(free, 1)
                for i in range(KT // 2):
                    b, free = next_pair()
                    t = sq_buf[:, i % 2, :]
                    for c in range(2):
                        m = 2 * i + c
                        ins = v.scalar_tensor_tensor(t[:, c * SEQ:(c + 1) * SEQ], half(b, c), vec("b_conv_proj", l, m),
                                                     gates[:, KT + m, :], ALU.add, ALU.mult)
                        ins.then_inc(free if c else dve_link, 1)
                    dve.wait_ge(dve_link, w.next(dve_link))
                    v.memset(tiny[:, 7, :], 0.0).then_inc(dve_link, 1)
                    dve.wait_ge(dve_link, w.next(dve_link))
                    ins = v.tensor_tensor(h[:, 2 * i:2 * i + 2, :], h[:, 2 * i:2 * i + 2, :], two(t), ALU.add)
                ins.then_inc(gmix_ready, 1)
                for i in range(KT // 2):
                    b, _ = next_pair()
                    v.tensor_tensor(x[:, 2 * i:2 * i + 2, :], two(bank[b][:, :]), x[:, 2 * i:2 * i + 2, :], ALU.add
                                    ).then_inc(res_pair, 1)

            def mod_vectors(l):
                dve.wait_ge(mod_col_full, w.next(mod_col_full))
                flat = modv[:, l, :, :].rearrange("p a b -> p (a b)")
                v.tensor_tensor(flat, bank[7][:, 0:MOD_PARTS * KT], vec("mod_b", l, 0, MOD_PARTS * KT),
                                ALU.add).then_inc(dve_link, 1)
                dve.wait_ge(dve_link, w.next(dve_link))
                for part, gain in ((1, "mix_pre"), (2, "mix_post"), (4, "ffn_pre"), (5, "ffn_post")):
                    ins = v.scalar_tensor_tensor(modv[:, l, part, :], modv[:, l, part, :], 1.0, vec(gain, l, 0, KT),
                                                 ALU.add, ALU.mult)
                ins.then_inc(mod_ready, 1)

            def recurrent_nsa_mixer():
                skip_pairs(2)
                v.memset(xpad[:, :, 0:RNN_TAPS - 1], 0.0).then_inc(dve_link, 1)
                dve.wait_ge(dve_link, w.next(dve_link))
                v.memset(hrep, 0.0)

                def xr_pair(i):
                    b, free = next_pair()
                    v.tensor_copy(xpad[:, 2 * i:2 * i + 2, RNN_TAPS - 1:], two(bank[b][:, :])).then_inc(free, 1)

                xr_pair(0)
                xr_pair(1)
                for kind in range(2):
                    dve.wait_ge(kdup_full, w.next(kdup_full))
                    for b in range(2):
                        src = two(bank[2 * kind + b][:, :])
                        v.tensor_copy(kcs[0:HD, kind, 2 * b:2 * b + 2, :], src[0:HD])
                        ins = v.tensor_copy(kcs[HD:P, kind, 2 * b:2 * b + 2, 0:SEQ - 1], src[HD:P, :, 1:SEQ])
                ins.then_inc(kcs_ready, 1)
                xr_pair(2)
                xr_pair(3)
                v.memset(tiny[:, 7, :], 0.0).then_inc(dve_link, 1)
                dve.wait_ge(dve_link, w.next(dve_link))
                for _ in depthwise(RNN_TAPS, xpad, xc, lambda m, k: vec("rnn_conv_w", 0, m * RNN_TAPS + k),
                                   lambda m: vec("rnn_conv_b", 0, m)):
                    pass
                v.memset(tiny[:, 7, :], 0.0).then_inc(xc_ready, 1)
                skip_pairs(6)
                for i in range(4):
                    dve.wait_ge(qrot_full, w.next(qrot_full))
                    t = two(rtmp[:, i % 2, :])
                    v.tensor_tensor(t, two(bank[6 + i % 2][:, :]), rows(tab("sin16"), 2), ALU.mult).then_inc(qrot_free, 1)
                    v.tensor_tensor(qr[:, 2 * i:2 * i + 2, :], qn[:, 2 * i:2 * i + 2, :], rows(tab("cos16"), 2),
                                    ALU.mult).then_inc(dve_link, 1)
                    dve.wait_ge(dve_link, w.next(dve_link))
                    v.tensor_tensor(qr[:, 2 * i:2 * i + 2, :], qr[:, 2 * i:2 * i + 2, :], t, ALU.add)
                for kind in range(2):
                    dve.wait_ge(kr_full, w.next(kr_full))
                    for b in range(2):
                        t = two(rtmp[:, b, :])
                        o = kr[:, kind, 2 * b:2 * b + 2, :]
                        v.tensor_tensor(t, two(bank[2 + b][:, :]), rows(tab("sin16"), 2), ALU.mult)
                        v.tensor_tensor(o, two(bank[b][:, :]), rows(tab("cos16"), 2), ALU.mult).then_inc(dve_link, 1)
                        dve.wait_ge(dve_link, w.next(dve_link))
                        ins = v.tensor_tensor(o, o, t, ALU.add)
                    ins.then_inc(kr_ready, 1)
                skip_pairs(4 + 2 + 1 + KT)
                dve.wait_ge(th_ready, w.next(th_ready))
                v.tensor_scalar(den, th, -1.0, 1.0, ALU.mult, ALU.add).then_inc(dve_link, 1)
                dve.wait_ge(dve_link, w.next(dve_link))
                v.reciprocal(den, den)
                v.tensor_tensor(it, it, xc, ALU.mult).then_inc(dve_link, 1)
                dve.wait_ge(dve_link, w.next(dve_link))
                v.tensor_tensor(it, it, den, ALU.mult).then_inc(dve_link, 1)
                dve.wait_ge(dve_link, w.next(dve_link))
                dve.wait_ge(amp_ready, w.next(amp_ready))
                v.tensor_tensor(it, it, work[:, :, :], ALU.mult).then_inc(dve_link, 1)
                dve.wait_ge(dve_link, w.next(dve_link))
                v.scalar_tensor_tensor(th, th, 1.0, den, ALU.add, ALU.mult).then_inc(dve_link, 1)
                dve.wait_ge(dve_link, w.next(dve_link))
                for m in range(KT):
                    ins = v.tensor_tensor_scan(xc[:, m, :], th[:, m, :], it[:, m, :], 0.0, ALU.mult, ALU.add)
                ins.then_inc(dve_link, 1)
                dve.wait_ge(dve_link, w.next(dve_link))
                v.tensor_tensor(yrnn, xc, gg, ALU.mult).then_inc(rnn_ready, 1)
                dve.wait_ge(rnn_ready, w.next(rnn_ready))
                skip_pairs(1)
                dve.wait_ge(hv_ready, w.next(hv_ready))
                hv_g = hv.rearrange("p (g n) -> p g n", g=NSA_KV)
                for r in range(NSA_REP):
                    ins = v.tensor_copy(hrep[:, :, r, 0:N_CMP], hv_g)
                ins.then_inc(hrep_ready, 1)
                v.memset(pc, 0.0)
                dve.wait_ge(cmp_full, w.next(cmp_full))
                v.tensor_copy(kcmp, bank[6][:, 0:NSA_KV * N_CMP])
                for g in range(NSA_KV):
                    src = bank[6][:, HD + g * HD:HD + (g + 1) * HD]
                    ins = v.tensor_tensor(v4[:, g], rows(src, NSA_REP), cols(tab("own_rep"), HD), ALU.mult)
                ins.then_inc(cmp_ready, 1)
                for qt in range(TT):
                    dve.wait_ge(cs_full, w.next(cs_full))
                    by_parity = scc.rearrange("p (h par) n -> p par h n", par=2)
                    for par in range(2):
                        src = bank[par][:, 0:NSA_HEADS // 2 * CMP_ROOM].rearrange(
                            "p (h n) -> p h n", n=CMP_ROOM)[:, :, 0:N_CMP]
                        ins = v.scalar_tensor_tensor(by_parity[:, par], src, SCALE,
                                                     rows(tab(f"cmp{qt}"), NSA_HEADS // 2), ALU.mult, ALU.add)
                    ins.then_inc(dve_link, 1)
                    dve.wait_ge(dve_link, w.next(dve_link))
                    mx, sm = nmax[:, 0:NSA_HEADS], rsum[:, 0:NSA_HEADS]
                    v.tensor_reduce(mx, scc, X_AXIS, ALU.max).then_inc(dve_link, 1)
                    dve.wait_ge(dve_link, w.next(dve_link))
                    v.tensor_tensor(scc, scc, cols(mx, N_CMP), ALU.subtract).then_inc(cs_ready, 1)
                    dve.wait_ge(cp_ready, w.next(cp_ready))
                    v.tensor_reduce(sm, pc[:, :, 0:N_CMP], X_AXIS, ALU.add).then_inc(dve_link, 1)
                    dve.wait_ge(dve_link, w.next(dve_link))
                    rc = rrec[:, 0:NSA_HEADS]
                    v.reciprocal(rc, sm).then_inc(dve_link, 1)
                    dve.wait_ge(dve_link, w.next(dve_link))
                    gate = glog[:, qt, :].rearrange("p (h b) -> p b h", b=3)[:, 0]
                    v.scalar_tensor_tensor(rc, rc, tab(f"seen{qt}"), gate, ALU.mult, ALU.mult).then_inc(dve_link, 1)
                    dve.wait_ge(dve_link, w.next(dve_link))
                    dve.wait_ge(co_full, w.next(co_full))
                    for b in range(2):
                        ins = v.tensor_tensor(
                            y2t[:, qt, b * 512:(b + 1) * 512].rearrange("p (h d) -> p h d", h=8),
                            bank[6 + b][:, :].rearrange("p (h d) -> p h d", h=8), cols(rc[:, 8 * b:8 * b + 8], HD),
                            ALU.mult)
                    ins.then_inc(co_free, 1)
                dve.wait_ge(co_free, w.next(co_free, TT))

                def add_branches(lot):
                    qt, g = lot // NSA_KV, lot % NSA_KV
                    k0, n = 2 * NSA_REP * lot, 2 * NSA_REP
                    dve.wait_ge(o_full, w.next(o_full, NSA_REP))
                    v.reciprocal(rrec[:, k0:k0 + n], rsum[:, k0:k0 + n]).then_inc(dve_link, 1)
                    dve.wait_ge(dve_link, w.next(dve_link))
                    gate = glog[:, qt, 3 * NSA_REP * g:3 * NSA_REP * (g + 1)].rearrange("p (r b) -> p r b", b=3)
                    rc = rrec[:, k0:k0 + n].rearrange("p (r b) -> p r b", b=2)
                    v.tensor_tensor(rc, rc, gate[:, :, 1:3], ALU.mult).then_inc(dve_link, 1)
                    dve.wait_ge(dve_link, w.next(dve_link))
                    v.tensor_tensor(otmp.rearrange("p (k d) -> p k d", d=HD),
                                    bank[6 + lot % 2][:, :].rearrange("p (k d) -> p k d", d=HD),
                                    cols(rrec[:, k0:k0 + n], HD), ALU.mult).then_inc(o_free, 1)
                    dve.wait_ge(o_free, w.next(o_free))
                    o = otmp.rearrange("p (r b d) -> p b r d", b=2, d=HD)
                    y = y2t[:, qt, g * SEQ:(g + 1) * SEQ].rearrange("p (r d) -> p r d", d=HD)
                    for br in range(2):
                        ins = v.tensor_tensor(y, y, o[:, br], ALU.add)
                        ins.then_inc(dve_link, 1)
                        dve.wait_ge(dve_link, w.next(dve_link))

                lots = nsa_units // NSA_REP
                for u in range(nsa_units):
                    qt = u // NSA_HEADS
                    length = (qt + 1) * P
                    s = s2[:, u % 2, 0:2 * length].rearrange("p (b k) -> p b k", b=2)
                    dve.wait_ge(sc_full, w.next(sc_full))
                    v.scalar_tensor_tensor(s, bank[u % 2][:, 0:2 * length].rearrange("p (b k) -> p b k", b=2), SCALE,
                                           rows(tab(f"causal{qt}"), 2), ALU.mult, ALU.add).then_inc(sc_free, 1)
                    dve.wait_ge(sc_free, w.next(sc_free))
                    v.tensor_reduce(nmax[:, 2 * u:2 * u + 2], s, X_AXIS, ALU.max, negate=True).then_inc(smax, 1)
                    if u >= NSA_REP + 2 and (u - 2) % NSA_REP == 0:
                        add_branches((u - 2) // NSA_REP - 1)
                add_branches(lots - 1)
                v.memset(tiny[:, 7, :], 0.0).then_inc(y2_ready, 1)
                for i in range(KT // 2):
                    b, _ = next_pair()
                    v.tensor_copy(h[:, 2 * i:2 * i + 2, :], two(bank[b][:, :])).then_inc(y_pair, 1)

            def short_conv_mixer():
                v.memset(vpad[:, :, 0:SHORT_TAPS - 1], 0.0).then_inc(dve_link, 1)
                dve.wait_ge(dve_link, w.next(dve_link))
                for m in range(KT):
                    b, free = next_pair(False)
                    dve.wait_ge(gate_copied, w.next(gate_copied))
                    v.tensor_tensor(vpad[:, m, SHORT_TAPS - 1:SHORT_TAPS - 1 + SEQ], gate_a[:, m % 2, :], half(b, 1),
                                    ALU.mult).then_inc(free, 1)
                v.memset(tiny[:, 7, :], 0.0).then_inc(dve_link, 1)
                dve.wait_ge(dve_link, w.next(dve_link))
                for _ in depthwise(SHORT_TAPS, vpad, vconv, lambda m, k: vec("sc_conv_w", 0, m * SHORT_TAPS + k),
                                   lambda m: vec("sc_conv_b", 0, m)):
                    pass
                for i in range(KT // 2):
                    b, free = next_pair()
                    v.tensor_tensor(vconv[:, 2 * i:2 * i + 2, :], vconv[:, 2 * i:2 * i + 2, :], two(bank[b][:, :]),
                                    ALU.mult).then_inc(free, 1)
                v.memset(tiny[:, 7, :], 0.0).then_inc(bgv_ready, 1)
                for i in range(KT // 2):
                    b, _ = next_pair()
                    v.tensor_copy(h[:, 2 * i:2 * i + 2, :], two(bank[b][:, :])).then_inc(y_pair, 1)

            for l in range(DEPTH):
                scale_tiles()
                ffn()
                first_mixer(l)
                scale_tiles()
                ffn()
                mod_vectors(l)
                scale_tiles()
            if not ONLY_FIRST:
                dve.wait_ge(mod_ready, w.next(mod_ready, DEPTH))
                for l in range(DEPTH):
                    scale_tiles()
                    recurrent_nsa_mixer() if l == 0 else short_conv_mixer()
                    add_normed(modv[:, l, 2, :], x_ready)
                    scale_tiles()
                    conv_ffn(l)
                    add_normed(modv[:, l, 5, :], x_ready if l < DEPTH - 1 else out_ready)


def block_tiles(w):
    k, n = w.shape
    return w.reshape(KT, P, n // P, P).transpose(2, 1, 0, 3).reshape(n // P, P, TILE)


def weight_tiles(a):
    lots = []

    def add(t):
        lots.append(t.reshape(-1, P, TILE))

    def ffn(gate, up, down):
        g, u = block_tiles(gate), block_tiles(up)
        d = down.reshape(FT, P, TILE)
        add(g[0]), add(u[0])
        for j in range(1, FT):
            add(g[j]), add(u[j]), add(d[j - 1])
        add(d[FT - 1])

    for l in range(DEPTH):
        up = a["ffn1_w_up"][l]
        ffn(up[:, :D_FF], up[:, D_FF:], a["ffn1_w_down"][l])
        w = a["w_in"][l]
        qk = 2 * QT * P
        v1 = 3 * QT * P
        glu = block_tiles(w[:, v1:v1 + 2 * D_MODEL])
        for m in range(KT):
            add(glu[m]), add(glu[KT + m])
        add(block_tiles(w[:, :qk]))
        add(block_tiles(w[:, qk:v1]))
        add(block_tiles(w[:, v1 + 2 * D_MODEL:]))
        add(a["w_attn_proj"][l].reshape(GT, P, KT // 2, 2, P).transpose(2, 1, 3, 0, 4))
        add(block_tiles(a["w_conv_proj"][l]))
        add(block_tiles(a["w_out"][l]))
        up = a["ffn2_w_up"][l]
        ffn(up[:, :D_FF], up[:, D_FF:], a["ffn2_w_down"][l])
    if ONLY_FIRST:
        return np.concatenate(lots)
    for l in range(DEPTH):
        if l == 0:
            w = a["ab_w_in_2"][0]
            at = {}
            n = 0
            for name, width in (("xr", 1024), ("gr", 1024), ("q", 1024), ("kc", 256), ("vc", 256), ("ks", 256),
                                ("vs", 256), ("kw", 256), ("vw", 256), ("gl", 48)):
                at[name] = w[:, n:n + width]
                n += width
            for name in ("kc", "vc", "xr", "q", "ks", "kw", "gr", "vs", "vw"):
                add(block_tiles(at[name]))
            gl = np.zeros((D_MODEL, P), w.dtype)
            gl[:, :3 * NSA_HEADS] = at["gl"]
            add(block_tiles(gl))
            for name in ("lru_w_r_2", "lru_w_i_2"):
                t = np.zeros((P, KT, P), w.dtype)
                pairs = a[name][0].reshape(KT, 2, HD, HD)
                for k in range(2):
                    t[k * HD:(k + 1) * HD, :, k * HD:(k + 1) * HD] = pairs[:, k].transpose(1, 0, 2)
                add(t)
            for name in ("cmp_wk1_2", "cmp_wv1_2"):
                add(a[name][0].reshape(2, KT, P, P).transpose(0, 2, 1, 3))
            o = a["ab_w_out_2"][0]
            top, low = block_tiles(o[:D_MODEL]), block_tiles(o[D_MODEL:])
            for m in range(KT):
                add(top[m]), add(low[m])
        else:
            w = block_tiles(a["sc_w_in_2"][0])
            for m in range(KT):
                add(w[KT + m]), add(w[2 * KT + m])
            add(w[:KT])
            add(block_tiles(a["sc_w_out_2"][0]))
        ffn(a["ffn_w_gate_2"][l], a["ffn_w_up_2"][l], a["ffn_w_down_2"][l])
    return np.concatenate(lots)


def vector_table(a):
    t = np.zeros((P, N_VEC), np.float32)

    def put(name, l, value):
        t[:, VEC[name, l]:VEC[name, l] + value.shape[1]] = value

    def columns(v):
        return v.reshape(-1, P).T

    def taps(w):
        k = w.shape[0]
        return w.reshape(k, -1, P).transpose(2, 1, 0).reshape(P, -1)

    for l in range(DEPTH):
        for name in ("ffn1_norm", "mix_norm", "ffn2_norm", "final_norm", "conv_b", "conv_ln_g", "conv_ln_b",
                     "b_conv_proj"):
            put(name, l, columns(a[name][l]))
        b = columns(a["b_in"][l])
        v1 = 3 * QT
        put("b_in", l, np.concatenate([b[:, v1:v1 + 2 * KT], b[:, :2 * QT], b[:, v1 + 2 * KT:]], 1))
        for name in ("q", "k"):
            g = a[name + "_norm"][l]
            swapped = g.reshape(GROUPS, 2, HD // 2)[:, ::-1].reshape(GROUPS, HD)
            put(name + "_gain", l, np.concatenate([g, g], 1).T)
            put(name + "_gain_swapped", l, np.concatenate([swapped, swapped], 1).T)
        put("conv_w", l, taps(a["conv_w"][l]))
        put("mod_b", l, columns(a["mod_b_2"][l]))
        for name, of in (("mix_pre", "norm_mix_pre_2"), ("mix_post", "norm_mix_post_2"),
                         ("ffn_pre", "norm_ffn_pre_2"), ("ffn_post", "norm_ffn_post_2")):
            put(name, l, columns(a[of][l]))
        put("ffn_conv_w", l, taps(a["ffn_conv_w_2"][l]))
        put("ffn_conv_b", l, columns(a["ffn_conv_b_2"][l]))
    put("c", 0, columns(a["c_2"][0]))
    put("rnn_conv_w", 0, taps(a["ab_conv_w_2"][0]))
    put("rnn_conv_b", 0, columns(a["ab_conv_b_2"][0]))
    put("b_r", 0, columns(a["lru_b_r_2"][0]))
    put("b_i", 0, columns(a["lru_b_i_2"][0]))
    put("lam", 0, columns(a["lru_lam_2"][0]))
    put("sc_conv_w", 0, taps(a["sc_conv_w_2"][0]))
    put("sc_conv_b", 0, columns(a["sc_conv_b_2"][0]))
    put("pe_k", 0, a["cmp_pe_k_2"][0].reshape(CMP_BLOCK // 2, P).T)
    put("pe_v", 0, a["cmp_pe_v_2"][0].reshape(CMP_BLOCK // 2, P).T)
    put("wk2", 0, np.concatenate([a["cmp_wk2_2"][0]] * 2, 1))
    put("wv2", 0, a["cmp_wv2_2"][0])
    return t


def kernel(**inputs):
    import concourse.bacc as bacc
    from concourse.bass_utils import run_bass_kernel_spmd

    a = {name: np.asarray(value) for name, value in inputs.items()}
    v0 = 2 * QT * P
    v_bias = a["b_in"][:, v0:v0 + QT * P]
    arrays = {
        "x_fm": a["x"][0].T.reshape(KT, P, SEQ).transpose(1, 0, 2),
        "weights": weight_tiles(a),
        "vectors": vector_table(a),
        "shape_tables": shape_tables(),
        "v_bias": np.broadcast_to(v_bias[:, None, :], (DEPTH, P, QT * P)),
        "mod_w": a["mod_w_2"].reshape(DEPTH * KT, P, MOD_PARTS, TILE).transpose(0, 2, 1, 3).reshape(-1, P, TILE),
    }
    arrays = {name: np.ascontiguousarray(value) for name, value in arrays.items()}
    nc = bacc.Bacc("TRN2", target_bir_lowering=False, num_devices=1)
    args = [nc.dram_tensor(name, value.shape, F32, kind="ExternalInput").ap() for name, value in arrays.items()]
    out = nc.dram_tensor("out_fm", (P, KT, SEQ), F32, kind="ExternalOutput").ap()
    build(nc, *args, out)
    result = run_bass_kernel_spmd(nc, [arrays], core_ids=[0]).results[0]["out_fm"]
    return result.transpose(1, 0, 2).reshape(D_MODEL, SEQ).T.reshape(1, SEQ, D_MODEL)
```

```python
import math
from contextlib import ExitStack

import numpy as np
import concourse.bass as bass
from concourse import mybir

ALU = mybir.AluOpType
ACT = mybir.ActivationFunctionType
F32 = mybir.dt.float32
F32R = mybir.dt.float32r
X_AXIS = mybir.AxisListType.X

P = 128
D_MODEL = 1024
SEQ = 256
DEPTH = 2
KT = D_MODEL // P
TT = SEQ // P
D_FF = 2816
FT = D_FF // P
HD = 64
GROUPS = 3
GH = 8
GT = GH * HD // P
QT = GROUPS * GT
CONV_TAPS = 31
CONV_PAD = CONV_TAPS // 2
EPS = 1e-6
NEG = -1e30
NSA_HEADS = 16
NSA_KV = 4
NSA_REP = NSA_HEADS // NSA_KV
NSA_TILES = NSA_HEADS * HD // P
RNN_TAPS = 4
SHORT_TAPS = 3
CMP_BLOCK = 32
CMP_STRIDE = 16
N_CMP = (SEQ - CMP_BLOCK) // CMP_STRIDE + 1
HALF_BLOCK = CMP_STRIDE // 2
CMP_ROOM = 32
SCALE = 1.0 / math.sqrt(HD)
MOD_PARTS = 6

RAW = 6
SPLIT = 3
TILE = KT * P

TAPS_GLU, TAPS_Q, TAPS_K, TAPS_V, TAPS_HEADS, TAPS_GATES = 8, 8, 1, 6, 6, 10



class Count:

    def __init__(self):
        self.count, self.now, self.per, self.before = {}, None, {}, {}

    def next(self, sem, k=1):
        self.count[sem.name] = n = self.count.get(sem.name, 0) + k
        return n if self.now is None else self.now * self.per[sem.name] + n

    def last(self, sem):
        return self.count[sem.name]

    def skip(self, sem, k):
        self.count[sem.name] = self.count.get(sem.name, 0) + k

    def turn(self, i, per):
        self.now, self.per = i, {sem.name: k for sem, k in per}
        self.before = {name: self.count.get(name, 0) for name in self.per}

    def turned(self, number):
        for name, k in self.per.items():
            asked = self.count.get(name, 0) - self.before[name]
            assert asked == k, (name, asked, k)
            self.count[name] = self.before[name] + k * number
        self.now = None


def vector_columns():
    at, n = {}, 0
    for l in range(DEPTH):
        for name, width in (("ffn1_norm", KT), ("mix_norm", KT), ("ffn2_norm", KT), ("final_norm", KT),
                            ("b_in", 2 * QT + 4 * KT), ("q_gain", GROUPS), ("q_gain_swapped", GROUPS),
                            ("k_gain", GROUPS), ("k_gain_swapped", GROUPS), ("conv_w", KT * CONV_TAPS),
                            ("conv_b", KT), ("conv_ln_g", KT), ("conv_ln_b", KT), ("b_conv_proj", KT),
                            ("mod_b", MOD_PARTS * KT), ("mix_pre", KT), ("mix_post", KT), ("ffn_pre", KT),
                            ("ffn_post", KT), ("ffn_conv_w", FT * SHORT_TAPS), ("ffn_conv_b", FT)):
            at[name, l] = n
            n += width
    for name, width in (("c", KT), ("rnn_conv_w", KT * RNN_TAPS), ("rnn_conv_b", KT), ("b_r", KT), ("b_i", KT),
                        ("lam", KT), ("sc_conv_w", KT * SHORT_TAPS), ("sc_conv_b", KT), ("pe_k", CMP_BLOCK // 2),
                        ("pe_v", CMP_BLOCK // 2), ("wk2", P), ("wv2", HD)):
        at[name, 0] = n
        n += width
    return at, n


VEC, N_VEC = vector_columns()

TABLES, N_TAB = {}, 0
for _name, _width in (("mean_all", P), ("one", 1), ("eps", 1),
                      ("identity", P), ("mean_head", P), ("rot", P), ("rot16", P),
                      ("dup0", P), ("dup1", P), ("rotdup0", P), ("rotdup1", P),
                      ("cos", SEQ), ("sin", SEQ), ("cos16", SEQ), ("sin16", SEQ),
                      ("mask0", 4 * P), ("mask1", 4 * P), ("causal0", P), ("causal1", 2 * P),
                      ("cmp0", N_CMP), ("cmp1", N_CMP), ("seen0", 1), ("seen1", 1),
                      ("own_rep", NSA_REP)):
    TABLES[_name] = (N_TAB, _width)
    N_TAB += _width


NORM_TAB = P + 2


def residue_order():
    return np.arange(SEQ).reshape(SEQ // 4, 2, 2).transpose(1, 0, 2).reshape(-1)


def shape_tables():
    t = {}
    eye = np.eye(P, dtype=np.float64)
    t["identity"] = eye
    t["mean_all"] = np.full((P, P), 1.0 / D_MODEL)
    head = np.kron(np.eye(P // HD), np.ones((HD, HD)))
    t["mean_head"] = head / HD

    def rotation(half):
        r = np.zeros((HD, HD))
        for d in range(half):
            r[d + half, d] = -1.0
            r[d, d + half] = 1.0
        return r

    rot, rot16 = rotation(HD // 2), rotation(HD // 8)
    t["rot"] = np.kron(np.eye(2), rot)
    t["rot16"] = np.kron(np.eye(2), rot16)
    for par in range(2):
        pick = np.zeros((2, 1))
        pick[par] = 1.0
        t[f"dup{par}"] = np.kron(pick, np.concatenate([np.eye(HD)] * 2, 1))
        t[f"rotdup{par}"] = np.kron(pick, np.concatenate([rot16] * 2, 1))
    pos = np.arange(SEQ, dtype=np.float32)
    inv = np.float32(10000.0) ** (-np.arange(0, HD, 2, dtype=np.float32) / np.float32(HD))
    ang = (pos[:, None] * inv[None, :]).astype(np.float32).astype(np.float64)
    order = residue_order()
    t["cos"] = np.tile(np.cos(ang).T, (4, 1))[:, order]
    t["sin"] = np.tile(np.sin(ang).T, (4, 1))[:, order]
    half = HD // 8
    inv = np.power(np.float32(500000.0), -np.arange(half, dtype=np.float32) / np.float32(half))
    ang = (pos[:, None] * inv[None, :]).astype(np.float32).astype(np.float64)
    c, s = np.ones((HD, SEQ)), np.zeros((HD, SEQ))
    c[:2 * half] = np.tile(np.cos(ang).T, (2, 1))
    s[:2 * half] = np.tile(np.sin(ang).T, (2, 1))
    t["cos16"], t["sin16"] = np.tile(c, (2, 1)), np.tile(s, (2, 1))
    for q in range(TT):
        i = order[q * P:(q + 1) * P][:, None]
        own = order[q * P:(q + 1) * P][None, :]
        blocks = []
        for (window, dil), keys in zip(((128, 1), (512, 4), (2048, 16)), (order[None, :], own, own)):
            ok = ((i - keys) % dil == 0) & (np.abs(i - keys) // dil <= window // (2 * dil))
            blocks.append(np.where(ok, 0.0, NEG))
        t[f"mask{q}"] = np.concatenate(blocks, 1)
        i = q * P + np.arange(P)[:, None]
        t[f"causal{q}"] = np.where(np.arange((q + 1) * P)[None, :] <= i, 0.0, NEG)
        end = np.arange(N_CMP)[None, :] * CMP_STRIDE + CMP_BLOCK - 1
        t[f"cmp{q}"] = np.where(end <= i, 0.0, NEG)
        t[f"seen{q}"] = (i >= CMP_BLOCK - 1).astype(np.float64)
    t["own_rep"] = np.kron(np.eye(NSA_REP), np.ones((CMP_ROOM, 1)))
    t["one"] = np.ones((P, 1))
    t["eps"] = np.full((P, 1), EPS)
    return np.concatenate([t[n] for n in TABLES], 1).astype(np.float32)


def build(nc, x_in, weights, vecs_in, tables_in, bv_in, mod_in, out):
    with ExitStack() as ctx:
        def sb(name, *shape, dt=F32):
            return ctx.enter_context(nc.sbuf_tensor(name, [P, *shape], dt))

        def sem(name):
            return ctx.enter_context(nc.semaphore(name))

        x = sb("x", KT, SEQ)
        work = sb("work", KT, SEQ)
        work_row = work[:, :, :].rearrange("p k t -> p (k t)")
        rinv = sb("rinv", SEQ)
        w_raw = sb("w_raw", RAW, TILE)
        w_hi = sb("w_hi", SPLIT, TILE, dt=F32R)
        w_lo = sb("w_lo", SPLIT, TILE, dt=F32R)
        h_hi = sb("h_hi", KT, SEQ, dt=F32R)
        h_lo = sb("h_lo", KT, SEQ, dt=F32R)
        vecs = sb("vecs", N_VEC)
        tabs = sb("tabs", N_TAB)
        gate_a = sb("gate_a", 2, SEQ)
        hid_hi = sb("hid_hi", 2, SEQ, dt=F32R)
        hid_lo = sb("hid_lo", 2, SEQ, dt=F32R)
        fpad = sb("fpad", 2, SHORT_TAPS - 1 + SEQ)
        mod_acc = sb("mod_acc", 2, D_MODEL)
        mod_w = sb("mod_w_buf", 2, TILE)
        modv = sb("modv", DEPTH, MOD_PARTS, KT)
        c_act = sb("c_act", KT)
        decay = sb("decay", KT)
        tiny = sb("tiny", 8, KT)
        nmax = sb("nmax", 2 * TT * NSA_HEADS)
        rsum = sb("rsum", 2 * TT * NSA_HEADS)
        rrec = sb("rrec", 2 * TT * NSA_HEADS)
        ARENA = 20750
        arena = sb("arena", ARENA)
        used = [0]

        def take(*shape):
            n = int(np.prod(shape))
            ap = arena[:, used[0]:used[0] + n]
            used[0] += n
            assert used[0] <= ARENA, used[0]
            if len(shape) == 2:
                return ap.rearrange("p (a b) -> p a b", a=shape[0])
            if len(shape) == 3:
                return ap.rearrange("p (a b c) -> p a b c", a=shape[0], b=shape[1])
            return ap

        upad = take(KT, SEQ + 2 * CONV_PAD)
        conv = take(KT, SEQ)
        qf = take(QT, SEQ)
        kf = take(QT, SEQ)
        vt = take(TT, QT * P)
        gates = take(2 * KT, SEQ)
        z_buf = take(2, 2 * SEQ)
        sq_buf = take(2, 2 * SEQ)
        root_buf = take(2, 2 * SEQ)
        v_bias = work_row[:, 0:QT * P]
        probs, scores_s, probs_t = sq_buf, root_buf, z_buf
        y_tm = kf[:, 0:GT, :].rearrange("p a b -> p (a b)").rearrange("p (a b) -> p a b", a=TT)
        gmix = qf[:, 0:KT, :]
        q_root = nmax[:, TT * GH:TT * GH + QT * 2 * TT]

        used[0] = 0
        zk = take(2, 2 * SEQ)
        kcs = take(2, NSA_KV, SEQ)
        xpad = take(KT, RNN_TAPS - 1 + SEQ)
        xc = take(KT, SEQ)
        qn = take(NSA_TILES, SEQ)
        qr = take(NSA_TILES, SEQ)
        kr = take(2, NSA_KV, SEQ)
        gg = take(KT, SEQ)
        vsw = take(2, TT, NSA_KV * HD)
        glog = take(TT, 3 * NSA_HEADS)
        it = take(KT, SEQ)
        th = take(KT, SEQ)
        hk = take(NSA_KV * N_CMP)
        hv = take(NSA_KV * N_CMP)
        hb = take(2)
        gg_row = gg.rearrange("p a b -> p (a b)")
        kcmp = zk[:, 0, 0:NSA_KV * N_CMP]
        hrep = gg_row[:, 0:512].rearrange("p (a b c) -> p a b c", a=NSA_KV, b=NSA_REP)
        v4 = gg_row[:, 1024:2048].rearrange("p (a b c) -> p a b c", a=NSA_KV, b=NSA_REP)
        xpad_row = xpad.rearrange("p a b -> p (a b)")
        xc_row = xc.rearrange("p a b -> p (a b)")
        den = xpad_row[:, 0:KT * SEQ].rearrange("p (a b) -> p a b", a=KT)
        s2 = xpad_row[:, 0:1024].rearrange("p (a b) -> p a b", a=2)
        p2 = xpad_row[:, 1024:2048].rearrange("p (a b) -> p a b", a=2)
        pt2 = xc_row[:, 0:1024].rearrange("p (a b) -> p a b", a=2)
        pc = xc_row[:, 1024:1536].rearrange("p (a b) -> p a b", a=NSA_HEADS)
        otmp = xc_row[:, 1536:2048]
        pct = work_row[:, 0:512]
        scc = work_row[:, 512:512 + NSA_HEADS * N_CMP].rearrange("p (a b) -> p a b", a=NSA_HEADS)
        rtmp = work_row[:, 1024:2048].rearrange("p (a b) -> p a b", a=2)
        y2t = it.rearrange("p a b -> p (a b)").rearrange("p (a b) -> p a b", a=TT)
        yrnn_out = th
        vpad, vconv = xpad, xc
        y = qn

        bank = [ctx.enter_context(nc.psum_tensor(f"bank{i}", [P, 512], F32)) for i in range(8)]
        UP = 4

        def half(b, k):
            return bank[b][:, k * SEQ:(k + 1) * SEQ]

        def two(ap):
            return ap.rearrange("p (a b) -> p a b", a=2)

        def tab(name):
            at, width = TABLES[name]
            return tabs[:, at:at + width]

        def vec(name, l, k=0, width=1):
            at = VEC[name, l] + k
            return vecs[:, at:at + width]

        def rows(ap, n):
            return ap[:, None, :].broadcast_to([P, n, ap.shape[-1]])

        def cols(ap, n):
            return ap[:, :, None].broadcast_to([P, ap.shape[1], n])

        def compression_operand():
            for kind, name in enumerate(("pe_k", "pe_v")):
                heads = slice(kind * NSA_KV, (kind + 1) * NSA_KV)
                for t in range(2):
                    at = t * (HALF_BLOCK + P)
                    pe = vec(name, 0, t * HALF_BLOCK, HALF_BLOCK)
                    yield lambda h, heads=heads, at=at: h[:, heads, at:at + HALF_BLOCK], rows(pe, NSA_KV)
                yield (lambda h, heads=heads: h[:, heads, HALF_BLOCK:HALF_BLOCK + P]), kcs[:, kind, :, 0:SEQ:2]

        x_loaded = sem("x_and_norm_tables_loaded")
        vecs_loaded = sem("vectors_loaded")
        tabs_loaded = sem("other_tables_loaded")
        w_full = [sem(f"weight_tile_full{i}") for i in range(RAW)]
        hi_ready = sem("weight_high_parts_ready")
        lo_ready = [sem(f"weight_low_part_ready{i}") for i in range(SPLIT)]
        w_used = sem("weight_tiles_used")
        pair_full = sem("pair_in_psum")
        pair_free = [sem(f"pair_bank_free{i}") for i in range(2)]
        dve_link = sem("dve_result_written")
        act_link = sem("act_result_written")
        pool_link = sem("pool_result_written")
        sq_ready = sem("squares_ready")
        stat_full = sem("mean_square_in_psum")
        root_ready = sem("root_ready")
        scaled = sem("tile_scaled_by_rinv")
        h_ready = sem("normed_tile_ready")
        x_ready = sem("x_tiles_updated")
        y_pair = sem("mixer_output_pair_taken")
        y_down = sem("ffn_output_bank_taken")
        gate_ready = sem("activated_gate_ready")
        gate_copied = sem("gate_tile_copied")
        gate_convolved = sem("gate_tile_convolved")
        hid_ready = sem("hidden_tile_ready")
        down_full = sem("down_bank_full")
        v_bias_full = sem("v_bias_loaded")
        high_ready = sem("high_part_ready")
        hm_full = sem("head_mean_in_psum")
        hm_root = sem("head_root_ready")
        rot_full = sem("rotated_in_psum")
        rot_free = sem("rotation_bank_free")
        qk_ready = sem("q_or_k_pair_ready")
        conv_link = sem("conv_tap_added")
        conv_ready = sem("convolution_ready")
        cmean_full = sem("conv_mean_in_psum")
        centred = sem("conv_centred")
        csq_ready = sem("conv_squares_ready")
        cvar_full = sem("conv_variance_in_psum")
        croot = sem("conv_root_ready")
        cnorm = sem("conv_normed")
        csilu = sem("conv_activated")
        sc_full = sem("scores_in_psum")
        sc_free = sem("scores_taken")
        smax = sem("score_maximum_ready")
        p_ready = sem("probabilities_ready")
        pt_full = sem("probabilities_turned_in_psum")
        pt_ready = sem("probabilities_turned_ready")
        o_full = sem("head_output_in_psum")
        o_free = sem("head_output_taken")
        ytm_ready = sem("attention_rows_ready")
        yt_full = sem("attention_turned_in_psum")
        ya_ready = sem("attention_turned_ready")
        csplit = sem("conv_output_split")
        gmix_sum = sem("gated_mix_summed")
        gmix_ready = sem("gated_mix_split")
        kcs_split = sem("doubled_kv_split")
        xc_sum = sem("recurrence_input_convolved")
        yrnn_ready = sem("recurrence_output_split")
        vc_sum = sem("short_conv_multiplied")
        res_pair = sem("residual_pair_added")
        lam_ready = sem("lam_magnitude_ready")
        lam_exp = sem("lam_exponential_ready")
        decay_ready = sem("decay_ready")
        c_ready = sem("c_activated")
        mod_w_full = [sem(f"mod_weight_full{i}") for i in range(2)]
        mod_acc_ready = sem("mod_products_ready")
        mod_col_full = sem("mod_columns_in_psum")
        mod_ready = sem("mod_vectors_ready")
        kdup_full = sem("doubled_kv_in_psum")
        kcs_ready = sem("doubled_kv_ready")
        xc_ready = sem("recurrence_input_ready")
        qrot_full = sem("nsa_q_rotated_in_psum")
        qrot_free = sem("nsa_q_rotation_taken")
        kr_full = sem("nsa_k_rotated_in_psum")
        kr_ready = sem("nsa_k_ready")
        th_ready = sem("decay_tanh_ready")
        amp_ready = sem("input_amplitude_ready")
        rnn_ready = sem("recurrence_ready")
        hk_ready = sem("compressed_k_hidden_ready")
        hv_ready = sem("compressed_v_hidden_ready")
        hrep_ready = sem("compressed_v_hidden_repeated")
        cmp_full = sem("compressed_kv_in_psum")
        cmp_ready = sem("compressed_kv_ready")
        cs_full = sem("compressed_scores_in_psum")
        cs_ready = sem("compressed_scores_ready")
        cp_ready = sem("compressed_probabilities_ready")
        cpt_full = sem("compressed_probabilities_turned_in_psum")
        cpt_ready = sem("compressed_probabilities_turned_ready")
        co_full = sem("compressed_output_in_psum")
        co_free = sem("compressed_output_taken")
        y2_ready = sem("nsa_rows_ready")
        yfm_full = sem("nsa_turned_in_psum")
        yfm_ready = sem("nsa_turned_ready")
        bgv_ready = sem("short_conv_gated")
        out_ready = sem("output_ready")
        out_done = sem("output_stored")

        block = ctx.enter_context(nc.Block())
        N_TILES = weights.shape[0]
        units = TT * GH
        LN_MEAN, LN_VAR = 2, 4
        nsa_units = TT * NSA_HEADS

        @block.sync
        def _(sp):
            w = Count()
            sp.dma_start(x[:, :, :], x_in).then_inc(x_loaded, 16)
            sp.dma_start(tabs[:, 0:NORM_TAB], tables_in[:, 0:NORM_TAB]).then_inc(x_loaded, 16)
            sp.dma_start(vecs[:, :], vecs_in).then_inc(vecs_loaded, 16)
            for n in range(RAW):
                sp.dma_start(w_raw[:, n, :], weights[n]).then_inc(w_full[n], 16)
                if n == SPLIT - 1:
                    sp.dma_start(tabs[:, NORM_TAB:], tables_in[:, NORM_TAB:]).then_inc(tabs_loaded, 16)
            whole = N_TILES // RAW
            with sp.Fori(1, whole) as i:
                for n in range(RAW):
                    sp.wait_ge(lo_ready[n % SPLIT], i * (RAW // SPLIT) + (n // SPLIT + 1 - RAW // SPLIT))
                    tile = weights[bass.ds(i * RAW + n, 1)].rearrange("a p w -> (a p) w")
                    sp.dma_start(w_raw[:, n, :], tile).then_inc(w_full[n], 16)
            for n in range(whole * RAW, N_TILES):
                sp.wait_ge(lo_ready[n % SPLIT], (n - RAW) // SPLIT + 1)
                sp.dma_start(w_raw[:, n % RAW, :], weights[n]).then_inc(w_full[n % RAW], 16)
            sp.wait_ge(out_ready, w.next(out_ready))
            sp.dma_start(out, x[:, :, :]).then_inc(out_done, 16)
            sp.wait_ge(out_done, w.next(out_done, 16))

        @block.gpsimd
        def _(pool):
            w = Count()
            state = {"tile": SPLIT - 1}

            def low_part():
                n = state["tile"]
                pool.wait_ge(hi_ready, w.next(hi_ready, SPLIT))
                nc.gpsimd.tensor_tensor(w_lo[:, SPLIT - 1, :], w_raw[:, n % RAW, :],
                                        w_hi[:, SPLIT - 1, :].bitcast(F32), ALU.subtract
                                        ).then_inc(lo_ready[SPLIT - 1], 1)
                state["tile"] += SPLIT

            def load(part, kt):
                if isinstance(part, int):
                    src = mod_in[part * KT + kt]
                else:
                    src = mod_in[bass.ds(part * KT + kt, 1)].rearrange("a p w -> (a p) w")
                pool.dma_start(mod_w[:, kt % 2, :], src).then_inc(mod_w_full[kt % 2], 16)

            def two_parts(part):
                for k in range(2):
                    acc = mod_acc[:, k, :]
                    load(part + k, 0)
                    load(part + k, 1)
                    for kt in range(KT):
                        low_part()
                        if kt == 0 and not (isinstance(part, int) and part == 0):
                            pool.wait_ge(mod_col_full, w.next(mod_col_full))
                        pool.wait_ge(mod_w_full[kt % 2], w.next(mod_w_full[kt % 2], 16))
                        if isinstance(part, int) and part + k + kt == 0:
                            pool.wait_ge(c_ready, w.next(c_ready))
                        terms = mod_w[:, kt % 2, :]
                        nc.gpsimd.tensor_tensor(terms if kt else acc, terms,
                                                c_act[:, kt:kt + 1].broadcast_to([P, TILE]), ALU.mult
                                                ).then_inc(pool_link, 1)
                        pool.wait_ge(pool_link, w.next(pool_link))
                        if kt % 2 == 0:
                            low_part()
                        if kt:
                            last = kt == KT - 1
                            nc.gpsimd.tensor_tensor(acc, acc, terms, ALU.add
                                                    ).then_inc(mod_acc_ready if last else pool_link, 1)
                            if last:
                                pool.wait_ge(mod_acc_ready, w.next(mod_acc_ready))
                            else:
                                pool.wait_ge(pool_link, w.next(pool_link))
                        if kt + 2 < KT:
                            load(part + k, kt + 2)

            two_parts(0)
            with pool.Fori(1, DEPTH * MOD_PARTS // 2) as i:
                w.turn(i - 1, [(hi_ready, 24 * SPLIT), (mod_col_full, 2), (mod_w_full[0], 128), (mod_w_full[1], 128),
                               (pool_link, 28), (mod_acc_ready, 2)])
                two_parts(i * 2)
            w.turned(DEPTH * MOD_PARTS // 2 - 1)
            done = 24 * DEPTH * MOD_PARTS // 2
            left = (N_TILES - (SPLIT - 1) + SPLIT - 1) // SPLIT - done
            with pool.Fori(0, left // 2) as i:
                w.turn(i, [(hi_ready, 2 * SPLIT)])
                low_part()
                low_part()
            w.turned(left // 2)
            if left % 2:
                low_part()

        @block.tensor
        def _(pe):
            w = Count()
            state = {"tile": 0, "pair": 0, "part": 0, "release": False}
            owed = [None, None]
            pe.wait_ge(x_loaded, w.next(x_loaded, 32))

            def mm(o, lhs, rhs, start=True, stop=True, sig=None, share=False):
                ins = pe.matmul(o, lhs, rhs, start=start, stop=stop, skip_group_check=share)
                if sig is not None:
                    ins.then_inc(sig, 1)
                elif state["release"]:
                    ins.then_inc(w_used, 1)
                    state["release"] = False
                return ins

            def slot():
                n = state["tile"] % SPLIT
                pe.wait_ge(lo_ready[n], w.next(lo_ready[n]))
                state["tile"] += 1
                return n

            def slot_done():
                assert not state["release"]
                state["release"] = True

            def product(o, n, k, hi, lo, first, last, sig=None, share=False):
                at = slice(k * P, k * P + P)
                mm(o, w_hi[:, n, at], hi, first, False, share=share)
                mm(o, w_hi[:, n, at], lo, False, False, share=share)
                mm(o, w_lo[:, n, at], hi, False, last, sig, share)

            def pair_bank(frees="pair"):
                k = state["pair"] % 2
                if owed[k] is not None:
                    pe.wait_ge(owed[k], w.next(owed[k]))
                owed[k] = pair_free[k] if frees == "pair" else frees
                state["pair"] += 1
                return UP + k

            def column(o, each=None, sig=None, order=range(KT), hi=h_hi, lo=h_lo):
                n = slot()
                for k, kt in enumerate(order):
                    if each is not None:
                        pe.wait_ge(each, w.next(each))
                    product(o, n, kt, hi[:, kt, :], lo[:, kt, :], k == 0, k == KT - 1,
                            sig if k == KT - 1 else None)
                slot_done()

            def column_pair(each=None, frees="pair", order=range(KT)):
                b = pair_bank(frees)
                column(half(b, 0), each, order=order)
                column(half(b, 1), sig=pair_full, order=order)

            def mean_squares():
                for kt in range(KT):
                    pe.wait_ge(sq_ready, w.next(sq_ready))
                    mm(half(6, 0), tab("mean_all"), work[:, kt, :], kt == 0, kt == KT - 1,
                       stat_full if kt == KT - 1 else None)

            def ffn():
                def down(j, par, last=False):
                    n = slot()
                    pe.wait_ge(hid_ready, w.next(hid_ready))
                    for m in range(KT):
                        product(half(m // 2, m % 2), n, m, hid_hi[:, par, :], hid_lo[:, par, :],
                                j == 0 and m % 2 == 0, last, down_full if last and m % 2 else None, share=True)
                    slot_done()

                column_pair(h_ready, None)
                column_pair(None, None)
                down(0, 0)
                t0, p0 = state["tile"], state["pair"]
                with pe.Fori(0, (FT - 2) // 2) as i:
                    w.turn(i, [(s, 2) for s in lo_ready] + [(hid_ready, 2)])
                    for s in range(2):
                        column_pair(None, None)
                        down(1, (1 + s) % 2)
                w.turned((FT - 2) // 2)
                state["tile"], state["pair"] = t0 + 3 * (FT - 2), p0 + FT - 2
                down(FT - 1, (FT - 1) % 2, last=True)

            def token_product(o, tok, kt, n, at, first, last, sig=None):
                mm(o, h_hi[:, kt, tok], w_hi[:, n, at], first, False, share=True)
                mm(o, h_lo[:, kt, tok], w_hi[:, n, at], False, False, share=True)
                mm(o, h_hi[:, kt, tok], w_lo[:, n, at], False, last, sig, share=True)

            def token_pair():
                b = pair_bank()
                for c in range(2):
                    n = slot()
                    for tt in range(TT):
                        for k in range(KT // 2):
                            last = c == 1 and k == KT // 2 - 1
                            token_product(bank[b][:, tt * SEQ:(tt + 1) * SEQ], slice(tt * P, (tt + 1) * P),
                                          c * KT // 2 + k, n, slice(k * SEQ, (k + 1) * SEQ),
                                          (c, tt, k) == (0, 0, 0), last, pair_full if last and tt == TT - 1 else None)
                    slot_done()

            def branch_gates():
                b = pair_bank()
                n = slot()
                for tt in range(TT):
                    for kt in range(KT):
                        token_product(bank[b][:, tt * SEQ:tt * SEQ + 3 * NSA_HEADS], slice(tt * P, (tt + 1) * P), kt, n,
                                      slice(kt * P, kt * P + 3 * NSA_HEADS), (tt, kt) == (0, 0), kt == KT - 1,
                                      pair_full if (tt, kt) == (TT - 1, KT - 1) else None)
                slot_done()

            def turn(o, src, sig=None):
                ins = pe.transpose(o, src, tab("identity"))
                if sig is not None:
                    ins.then_inc(sig, 1)

            def first_mixer(l):
                if l == 0:
                    pe.wait_ge(tabs_loaded, w.next(tabs_loaded, 16))
                for m in range(KT):
                    column_pair(h_ready if m == 0 else None)

                def qk_stats(i):
                    k = i % 2
                    pe.wait_ge(owed[k], w.next(owed[k]))
                    owed[k] = None
                    if i >= 1:
                        pe.wait_ge(hm_root, w.next(hm_root))
                        pe.wait_ge(rot_free, w.next(rot_free))
                    if i < QT // 2:
                        for c in range(2):
                            for qt in range(TT):
                                at = (c * TT + qt) * 2
                                mm(bank[6][:, at:at + 2], sq_buf[:, i % 2, c * SEQ + qt * P:c * SEQ + (qt + 1) * P],
                                   tab("mean_head")[:, 0:P:HD], sig=hm_full if (c, qt) == (1, TT - 1) else None)
                    else:
                        mm(bank[6][:, :], tab("mean_head"), sq_buf[:, i % 2, :], sig=hm_full)
                    mm(bank[7][:, :], tab("rot"), z_buf[:, i % 2, :], sig=rot_full)

                for i in range(QT):
                    column_pair()
                    if i >= 1:
                        qk_stats(i - 1)
                mod_part()
                for i in range(QT // 2):
                    token_pair()
                    if i == 0:
                        qk_stats(QT - 1)
                pe.wait_ge(qk_ready, w.next(qk_ready, QT))
                w.skip(hm_root, 1)
                w.skip(rot_free, 1)

                def scores(u):
                    hd, qt = u // TT, u % TT
                    p0 = HD * (hd % 2)
                    if u >= 2:
                        pe.wait_ge(sc_free, w.next(sc_free))
                    for g in range(GROUPS):
                        k0, k1 = (0, SEQ) if g == 0 else (qt * P, (qt + 1) * P)
                        at = 0 if g == 0 else SEQ + (g - 1) * P
                        mm(bank[u % 2][:, at:at + k1 - k0],
                           qf[p0:p0 + HD, g * GT + hd // 2, qt * P:(qt + 1) * P],
                           kf[p0:p0 + HD, g * GT + hd // 2, k0:k1], sig=sc_full if g == GROUPS - 1 else None)

                def turns(u):
                    pe.wait_ge(p_ready, w.next(p_ready))
                    for b in range(4):
                        turn(bank[2 + u % 2][:, b * P:(b + 1) * P], probs[:, u % 2, b * P:(b + 1) * P],
                             pt_full if b == 3 else None)

                def values(u):
                    hd, qt = u // TT, u % TT
                    pe.wait_ge(pt_ready, w.next(pt_ready))
                    for b, (tt, g) in enumerate(((0, 0), (1, 0), (qt, 1), (qt, 2))):
                        mm(bank[6 + qt][:, hd * HD:(hd + 1) * HD], probs_t[:, u % 2, b * P:(b + 1) * P],
                           vt[:, tt, (g * GH + hd) * HD:(g * GH + hd + 1) * HD], b == 0, b == 3,
                           o_full if b == 3 else None)

                for u in range(units + 2):
                    if u < units:
                        scores(u)
                    if 1 <= u <= units:
                        turns(u - 1)
                    if u >= 2:
                        values(u - 2)
                pe.wait_ge(sc_free, w.next(sc_free, 2))
                for i in range(KT):
                    column_pair()
                    if i == 1:
                        pe.wait_ge(ytm_ready, w.next(ytm_ready))
                        for qt in range(TT):
                            for b in range(GT):
                                turn(bank[2 + qt][:, b * P:(b + 1) * P], y_tm[:, qt, b * P:(b + 1) * P],
                                     yt_full if (qt, b) == (TT - 1, GT - 1) else None)
                    if i == LN_MEAN:
                        pe.wait_ge(conv_ready, w.next(conv_ready))
                        for kt in range(KT):
                            mm(half(6, 0), tab("mean_all"), conv[:, kt, :], kt == 0, kt == KT - 1,
                               cmean_full if kt == KT - 1 else None)
                    if i == LN_VAR:
                        pe.wait_ge(csq_ready, w.next(csq_ready))
                        for kt in range(KT):
                            mm(half(6, 1), tab("mean_all"), work[:, kt, :], kt == 0, kt == KT - 1,
                               cvar_full if kt == KT - 1 else None)
                mod_part(7)
                pe.wait_ge(ya_ready, w.next(ya_ready))
                for i in range(KT // 2):
                    b = pair_bank()
                    n = slot()
                    for c in range(2):
                        for kt in range(GT):
                            product(half(b, c), n, c * GT + kt, h_hi[:, kt, :], h_lo[:, kt, :], kt == 0,
                                    kt == GT - 1, pair_full if (c, kt) == (1, GT - 1) else None)
                    slot_done()
                pe.wait_ge(csplit, w.next(csplit, 2))
                for i in range(KT // 2):
                    column_pair(order=list(range(GT, KT)) + list(range(GT)))
                for i in range(KT // 2):
                    column_pair(gmix_ready if i == 0 else None, res_pair)

            def mod_part(b=3):
                p = state["part"]
                state["part"] += 1
                pe.wait_ge(mod_acc_ready, w.next(mod_acc_ready))
                for c in range(KT):
                    mm(bank[b][:, c:c + 1], mod_acc[:, p % 2, c * P:(c + 1) * P], tab("one"),
                       sig=mod_col_full if c == KT - 1 else None)

            def recurrent_nsa_mixer():
                column_pair(h_ready)
                column_pair()
                column_pair()
                column_pair()
                for kind in range(2):
                    for g in range(NSA_KV):
                        mm(half(2 * kind + g // 2, g % 2), tab(f"dup{g % 2}"),
                           zk[:, kind, (g // 2) * SEQ:(g // 2 + 1) * SEQ],
                           sig=kdup_full if g == NSA_KV - 1 else None)
                column_pair()
                column_pair()

                def q_rotated(i):
                    if i >= 2:
                        pe.wait_ge(qrot_free, w.next(qrot_free))
                    mm(bank[6 + i % 2][:, :], tab("rot16"), qn[:, 2 * i:2 * i + 2, :].rearrange("p a b -> p (a b)"),
                       sig=qrot_full)

                def k_rotated(kind):
                    for g in range(NSA_KV):
                        src = zk[:, kind, (g // 2) * SEQ:(g // 2 + 1) * SEQ]
                        mm(half(g // 2, g % 2), tab(f"dup{g % 2}"), src)
                        mm(half(2 + g // 2, g % 2), tab(f"rotdup{g % 2}"), src,
                           sig=kr_full if g == NSA_KV - 1 else None)

                for i in range(4):
                    column_pair()
                    if i >= 2:
                        q_rotated(i - 2)
                for i in range(2):
                    column_pair()
                    q_rotated(2 + i)
                pe.wait_ge(kcs_ready, w.next(kcs_ready))
                for i in range(4):
                    column_pair()
                    if i == 1:
                        k_rotated(0)
                    if i == 3:
                        pe.wait_ge(kr_ready, w.next(kr_ready))
                        k_rotated(1)
                for i in range(2):
                    token_pair()
                branch_gates()
                pe.wait_ge(xc_ready, w.next(xc_ready))
                r_slot = slot()
                i_slot = slot()
                for m in range(KT):
                    b = pair_bank()
                    product(half(b, 0), r_slot, m, h_hi[:, m, :], h_lo[:, m, :], True, True)
                    product(half(b, 1), i_slot, m, h_hi[:, m, :], h_lo[:, m, :], True, True, pair_full)
                slot_done()
                pe.wait_ge(kcs_split, w.next(kcs_split))
                b = pair_bank(hv_ready)
                for kind in range(2):
                    for t in range(2):
                        n = slot()
                        at = kind * SEQ + t * NSA_KV
                        heads = slice(kind * NSA_KV, (kind + 1) * NSA_KV)
                        for k in range(KT):
                            first = t * 2 * HALF_BLOCK + k
                            pairs = slice(first, first + HALF_BLOCK * N_CMP + 1, HALF_BLOCK)
                            last = t == 1 and k == KT - 1
                            product(bank[b][:, at:at + (N_CMP + 1) * NSA_KV], n, k,
                                    h_hi[:, heads, pairs].rearrange("p g n -> p n g"),
                                    h_lo[:, heads, pairs].rearrange("p g n -> p n g"),
                                    (kind, t, k) == (0, 0, 0), last, pair_full if kind == 1 and last else None,
                                    share=True)
                            if (kind, t, k) == (0, 0, 0):
                                slot_done()
                        slot_done()
                pe.wait_ge(hk_ready, w.next(hk_ready))
                mm(bank[6][:, 0:NSA_KV * N_CMP], vec("wk2", 0, 0, P), hk)
                pe.wait_ge(hrep_ready, w.next(hrep_ready))
                for g in range(NSA_KV):
                    mm(bank[6][:, HD + g * HD:HD + (g + 1) * HD], hrep[:, g].rearrange("p a b -> p (a b)"),
                       vec("wv2", 0, 0, HD), sig=cmp_full if g == NSA_KV - 1 else None)
                pe.wait_ge(cmp_ready, w.next(cmp_ready))
                pe.wait_ge(kr_ready, w.next(kr_ready))
                for i in range(KT // 2):
                    column_pair(yrnn_ready if i == 0 else None)

                def q_half(src, hd, qt):
                    p0 = HD * (hd % 2)
                    return src[p0:p0 + HD, hd // 2, qt * P:(qt + 1) * P]

                for qt in range(TT):
                    for par in range(2):
                        for k in range(NSA_HEADS // 2):
                            hd = 2 * k + par
                            g, p0 = hd // NSA_REP, HD * par
                            mm(bank[par][:, k * CMP_ROOM:k * CMP_ROOM + N_CMP], q_half(qn, hd, qt),
                               kcmp[p0:p0 + HD, g * N_CMP:(g + 1) * N_CMP],
                               sig=cs_full if (par, k) == (1, NSA_HEADS // 2 - 1) else None)
                    pe.wait_ge(cp_ready, w.next(cp_ready))
                    for g in range(NSA_KV):
                        turn(bank[2][:, g * P:(g + 1) * P],
                             pc[:, NSA_REP * g:NSA_REP * (g + 1), :].rearrange("p a b -> p (a b)"),
                             cpt_full if g == NSA_KV - 1 else None)
                    pe.wait_ge(cpt_ready, w.next(cpt_ready))
                    if qt:
                        pe.wait_ge(co_free, w.next(co_free))
                    for g in range(NSA_KV):
                        mm(half(6 + g // 2, g % 2), pct[:, g * P:(g + 1) * P],
                           v4[:, g].rearrange("p a b -> p (a b)"), sig=co_full if g == NSA_KV - 1 else None)
                pe.wait_ge(co_free, w.next(co_free))

                def scores(u):
                    qt, hd = u // NSA_HEADS, u % NSA_HEADS
                    length, p0 = (qt + 1) * P, HD * (hd % 2)
                    if u >= 2:
                        pe.wait_ge(sc_free, w.next(sc_free))
                    for br in range(2):
                        mm(bank[u % 2][:, br * length:(br + 1) * length], q_half(qr, hd, qt),
                           kr[p0:p0 + HD, br, hd // NSA_REP, 0:length], sig=sc_full if br else None)

                def turns(u):
                    n = 2 * (u // NSA_HEADS + 1)
                    pe.wait_ge(p_ready, w.next(p_ready))
                    for b in range(n):
                        turn(bank[2 + u % 2][:, b * P:(b + 1) * P], p2[:, u % 2, b * P:(b + 1) * P],
                             pt_full if b == n - 1 else None)

                def values(u):
                    qt, hd = u // NSA_HEADS, u % NSA_HEADS
                    g, r = hd // NSA_REP, hd % NSA_REP
                    lot = u // NSA_REP
                    pe.wait_ge(pt_ready, w.next(pt_ready))
                    if r == 0 and lot >= 2:
                        pe.wait_ge(o_free, w.next(o_free))
                    for br in range(2):
                        for kt in range(qt + 1):
                            at = (r * 2 + br) * HD
                            mm(bank[6 + lot % 2][:, at:at + HD],
                               pt2[:, u % 2, (br * (qt + 1) + kt) * P:(br * (qt + 1) + kt + 1) * P],
                               vsw[:, br, kt, g * HD:(g + 1) * HD], kt == 0, kt == qt,
                               o_full if br and kt == qt else None)

                for u in range(nsa_units + 2):
                    if u < nsa_units:
                        scores(u)
                    if 1 <= u <= nsa_units:
                        turns(u - 1)
                    if u >= 2:
                        values(u - 2)
                pe.wait_ge(sc_free, w.next(sc_free, 2))
                pe.wait_ge(y2_ready, w.next(y2_ready))
                for b in range(4):
                    for k in range(4):
                        qt, f = b // 2, (b % 2) * 4 + k
                        turn(bank[b][:, k * P:(k + 1) * P], y2t[:, qt, f * P:(f + 1) * P],
                             yfm_full if k == 3 else None)
                pe.wait_ge(yfm_ready, w.next(yfm_ready))
                for i in range(KT // 2):
                    column_pair(None, y_pair)

            def short_conv_mixer():
                for m in range(KT):
                    column_pair(h_ready if m == 0 else None)
                for i in range(KT // 2):
                    column_pair(None, vc_sum)
                for i in range(KT // 2):
                    column_pair(bgv_ready if i == 0 else None, y_pair)

            for l in range(DEPTH):
                mean_squares()
                if l:
                    mod_part()
                ffn()
                mean_squares()
                mod_part()
                first_mixer(l)
                mean_squares()
                mod_part()
                ffn()
                mean_squares()
                mod_part()
            for l in range(DEPTH):
                mean_squares()
                if l == 0:
                    mod_part()
                recurrent_nsa_mixer() if l == 0 else short_conv_mixer()
                mean_squares()
                mean_squares()
                ffn()
                mean_squares()
            assert state["tile"] == N_TILES, (state["tile"], N_TILES)

        @block.scalar
        def _(act):
            w = Count()
            state = {"pair": 0, "tile": 0, "split": 0}
            act_f = nc.scalar.activation

            def first_vectors():
                act_f(c_act[:, :], vec("c", 0, 0, KT), ACT.Silu).then_inc(c_ready, 1)
                act.wait_ge(lam_ready, w.next(lam_ready))
                act_f(tiny[:, 1, :], tiny[:, 0, :], ACT.Exp, scale=-1.0).then_inc(lam_exp, 1)

            def high_parts(upto):
                while state["split"] <= min(upto, N_TILES - 1):
                    n = state["split"]
                    act.wait_ge(w_full[n % RAW], w.next(w_full[n % RAW], 16))
                    if n >= SPLIT:
                        act.wait_ge(w_used, w.next(w_used))
                    act_f(w_hi[:, n % SPLIT, :], w_raw[:, n % RAW, :], ACT.Copy).then_inc(hi_ready, 1)
                    state["split"] += 1

            def next_pair(tiles=2, wait=True):
                state["tile"] += tiles
                high_parts(state["tile"] + 1)
                if wait:
                    act.wait_ge(pair_full, w.next(pair_full))
                else:
                    w.skip(pair_full, 1)
                b = UP + state["pair"] % 2
                state["pair"] += 1
                return b, pair_free[b - UP]

            def squares(src, ready):
                for kt in range(KT):
                    if kt % 2 == 0 and ready is not None:
                        act.wait_ge(ready, w.next(ready))
                    act_f(work[:, kt, :], src[:, kt, :], ACT.Square).then_inc(sq_ready, 1)
                act.wait_ge(stat_full, w.next(stat_full))
                act_f(rinv[:, :], half(6, 0), ACT.Sqrt, bias=tab("eps")).then_inc(root_ready, 1)

            def norm(ready, shift):
                squares(x, ready)
                for kt in range(KT):
                    act.wait_ge(scaled, w.next(scaled))
                    act_f(h_hi[:, kt, :], work[:, kt, :], ACT.Identity,
                          bias=shift[:, kt:kt + 1] if shift is not None else 0.0).then_inc(high_ready, 1)
                w.skip(h_ready, KT)

            def split_high(raw, ready):
                for i in range(0, KT, 2):
                    act.wait_ge(ready, w.next(ready))
                    act_f(h_hi[:, i:i + 2, :], raw[:, i:i + 2, :], ACT.Copy).then_inc(high_ready, 1)

            def ffn_steps(step):
                t0 = state["tile"]
                high_parts(t0 + 2)
                with act.Fori(0, FT // 2 - 1) as i:
                    w.turn(i, [(pair_full, 2), (gate_convolved, 2 * (step is conv_step)), (w_used, 6)]
                           + [(s, 16) for s in w_full])
                    for j in range(2):
                        step(j, t0 + 3 * j)
                        high_parts(t0 + 3 * j + 5)
                w.turned(FT // 2 - 1)
                state["split"] += 3 * (FT - 4)
                for j in range(FT - 2, FT):
                    step(j % 2, t0 + 3 * j)
                    high_parts(min(t0 + 3 * j + 5, t0 + 3 * FT + 1))
                state["tile"], state["pair"] = t0 + 3 * FT, state["pair"] + FT

            def plain_step(par, t):
                act.wait_ge(pair_full, w.next(pair_full))
                act_f(gate_a[:, par, :], half(UP + par, 0), ACT.Silu).then_inc(gate_ready, 1)

            def conv_step(par, t):
                act.wait_ge(pair_full, w.next(pair_full))
                act_f(fpad[:, par, SHORT_TAPS - 1:], half(UP + par, 0), ACT.Copy).then_inc(gate_copied, 1)
                high_parts(t + 3)
                act.wait_ge(gate_convolved, w.next(gate_convolved))
                act_f(gate_a[:, par, :], gate_a[:, par, :], ACT.Silu).then_inc(gate_ready, 1)

            def heads(count, exponentials, turned, n_turned):
                for u in range(count + 1):
                    if u < count:
                        act.wait_ge(smax, w.next(smax))
                        exponentials(u)
                    if u >= 1:
                        act.wait_ge(pt_full, w.next(pt_full))
                        n = n_turned(u - 1)
                        act_f(turned[:, (u - 1) % 2, 0:n], bank[2 + (u - 1) % 2][:, 0:n], ACT.Copy).then_inc(pt_ready, 1)

            def first_mixer(l):
                norm(x_ready, None)
                act.wait_ge(h_ready, w.last(h_ready))
                act.dma_start(v_bias, bv_in[l]).then_inc(v_bias_full, 16)
                for m in range(KT):
                    b, _ = next_pair()
                    act_f(gate_a[:, m % 2, :], half(b, 1), ACT.Sigmoid,
                          bias=vec("b_in", l, KT + m)).then_inc(gate_ready, 1)
                    high_parts(state["tile"] + 2)

                def head_root(i):
                    act.wait_ge(hm_full, w.next(hm_full))
                    if i < QT // 2:
                        act_f(q_root[:, 4 * TT * i:4 * TT * (i + 1)], bank[6][:, 0:4 * TT], ACT.Sqrt, bias=tab("eps")
                              ).then_inc(hm_root, 1)
                    else:
                        act_f(root_buf[:, i % 2, :], bank[6][:, :], ACT.Sqrt, bias=tab("eps")).then_inc(hm_root, 1)

                for i in range(QT):
                    b, free = next_pair()
                    if i >= 1:
                        head_root(i - 1)
                    high_parts(state["tile"] + 2)
                    if i >= 2:
                        act.wait_ge(qk_ready, w.next(qk_ready))
                    for c in range(2):
                        bias = vec("b_in", l, 2 * KT + 2 * i + c)
                        act_f(z_buf[:, i % 2, c * SEQ:(c + 1) * SEQ], half(b, c), ACT.Identity, bias=bias)
                        ins = act_f(sq_buf[:, i % 2, c * SEQ:(c + 1) * SEQ], half(b, c), ACT.Square, bias=bias)
                    ins.then_inc(free, 1)
                w.skip(qk_ready, 2)
                for i in range(QT // 2):
                    next_pair(wait=False)
                    if i == 0:
                        head_root(QT - 1)
                high_parts(state["tile"] + 2)

                def exponential(u):
                    act_f(probs[:, u % 2, :], scores_s[:, u % 2, :], ACT.Exp, bias=nmax[:, u:u + 1],
                          accum_out=rsum[:, u:u + 1]).then_inc(p_ready, 1)

                heads(units, exponential, probs_t, lambda u: 4 * P)
                for i in range(KT):
                    b, free = next_pair()
                    for c in range(2):
                        ins = act_f(gates[:, 2 * i + c, :], half(b, c), ACT.Sigmoid,
                                    bias=vec("b_in", l, 2 * KT + 2 * QT + 2 * i + c))
                    ins.then_inc(free, 1)
                    if i == LN_VAR - 1:
                        act.wait_ge(centred, w.next(centred))
                        act_f(work[:, :, :], conv, ACT.Square).then_inc(csq_ready, 1)
                    if i == LN_VAR:
                        act.wait_ge(cvar_full, w.next(cvar_full))
                        act_f(rinv[:, :], half(6, 1), ACT.Sqrt, bias=tab("eps")).then_inc(croot, 1)
                    if i == LN_VAR + 1:
                        act.wait_ge(cnorm, w.next(cnorm))
                        for kt in range(KT):
                            ins = act_f(work[:, kt, :].rearrange("p (h a l) -> p h a l", h=2, l=2),
                                        conv[:, kt, :].rearrange("p (a h l) -> p h a l", h=2, l=2), ACT.Silu,
                                        scale=vec("conv_ln_g", l, kt), bias=vec("conv_ln_b", l, kt))
                        ins.then_inc(csilu, 1)
                act.wait_ge(yt_full, w.next(yt_full))
                for qt in range(TT):
                    act_f(h_hi[:, 0:GT, qt * P:(qt + 1) * P], bank[2 + qt][:, :].rearrange("p (k t) -> p k t", k=GT),
                          ACT.Copy).then_inc(high_ready, 1)
                act.wait_ge(csilu, w.next(csilu))
                act_f(h_hi[:, GT:, :], work[:, GT:, :], ACT.Copy).then_inc(high_ready, 1)
                for i in range(KT // 2):
                    next_pair(1, wait=i == KT // 2 - 1)
                act_f(h_hi[:, 0:GT, :], work[:, 0:GT, :], ACT.Copy).then_inc(high_ready, 1)
                for i in range(KT // 2):
                    next_pair(wait=i == KT // 2 - 1)
                split_high(gmix, gmix_sum)
                for i in range(KT // 2):
                    next_pair(wait=False)

            def recurrent_nsa_mixer():
                for kind in range(2):
                    b, free = next_pair()
                    act_f(zk[:, kind, :], bank[b][:, :], ACT.Copy).then_inc(free, 1)
                for i in range(KT // 2):
                    next_pair(wait=False)
                for i in range(4):
                    b, free = next_pair()
                    act_f(qn[:, 2 * i:2 * i + 2, :], two(bank[b][:, :]), ACT.Copy).then_inc(free, 1)
                for kind in range(2):
                    b, free = next_pair()
                    act_f(zk[:, kind, :], bank[b][:, :], ACT.Copy).then_inc(free, 1)
                for i in range(4):
                    b, free = next_pair()
                    act_f(gg[:, 2 * i:2 * i + 2, :], two(bank[b][:, :]), ACT.Gelu_apprx_tanh).then_inc(free, 1)
                for kind in range(2):
                    b, free = next_pair()
                    act_f(vsw[:, kind, :, :], two(bank[b][:, :]), ACT.Copy).then_inc(free, 1)
                b, free = next_pair(1)
                act_f(glog, two(bank[b][:, :])[:, :, 0:3 * NSA_HEADS], ACT.Sigmoid).then_inc(free, 1)
                act.wait_ge(xc_sum, w.next(xc_sum))
                act_f(h_hi[:, :, :], xc, ACT.Copy).then_inc(high_ready, 1)
                state["tile"] += 1
                for m in range(KT):
                    b, free = next_pair(0)
                    act_f(th[:, m, :], half(b, 0), ACT.Sigmoid, bias=vec("b_r", 0, m)).then_inc(act_link, 1)
                    act_f(it[:, m, :], half(b, 1), ACT.Sigmoid, bias=vec("b_i", 0, m)).then_inc(free, 1)
                state["tile"] += 1
                act.wait_ge(kcs_ready, w.next(kcs_ready))
                for o, src in compression_operand():
                    ins = act_f(o(h_hi), src, ACT.Copy)
                ins.then_inc(high_ready, 1)
                act.wait_ge(act_link, w.next(act_link, KT))
                act.wait_ge(decay_ready, w.next(decay_ready))
                for m in range(KT):
                    ins = act_f(th[:, m, :], th[:, m, :], ACT.Tanh, scale=decay[:, m:m + 1])
                ins.then_inc(th_ready, 1)
                act.wait_ge(th_ready, w.next(th_ready))
                act.wait_ge(kr_ready, w.next(kr_ready, 2))
                high_parts(state["tile"] + 1)
                act_f(work[:, :, :], th, ACT.Sqrt, scale=-4.0).then_inc(amp_ready, 1)
                b, _ = next_pair(4)
                for kind in range(2):
                    ins = act_f(tiny[:, 6, kind:kind + 1], bank[b][:, kind * SEQ:kind * SEQ + 1], ACT.Copy)
                ins.then_inc(act_link, 1)
                act.wait_ge(act_link, w.next(act_link))
                for kind in range(2):
                    at = kind * SEQ + (N_CMP + 1) * NSA_KV
                    ins = act_f(hb[:, kind:kind + 1], bank[b][:, at:at + 1], ACT.Identity,
                                bias=tiny[:, 6, kind:kind + 1])
                ins.then_inc(act_link, 1)
                act.wait_ge(act_link, w.next(act_link))
                for kind, o, ready in ((0, hk, hk_ready), (1, hv, hv_ready)):
                    at = kind * SEQ + NSA_KV
                    src = bank[b][:, at:at + NSA_KV * N_CMP].rearrange("p (n g) -> p g n", g=NSA_KV)
                    act_f(o.rearrange("p (g n) -> p g n", g=NSA_KV), src, ACT.Gelu_apprx_tanh,
                          bias=hb[:, kind:kind + 1]).then_inc(ready, 1)
                split_high(th, rnn_ready)
                for i in range(KT // 2):
                    next_pair(wait=False)
                for qt in range(TT):
                    act.wait_ge(cs_ready, w.next(cs_ready))
                    act_f(pc[:, :, 0:N_CMP], scc, ACT.Exp).then_inc(cp_ready, 1)
                    act.wait_ge(cpt_full, w.next(cpt_full))
                    act_f(pct, bank[2][:, :], ACT.Copy).then_inc(cpt_ready, 1)

                def exponentials(u):
                    length = (u // NSA_HEADS + 1) * P
                    for br in range(2):
                        k = 2 * u + br
                        ins = act_f(p2[:, u % 2, br * length:(br + 1) * length],
                                    s2[:, u % 2, br * length:(br + 1) * length], ACT.Exp, bias=nmax[:, k:k + 1],
                                    accum_out=rsum[:, k:k + 1])
                    ins.then_inc(p_ready, 1)

                heads(nsa_units, exponentials, pt2, lambda u: 2 * (u // NSA_HEADS + 1) * P)
                for b in range(4):
                    act.wait_ge(yfm_full, w.next(yfm_full))
                    act_f(h_hi[:, 4 * (b % 2):4 * (b % 2) + 4, (b // 2) * P:(b // 2 + 1) * P],
                          bank[b][:, :].rearrange("p (k t) -> p k t", k=4), ACT.Copy).then_inc(high_ready, 1)
                for i in range(KT // 2):
                    next_pair(wait=False)

            def short_conv_mixer():
                for m in range(KT):
                    b, _ = next_pair()
                    act_f(gate_a[:, m % 2, :], half(b, 0), ACT.Copy).then_inc(gate_copied, 1)
                for i in range(KT // 2):
                    next_pair(wait=i == KT // 2 - 1)
                split_high(vconv, vc_sum)
                for i in range(KT // 2):
                    next_pair(wait=False)

            act.wait_ge(x_loaded, w.next(x_loaded, 32))
            for l in range(DEPTH):
                norm(None if l == 0 else x_ready, None)
                if l == 0:
                    act.wait_ge(vecs_loaded, w.next(vecs_loaded, 16))
                    high_parts(2)
                    first_vectors()
                ffn_steps(plain_step)
                first_mixer(l)
                norm(res_pair, None)
                ffn_steps(plain_step)
                squares(x, x_ready)
            act.wait_ge(scaled, w.next(scaled, KT))
            for r in range(2):
                for k in range(0, KT, 4):
                    ins = act_f(x[:, k:k + 4, :].rearrange("p k (a h l) -> p h k a l", h=2, l=2)[:, r],
                                work[:, k:k + 4, r * P:(r + 1) * P].rearrange("p k (a l) -> p k a l", l=2), ACT.Copy)
            ins.then_inc(act_link, 1)
            act.wait_ge(act_link, w.next(act_link))
            for l in range(DEPTH):
                act.wait_ge(mod_ready, w.next(mod_ready, MOD_PARTS))
                norm(x_ready if l else None, modv[:, l, 0, :])
                recurrent_nsa_mixer() if l == 0 else short_conv_mixer()
                squares(y, y_pair)
                norm(x_ready, modv[:, l, 3, :])
                ffn_steps(conv_step)
                squares(y, y_down)

        @block.vector
        def _(dve):
            w = Count()
            state = {"pair": 0, "conv": 0, "tile": 0, "split": 0, "part": 0}
            v = nc.vector

            def first_vectors():
                lam = vec("lam", 0, 0, KT)
                v.scalar_tensor_tensor(tiny[:, 0, :], lam, -1.0, lam, ALU.mult, ALU.max).then_inc(lam_ready, 1)
                v.tensor_scalar(tiny[:, 5, :], lam, -1.0, 0.0, ALU.mult, ALU.max).then_inc(dve_link, 1)
                dve.wait_ge(dve_link, w.next(dve_link))
                dve.wait_ge(lam_exp, w.next(lam_exp))
                e, s, q, r = tiny[:, 1, :], tiny[:, 2, :], tiny[:, 3, :], tiny[:, 4, :]
                v.tensor_scalar(s, e, 2.0, None, ALU.add).then_inc(dve_link, 1)
                dve.wait_ge(dve_link, w.next(dve_link))
                v.reciprocal(s, s).then_inc(dve_link, 1)
                dve.wait_ge(dve_link, w.next(dve_link))
                v.tensor_tensor(s, s, e, ALU.mult).then_inc(dve_link, 1)
                dve.wait_ge(dve_link, w.next(dve_link))
                v.tensor_tensor(q, s, s, ALU.mult).then_inc(dve_link, 1)
                dve.wait_ge(dve_link, w.next(dve_link))
                v.tensor_scalar(r, q, 1.0 / 17, None, ALU.mult).then_inc(dve_link, 1)
                dve.wait_ge(dve_link, w.next(dve_link))
                for odd in range(15, 1, -2):
                    v.scalar_tensor_tensor(r, r, 1.0 / odd, q, ALU.add, ALU.mult).then_inc(dve_link, 1)
                    dve.wait_ge(dve_link, w.next(dve_link))
                v.scalar_tensor_tensor(r, r, 1.0, s, ALU.add, ALU.mult).then_inc(dve_link, 1)
                dve.wait_ge(dve_link, w.next(dve_link))
                v.scalar_tensor_tensor(r, r, 2.0, tiny[:, 5, :], ALU.mult, ALU.add).then_inc(dve_link, 1)
                dve.wait_ge(dve_link, w.next(dve_link))
                v.tensor_scalar(decay[:, :], r, -4.0, None, ALU.mult).then_inc(decay_ready, 1)
                v.memset(fpad[:, :, 0:SHORT_TAPS - 1], 0.0).then_inc(dve_link, 1)
                dve.wait_ge(dve_link, w.next(dve_link))

            def low_parts(upto):
                while state["split"] <= min(upto, N_TILES - 1):
                    n = state["split"]
                    if n % SPLIT == SPLIT - 1:
                        w.skip(hi_ready, 1)
                    else:
                        dve.wait_ge(hi_ready, w.next(hi_ready))
                        v.tensor_tensor(w_lo[:, n % SPLIT, :], w_raw[:, n % RAW, :],
                                        w_hi[:, n % SPLIT, :].bitcast(F32), ALU.subtract
                                        ).then_inc(lo_ready[n % SPLIT], 1)
                    state["split"] += 1

            def advance(tiles=2):
                state["tile"] += tiles
                low_parts(state["tile"] + 1)

            def next_pair(tiles=2, wait=True):
                advance(tiles)
                if wait:
                    dve.wait_ge(pair_full, w.next(pair_full))
                else:
                    w.skip(pair_full, 1)
                b = UP + state["pair"] % 2
                state["pair"] += 1
                return b, pair_free[b - UP]

            def skip_pairs(n, tiles=2):
                for _ in range(n):
                    next_pair(tiles, False)

            def h_low(kt, shift=0.0, done=h_ready):
                dve.wait_ge(high_ready, w.next(high_ready))
                v.scalar_tensor_tensor(h_lo[:, kt, :], work[:, kt, :], shift, h_hi[:, kt, :].bitcast(F32),
                                       ALU.add, ALU.subtract).then_inc(done, 1)

            def norm(gain, shift=None):
                dve.wait_ge(root_ready, w.next(root_ready))
                v.reciprocal(rinv[:, :], rinv[:, :]).then_inc(dve_link, 1)
                dve.wait_ge(dve_link, w.next(dve_link))
                for kt in range(KT + 2):
                    if kt < KT:
                        v.scalar_tensor_tensor(work[:, kt, :], x[:, kt, :], gain[:, kt:kt + 1], rinv[:, :],
                                               ALU.mult, ALU.mult).then_inc(scaled, 1)
                    if kt >= 2:
                        h_low(kt - 2, 0.0 if shift is None else shift[:, kt - 2:kt - 1])

            def final_norm(l):
                gain = vec("final_norm", l, 0, KT)
                dve.wait_ge(root_ready, w.next(root_ready))
                v.reciprocal(rinv[:, :], rinv[:, :]).then_inc(dve_link, 1)
                dve.wait_ge(dve_link, w.next(dve_link))
                for kt in range(KT):
                    o = x if l == 0 else work
                    ins = v.scalar_tensor_tensor(o[:, kt, :], x[:, kt, :], gain[:, kt:kt + 1], rinv[:, :],
                                                 ALU.mult, ALU.mult)
                    if l or kt % 2:
                        ins.then_inc(scaled if l else x_ready, 1)

            def split_low(raw, done):
                for kt in range(KT):
                    if kt % 2 == 0:
                        dve.wait_ge(high_ready, w.next(high_ready))
                    v.tensor_tensor(h_lo[:, kt, :], raw[:, kt, :], h_hi[:, kt, :].bitcast(F32), ALU.subtract
                                    ).then_inc(done, 1)

            def add_normed(gain, done):
                dve.wait_ge(root_ready, w.next(root_ready))
                v.reciprocal(rinv[:, :], rinv[:, :]).then_inc(dve_link, 1)
                dve.wait_ge(dve_link, w.next(dve_link))
                for kt in range(KT):
                    ins = v.scalar_tensor_tensor(work[:, kt, :], y[:, kt, :], gain[:, kt:kt + 1], rinv[:, :],
                                                 ALU.mult, ALU.mult)
                ins.then_inc(dve_link, 1)
                dve.wait_ge(dve_link, w.next(dve_link))
                for kt in range(0, KT, 2):
                    ins = v.tensor_tensor(x[:, kt:kt + 2, :], x[:, kt:kt + 2, :], work[:, kt:kt + 2, :], ALU.add)
                    if done is x_ready or kt == KT - 2:
                        ins.then_inc(done, 1)

            def hidden(par):
                g, b = gate_a[:, par, :], UP + par
                dve.wait_ge(gate_ready, w.next(gate_ready))
                v.tensor_tensor(hid_hi[:, par, :], g, half(b, 1), ALU.mult)
                v.tensor_tensor(g, g, half(b, 1), ALU.mult).then_inc(dve_link, 1)
                dve.wait_ge(dve_link, w.next(dve_link))
                v.tensor_tensor(hid_lo[:, par, :], g, hid_hi[:, par, :].bitcast(F32), ALU.subtract
                                ).then_inc(hid_ready, 1)

            def gate_conv(par, j, at_w, at_b):
                dve.wait_ge(gate_copied, w.next(gate_copied))
                g = gate_a[:, par, :]
                for k in range(SHORT_TAPS):
                    src = fpad[:, par, k:k + SEQ]
                    tap = vecs[:, bass.ds(j * SHORT_TAPS + (at_w + k), 1)]
                    if k == 0:
                        ins = v.tensor_scalar(g, src, tap, vecs[:, bass.ds(j + at_b, 1)], ALU.mult, ALU.add)
                    else:
                        ins = v.scalar_tensor_tensor(g, src, tap, g, ALU.mult, ALU.add)
                    if k < SHORT_TAPS - 1:
                        ins.then_inc(dve_link, 1)
                        dve.wait_ge(dve_link, w.next(dve_link))
                ins.then_inc(gate_convolved, 1)

            def ffn_steps(l=None):
                assert state["pair"] % 2 == 0
                t0 = state["tile"]
                links = 2 if l is None else 2 * SHORT_TAPS
                at = None if l is None else (VEC["ffn_conv_w", l], VEC["ffn_conv_b", l])
                low_parts(t0 + 2)
                with dve.Fori(0, FT // 2 - 1) as i:
                    w.turn(i, [(gate_ready, 2), (dve_link, links), (hi_ready, 6), (gate_copied, 2 * (l is not None))])
                    for j in range(2):
                        if at:
                            gate_conv(j, i * 2 + j, *at)
                            low_parts(t0 + 3 * j + 3)
                        hidden(j)
                        low_parts(t0 + 3 * j + 5)
                w.turned(FT // 2 - 1)
                state["split"] += 3 * (FT - 4)
                for j in range(FT - 2, FT):
                    if at:
                        gate_conv(j % 2, j, *at)
                        low_parts(t0 + 3 * j + 3)
                    hidden(j % 2)
                    low_parts(min(t0 + 3 * j + 5, t0 + 3 * FT + 1))
                state["tile"] = t0 + 3 * FT
                w.skip(pair_full, FT)
                state["pair"] += FT
                for b in range(4):
                    dve.wait_ge(down_full, w.next(down_full))
                    if l is None:
                        v.scalar_tensor_tensor(x[:, 2 * b:2 * b + 2, :], two(bank[b][:, :]), 0.5,
                                               x[:, 2 * b:2 * b + 2, :], ALU.mult, ALU.add).then_inc(x_ready, 1)
                    else:
                        v.tensor_copy(y[:, 2 * b:2 * b + 2, :], two(bank[b][:, :])).then_inc(y_down, 1)

            def depthwise(taps, src, dst, weight, bias):
                for m0 in range(0, KT, 2):
                    v.memset(tiny[:, 7, :], 0.0).then_inc(dve_link, 1)
                    dve.wait_ge(dve_link, w.next(dve_link))
                    for k in range(taps):
                        for m in (m0, m0 + 1):
                            if state["conv"] % (2 * taps) >= 2:
                                dve.wait_ge(conv_link, w.next(conv_link))
                            state["conv"] += 1
                            tap = weight(m, k)
                            if k == 0:
                                ins = v.tensor_scalar(dst[:, m, :], src[:, m, k:k + SEQ], tap, bias(m),
                                                      ALU.mult, ALU.add)
                            else:
                                ins = v.scalar_tensor_tensor(dst[:, m, :], src[:, m, k:k + SEQ], tap, dst[:, m, :],
                                                             ALU.mult, ALU.add)
                            ins.then_inc(conv_link, 1)
                            yield ins
                    dve.wait_ge(conv_link, w.next(conv_link, 2))

            def first_mixer(l):
                if l == 0:
                    dve.wait_ge(tabs_loaded, w.next(tabs_loaded, 16))
                norm(vec("mix_norm", l, 0, KT))
                mod_vector()
                v.memset(upad[:, :, 0:CONV_PAD], 0.0)
                v.memset(upad[:, :, CONV_PAD + SEQ:], 0.0)
                steps = depthwise(CONV_TAPS, upad, conv, lambda m, k: vec("conv_w", l, m * CONV_TAPS + k),
                                  lambda m: vec("conv_b", l, m))

                def some_taps(n):
                    for _ in range(n):
                        next(steps, None)

                for m in range(KT):
                    b, free = next_pair(wait=False)
                    dve.wait_ge(gate_ready, w.next(gate_ready))
                    tokens = upad[:, m, CONV_PAD:CONV_PAD + SEQ].rearrange("p (a h l) -> p h a l", h=2, l=2)
                    for r in range(2):
                        at = slice(r * P, (r + 1) * P)
                        ins = v.scalar_tensor_tensor(
                            tokens[:, r], half(b, 0)[:, at].rearrange("p (a l) -> p a l", l=2), vec("b_in", l, m),
                            gate_a[:, m % 2, at].rearrange("p (a l) -> p a l", l=2), ALU.add, ALU.mult)
                    ins.then_inc(free, 1)
                    if m >= 2:
                        some_taps(TAPS_GLU - TAPS_GLU // 2)
                    low_parts(state["tile"] + 2)
                    if m >= 2:
                        some_taps(TAPS_GLU // 2)

                def q_or_k(i):
                    gain, dst = ("q", qf) if i < QT // 2 else ("k", kf)
                    g, t0 = (2 * i % QT) // GT, 2 * i % QT
                    z, t2, root = z_buf[:, i % 2, :], sq_buf[:, i % 2, :], root_buf[:, i % 2, :]
                    if i < QT // 2:
                        w.skip(hm_root, 1)
                    else:
                        dve.wait_ge(hm_root, w.next(hm_root))
                        v.reciprocal(root, root)
                    low_parts(state["tile"] + 2)
                    dve.wait_ge(rot_full, w.next(rot_full))
                    v.scalar_tensor_tensor(two(t2), two(bank[7][:, :]), vec(gain + "_gain_swapped", l, g),
                                           rows(tab("sin"), 2), ALU.mult, ALU.mult).then_inc(rot_free, 1)
                    v.scalar_tensor_tensor(two(z), two(z), vec(gain + "_gain", l, g), rows(tab("cos"), 2),
                                           ALU.mult, ALU.mult).then_inc(dve_link, 1)
                    dve.wait_ge(dve_link, w.next(dve_link))
                    if i < QT // 2:
                        v.tensor_tensor(dst[:, t0:t0 + 2, :], two(z), two(t2), ALU.add).then_inc(qk_ready, 1)
                    else:
                        v.tensor_tensor(z, z, t2, ALU.add).then_inc(dve_link, 1)
                        dve.wait_ge(dve_link, w.next(dve_link))
                        v.tensor_tensor(dst[:, t0:t0 + 2, :], two(z), two(root), ALU.mult).then_inc(qk_ready, 1)

                w.skip(pair_full, QT)
                state["pair"] += QT
                advance()
                for i in range(QT):
                    advance()
                    q_or_k(i)
                    some_taps(TAPS_Q if i < QT // 2 else TAPS_K)
                    if i == QT - 2:
                        mod_vector()
                v.reciprocal(q_root, q_root).then_inc(dve_link, 1)
                dve.wait_ge(dve_link, w.next(dve_link))
                v.tensor_scalar(q_root, q_root, SCALE, None, ALU.mult).then_inc(dve_link, 1)
                dve.wait_ge(dve_link, w.next(dve_link))
                dve.wait_ge(v_bias_full, w.next(v_bias_full, 16))
                for i in range(QT // 2):
                    b, free = next_pair(2 if i else 0)
                    v.tensor_tensor(vt[:, :, i * SEQ:(i + 1) * SEQ], two(bank[b][:, :]),
                                    rows(v_bias[:, i * SEQ:(i + 1) * SEQ], TT), ALU.add).then_inc(free, 1)
                    some_taps(TAPS_V - TAPS_V // 2)
                    low_parts(state["tile"] + 2)
                    some_taps(TAPS_V // 2)

                for u in range(units):
                    dve.wait_ge(sc_full, w.next(sc_full))
                    hd, qt = u // TT, u % TT
                    for g, (a0, a1) in enumerate(((0, 2 * P), (2 * P, 3 * P), (3 * P, 4 * P))):
                        at = (g * GT + hd // 2) * 2 * TT + qt * 2 + hd % 2
                        ins = v.scalar_tensor_tensor(scores_s[:, u % 2, a0:a1], bank[u % 2][:, a0:a1],
                                                     q_root[:, at:at + 1], tab(f"mask{qt}")[:, a0:a1],
                                                     ALU.mult, ALU.add)
                    ins.then_inc(sc_free, 1)
                    dve.wait_ge(sc_free, w.next(sc_free))
                    v.tensor_reduce(nmax[:, u:u + 1], scores_s[:, u % 2, :], X_AXIS, ALU.max, negate=True
                                    ).then_inc(smax, 1)
                    some_taps(TAPS_HEADS)
                next_pair(wait=False)
                dve.wait_ge(o_full, w.next(o_full, units))
                v.reciprocal(rrec[:, 0:units], rsum[:, 0:units]).then_inc(dve_link, 1)
                dve.wait_ge(dve_link, w.next(dve_link))
                for qt in range(TT):
                    share = rrec[:, 0:units].rearrange("p (h t) -> p t h", t=TT)[:, qt]
                    ins = v.tensor_tensor(y_tm[:, qt, :].rearrange("p (h d) -> p h d", h=GH),
                                          bank[6 + qt][:, :].rearrange("p (h d) -> p h d", h=GH),
                                          cols(share, HD), ALU.mult)
                ins.then_inc(ytm_ready, 1)
                some_taps(TAPS_GATES)
                for i in range(1, KT):
                    next_pair(wait=False)
                    if i == LN_MEAN - 1:
                        some_taps(KT * CONV_TAPS)
                        v.memset(tiny[:, 7, :], 0.0).then_inc(conv_ready, 1)
                    if i == LN_MEAN:
                        dve.wait_ge(cmean_full, w.next(cmean_full))
                        v.tensor_tensor(conv, conv, half(6, 0)[:, None, :].broadcast_to([P, KT, SEQ]), ALU.subtract
                                        ).then_inc(centred, 1)
                    if i == LN_VAR:
                        dve.wait_ge(croot, w.next(croot))
                        v.reciprocal(rinv[:, :], rinv[:, :]).then_inc(dve_link, 1)
                        dve.wait_ge(dve_link, w.next(dve_link))
                        v.tensor_tensor(conv, conv, rows(rinv[:, :], KT), ALU.mult).then_inc(cnorm, 1)
                dve.wait_ge(yt_full, w.next(yt_full))
                for qt in range(TT):
                    dve.wait_ge(high_ready, w.next(high_ready))
                    at = slice(qt * P, (qt + 1) * P)
                    ins = v.tensor_tensor(h_lo[:, 0:GT, at], bank[2 + qt][:, :].rearrange("p (k t) -> p k t", k=GT),
                                          h_hi[:, 0:GT, at].bitcast(F32), ALU.subtract)
                ins.then_inc(ya_ready, 1)
                dve.wait_ge(high_ready, w.next(high_ready))
                v.tensor_tensor(h_lo[:, GT:, :], work[:, GT:, :], h_hi[:, GT:, :].bitcast(F32), ALU.subtract
                                ).then_inc(csplit, 1)
                mod_vector(7)
                for i in range(KT // 2):
                    b, free = next_pair(1)
                    v.tensor_tensor(gmix[:, 2 * i:2 * i + 2, :], two(bank[b][:, :]), gates[:, 2 * i:2 * i + 2, :],
                                    ALU.mult).then_inc(free, 1)
                dve.wait_ge(high_ready, w.next(high_ready))
                v.tensor_tensor(h_lo[:, 0:GT, :], work[:, 0:GT, :], h_hi[:, 0:GT, :].bitcast(F32), ALU.subtract
                                ).then_inc(csplit, 1)
                for i in range(KT // 2):
                    b, free = next_pair()
                    t = sq_buf[:, i % 2, :]
                    for c in range(2):
                        m = 2 * i + c
                        ins = v.scalar_tensor_tensor(t[:, c * SEQ:(c + 1) * SEQ], half(b, c), vec("b_conv_proj", l, m),
                                                     gates[:, KT + m, :], ALU.add, ALU.mult)
                        ins.then_inc(free if c else dve_link, 1)
                    dve.wait_ge(dve_link, w.next(dve_link))
                    v.memset(tiny[:, 7, :], 0.0).then_inc(dve_link, 1)
                    dve.wait_ge(dve_link, w.next(dve_link))
                    v.tensor_tensor(gmix[:, 2 * i:2 * i + 2, :], gmix[:, 2 * i:2 * i + 2, :], two(t), ALU.add
                                    ).then_inc(gmix_sum, 1)
                split_low(gmix, gmix_ready)
                for i in range(KT // 2):
                    b, _ = next_pair()
                    v.tensor_tensor(x[:, 2 * i:2 * i + 2, :], two(bank[b][:, :]), x[:, 2 * i:2 * i + 2, :], ALU.add
                                    ).then_inc(res_pair, 1)

            def mod_vector(b=3):
                l, part = divmod(state["part"], MOD_PARTS)
                state["part"] += 1
                name = {1: "mix_pre", 2: "mix_post", 4: "ffn_pre", 5: "ffn_post"}.get(part)
                o = modv[:, l, part, :]
                dve.wait_ge(mod_col_full, w.next(mod_col_full))
                v.tensor_tensor(o, bank[b][:, 0:KT], vec("mod_b", l, part * KT, KT), ALU.add
                                ).then_inc(dve_link if name else mod_ready, 1)
                if name:
                    dve.wait_ge(dve_link, w.next(dve_link))
                    v.scalar_tensor_tensor(o, o, 1.0, vec(name, l, 0, KT), ALU.add, ALU.mult).then_inc(mod_ready, 1)

            def recurrent_nsa_mixer():
                skip_pairs(2)
                v.memset(xpad[:, :, 0:RNN_TAPS - 1], 0.0)
                v.memset(kcs[HD:P, :, :, SEQ - 1:SEQ], 0.0)

                def xr_pair(i):
                    b, free = next_pair()
                    v.tensor_copy(xpad[:, 2 * i:2 * i + 2, RNN_TAPS - 1:], two(bank[b][:, :])).then_inc(free, 1)

                xr_pair(0)
                xr_pair(1)
                for kind in range(2):
                    dve.wait_ge(kdup_full, w.next(kdup_full))
                    for b in range(2):
                        src = two(bank[2 * kind + b][:, :])
                        v.tensor_copy(kcs[0:HD, kind, 2 * b:2 * b + 2, :], src[0:HD])
                        ins = v.tensor_copy(kcs[HD:P, kind, 2 * b:2 * b + 2, 0:SEQ - 1], src[HD:P, :, 1:SEQ])
                ins.then_inc(kcs_ready, 1)
                xr_pair(2)
                xr_pair(3)
                steps = depthwise(RNN_TAPS, xpad, xc, lambda m, k: vec("rnn_conv_w", 0, m * RNN_TAPS + k),
                                  lambda m: vec("rnn_conv_b", 0, m))

                def rotate_q(i):
                    dve.wait_ge(qrot_full, w.next(qrot_full))
                    t = two(rtmp[:, i % 2, :])
                    v.tensor_tensor(t, two(bank[6 + i % 2][:, :]), rows(tab("sin16"), 2), ALU.mult).then_inc(qrot_free, 1)
                    v.tensor_tensor(qr[:, 2 * i:2 * i + 2, :], qn[:, 2 * i:2 * i + 2, :], rows(tab("cos16"), 2),
                                    ALU.mult).then_inc(dve_link, 1)
                    dve.wait_ge(dve_link, w.next(dve_link))
                    v.tensor_tensor(qr[:, 2 * i:2 * i + 2, :], qr[:, 2 * i:2 * i + 2, :], t, ALU.add)

                for i in range(6):
                    skip_pairs(1)
                    if i >= 2:
                        rotate_q(i - 2)
                    for _ in range(2 * RNN_TAPS):
                        next(steps, None)
                v.memset(tiny[:, 7, :], 0.0).then_inc(xc_sum, 1)
                for kind in range(2):
                    skip_pairs(2)
                    dve.wait_ge(kr_full, w.next(kr_full))
                    for b in range(2):
                        t = two(rtmp[:, b, :])
                        o = kr[:, kind, 2 * b:2 * b + 2, :]
                        v.tensor_tensor(t, two(bank[2 + b][:, :]), rows(tab("sin16"), 2), ALU.mult)
                        v.tensor_tensor(o, two(bank[b][:, :]), rows(tab("cos16"), 2), ALU.mult).then_inc(dve_link, 1)
                        dve.wait_ge(dve_link, w.next(dve_link))
                        ins = v.tensor_tensor(o, o, t, ALU.add)
                    ins.then_inc(kr_ready, 1)
                skip_pairs(2)
                skip_pairs(1, 1)
                dve.wait_ge(high_ready, w.next(high_ready))
                v.tensor_tensor(h_lo[:, :, :], xc, h_hi[:, :, :].bitcast(F32), ALU.subtract).then_inc(xc_ready, 1)
                state["tile"] += 1
                skip_pairs(KT, 0)
                state["tile"] += 1
                dve.wait_ge(high_ready, w.next(high_ready))
                for o, src in compression_operand():
                    ins = v.tensor_tensor(o(h_lo), src, o(h_hi).bitcast(F32), ALU.subtract)
                ins.then_inc(kcs_split, 1)
                dve.wait_ge(th_ready, w.next(th_ready))
                v.tensor_scalar(den, th, -1.0, 1.0, ALU.mult, ALU.add).then_inc(dve_link, 1)
                dve.wait_ge(dve_link, w.next(dve_link))
                low_parts(state["tile"] + 1)
                for i in range(0, KT, KT // 2):
                    v.reciprocal(den[:, i:i + KT // 2], den[:, i:i + KT // 2])
                    low_parts(state["tile"] + 2 + 2 * i // KT)
                v.tensor_tensor(it, it, xc, ALU.mult).then_inc(dve_link, 1)
                dve.wait_ge(dve_link, w.next(dve_link))
                v.tensor_tensor(it, it, den, ALU.mult).then_inc(dve_link, 1)
                dve.wait_ge(dve_link, w.next(dve_link))
                dve.wait_ge(amp_ready, w.next(amp_ready))
                v.tensor_tensor(it, it, work[:, :, :], ALU.mult).then_inc(dve_link, 1)
                dve.wait_ge(dve_link, w.next(dve_link))
                v.scalar_tensor_tensor(th, th, 1.0, den, ALU.add, ALU.mult).then_inc(dve_link, 1)
                dve.wait_ge(dve_link, w.next(dve_link))
                for m in range(KT):
                    ins = v.tensor_tensor_scan(xc[:, m, :], th[:, m, :], it[:, m, :], 0.0, ALU.mult, ALU.add)
                ins.then_inc(dve_link, 1)
                dve.wait_ge(dve_link, w.next(dve_link))
                for i in range(0, KT, 2):
                    v.tensor_tensor(th[:, i:i + 2, :], xc[:, i:i + 2, :], gg[:, i:i + 2, :], ALU.mult
                                    ).then_inc(rnn_ready, 1)
                skip_pairs(1, 4)
                dve.wait_ge(rnn_ready, w.next(rnn_ready, KT // 2))
                v.memset(hrep[:, :, :, N_CMP:], 0.0)
                dve.wait_ge(hv_ready, w.next(hv_ready))
                hv_g = hv.rearrange("p (g n) -> p g n", g=NSA_KV)
                for r in range(NSA_REP):
                    ins = v.tensor_copy(hrep[:, :, r, 0:N_CMP], hv_g)
                ins.then_inc(hrep_ready, 1)
                v.memset(pc[:, :, N_CMP:], 0.0)
                split_low(th, yrnn_ready)
                dve.wait_ge(cmp_full, w.next(cmp_full))
                v.tensor_copy(kcmp, bank[6][:, 0:NSA_KV * N_CMP])
                for g in range(NSA_KV):
                    src = bank[6][:, HD + g * HD:HD + (g + 1) * HD]
                    ins = v.tensor_tensor(v4[:, g], rows(src, NSA_REP), cols(tab("own_rep"), HD), ALU.mult)
                ins.then_inc(cmp_ready, 1)
                for i in range(KT // 2):
                    b, free = next_pair()
                    v.tensor_copy(yrnn_out[:, 2 * i:2 * i + 2, :], two(bank[b][:, :])).then_inc(free, 1)
                for qt in range(TT):
                    dve.wait_ge(cs_full, w.next(cs_full))
                    by_parity = scc.rearrange("p (h par) n -> p par h n", par=2)
                    for par in range(2):
                        src = bank[par][:, 0:NSA_HEADS // 2 * CMP_ROOM].rearrange(
                            "p (h n) -> p h n", n=CMP_ROOM)[:, :, 0:N_CMP]
                        ins = v.scalar_tensor_tensor(by_parity[:, par], src, SCALE,
                                                     rows(tab(f"cmp{qt}"), NSA_HEADS // 2), ALU.mult, ALU.add)
                    ins.then_inc(dve_link, 1)
                    dve.wait_ge(dve_link, w.next(dve_link))
                    mx, sm = nmax[:, 0:NSA_HEADS], rsum[:, 0:NSA_HEADS]
                    v.tensor_reduce(mx, scc, X_AXIS, ALU.max).then_inc(dve_link, 1)
                    dve.wait_ge(dve_link, w.next(dve_link))
                    v.tensor_tensor(scc, scc, cols(mx, N_CMP), ALU.subtract).then_inc(cs_ready, 1)
                    dve.wait_ge(cp_ready, w.next(cp_ready))
                    v.tensor_reduce(sm, pc[:, :, 0:N_CMP], X_AXIS, ALU.add).then_inc(dve_link, 1)
                    dve.wait_ge(dve_link, w.next(dve_link))
                    rc = rrec[:, 0:NSA_HEADS]
                    v.reciprocal(rc, sm).then_inc(dve_link, 1)
                    dve.wait_ge(dve_link, w.next(dve_link))
                    gate = glog[:, qt, :].rearrange("p (h b) -> p b h", b=3)[:, 0]
                    v.scalar_tensor_tensor(rc, rc, tab(f"seen{qt}"), gate, ALU.mult, ALU.mult).then_inc(dve_link, 1)
                    dve.wait_ge(dve_link, w.next(dve_link))
                    dve.wait_ge(co_full, w.next(co_full))
                    for b in range(2):
                        ins = v.tensor_tensor(
                            y2t[:, qt, b * 512:(b + 1) * 512].rearrange("p (h d) -> p h d", h=8),
                            bank[6 + b][:, :].rearrange("p (h d) -> p h d", h=8), cols(rc[:, 8 * b:8 * b + 8], HD),
                            ALU.mult)
                    ins.then_inc(co_free, 1)
                dve.wait_ge(co_free, w.next(co_free, TT))

                def add_branches(lot):
                    qt, g = lot // NSA_KV, lot % NSA_KV
                    k0, n = 2 * NSA_REP * lot, 2 * NSA_REP
                    dve.wait_ge(o_full, w.next(o_full, NSA_REP))
                    v.reciprocal(rrec[:, k0:k0 + n], rsum[:, k0:k0 + n]).then_inc(dve_link, 1)
                    dve.wait_ge(dve_link, w.next(dve_link))
                    gate = glog[:, qt, 3 * NSA_REP * g:3 * NSA_REP * (g + 1)].rearrange("p (r b) -> p r b", b=3)
                    rc = rrec[:, k0:k0 + n].rearrange("p (r b) -> p r b", b=2)
                    v.tensor_tensor(rc, rc, gate[:, :, 1:3], ALU.mult).then_inc(dve_link, 1)
                    dve.wait_ge(dve_link, w.next(dve_link))
                    v.tensor_tensor(otmp.rearrange("p (k d) -> p k d", d=HD),
                                    bank[6 + lot % 2][:, :].rearrange("p (k d) -> p k d", d=HD),
                                    cols(rrec[:, k0:k0 + n], HD), ALU.mult).then_inc(o_free, 1)
                    dve.wait_ge(o_free, w.next(o_free))
                    o = otmp.rearrange("p (r b d) -> p b r d", b=2, d=HD)
                    yt = y2t[:, qt, g * SEQ:(g + 1) * SEQ].rearrange("p (r d) -> p r d", d=HD)
                    for br in range(2):
                        ins = v.tensor_tensor(yt, yt, o[:, br], ALU.add)
                        ins.then_inc(dve_link, 1)
                        dve.wait_ge(dve_link, w.next(dve_link))

                lots = nsa_units // NSA_REP
                for u in range(nsa_units):
                    qt = u // NSA_HEADS
                    length = (qt + 1) * P
                    s = s2[:, u % 2, 0:2 * length].rearrange("p (b k) -> p b k", b=2)
                    dve.wait_ge(sc_full, w.next(sc_full))
                    v.scalar_tensor_tensor(s, bank[u % 2][:, 0:2 * length].rearrange("p (b k) -> p b k", b=2), SCALE,
                                           rows(tab(f"causal{qt}"), 2), ALU.mult, ALU.add).then_inc(sc_free, 1)
                    dve.wait_ge(sc_free, w.next(sc_free))
                    v.tensor_reduce(nmax[:, 2 * u:2 * u + 2], s, X_AXIS, ALU.max, negate=True).then_inc(smax, 1)
                    if u >= NSA_REP + 2 and (u - 2) % NSA_REP == 0:
                        add_branches((u - 2) // NSA_REP - 1)
                add_branches(lots - 1)
                v.memset(tiny[:, 7, :], 0.0).then_inc(y2_ready, 1)
                for b in range(4):
                    dve.wait_ge(high_ready, w.next(high_ready))
                    k, at = slice(4 * (b % 2), 4 * (b % 2) + 4), slice((b // 2) * P, (b // 2 + 1) * P)
                    ins = v.tensor_tensor(h_lo[:, k, at], bank[b][:, :].rearrange("p (k t) -> p k t", k=4),
                                          h_hi[:, k, at].bitcast(F32), ALU.subtract)
                ins.then_inc(yfm_ready, 1)
                for i in range(KT // 2):
                    b, _ = next_pair()
                    v.tensor_tensor(y[:, 2 * i:2 * i + 2, :], two(bank[b][:, :]), yrnn_out[:, 2 * i:2 * i + 2, :],
                                    ALU.add).then_inc(y_pair, 1)

            def short_conv_mixer():
                v.memset(vpad[:, :, 0:SHORT_TAPS - 1], 0.0)
                for m in range(KT):
                    b, free = next_pair(wait=False)
                    dve.wait_ge(gate_copied, w.next(gate_copied))
                    v.tensor_tensor(vpad[:, m, SHORT_TAPS - 1:SHORT_TAPS - 1 + SEQ], gate_a[:, m % 2, :], half(b, 1),
                                    ALU.mult).then_inc(free, 1)
                steps = depthwise(SHORT_TAPS, vpad, vconv, lambda m, k: vec("sc_conv_w", 0, m * SHORT_TAPS + k),
                                  lambda m: vec("sc_conv_b", 0, m))
                next(steps)
                for i in range(KT // 2):
                    b, _ = next_pair()
                    for _ in range(2 * SHORT_TAPS):
                        next(steps, None)
                    v.tensor_tensor(vconv[:, 2 * i:2 * i + 2, :], vconv[:, 2 * i:2 * i + 2, :], two(bank[b][:, :]),
                                    ALU.mult).then_inc(vc_sum, 1)
                split_low(vconv, bgv_ready)
                for i in range(KT // 2):
                    b, _ = next_pair()
                    v.tensor_copy(y[:, 2 * i:2 * i + 2, :], two(bank[b][:, :])).then_inc(y_pair, 1)

            dve.wait_ge(x_loaded, w.next(x_loaded, 32))
            dve.wait_ge(vecs_loaded, w.next(vecs_loaded, 16))
            for l in range(DEPTH):
                norm(vec("ffn1_norm", l, 0, KT))
                if l:
                    mod_vector()
                else:
                    low_parts(2)
                    first_vectors()
                ffn_steps()
                first_mixer(l)
                norm(vec("ffn2_norm", l, 0, KT))
                mod_vector()
                ffn_steps()
                mod_vector()
                final_norm(l)
            for l in range(DEPTH):
                dve.wait_ge(mod_ready, w.next(mod_ready, MOD_PARTS))
                norm(modv[:, l, 1, :], modv[:, l, 0, :])
                if l == 0:
                    mod_vector()
                    recurrent_nsa_mixer()
                else:
                    short_conv_mixer()
                add_normed(modv[:, l, 2, :], x_ready)
                norm(modv[:, l, 4, :], modv[:, l, 3, :])
                ffn_steps(l)
                add_normed(modv[:, l, 5, :], x_ready if l < DEPTH - 1 else out_ready)


def block_tiles(w):
    k, n = w.shape
    return w.reshape(KT, P, n // P, P).transpose(2, 1, 0, 3).reshape(n // P, P, TILE)


def token_tiles(w):
    k, n = w.shape
    return w.reshape(2, KT // 2, P, n // SEQ, SEQ).transpose(3, 0, 2, 1, 4).reshape(2 * n // SEQ, P, TILE)


def weight_tiles(a):
    lots = []

    def add(t):
        lots.append(t.reshape(-1, P, TILE))

    def ffn(gate, up, down):
        g, u = block_tiles(gate), block_tiles(up)
        d = down.reshape(FT, P, TILE)
        add(g[0]), add(u[0])
        for j in range(1, FT):
            add(g[j]), add(u[j]), add(d[j - 1])
        add(d[FT - 1])

    for l in range(DEPTH):
        up = a["ffn1_w_up"][l]
        ffn(up[:, :D_FF], up[:, D_FF:], a["ffn1_w_down"][l])
        w = a["w_in"][l]
        qk = 2 * QT * P
        v1 = 3 * QT * P
        glu = block_tiles(w[:, v1:v1 + 2 * D_MODEL])
        for m in range(KT):
            add(glu[m]), add(glu[KT + m])
        add(block_tiles(w[:, :qk]))
        add(token_tiles(w[:, qk:v1]))
        add(block_tiles(w[:, v1 + 2 * D_MODEL:]))
        add(a["w_attn_proj"][l].reshape(GT, P, KT // 2, 2, P).transpose(2, 1, 3, 0, 4))
        add(block_tiles(a["w_conv_proj"][l]))
        add(block_tiles(a["w_out"][l]))
        up = a["ffn2_w_up"][l]
        ffn(up[:, :D_FF], up[:, D_FF:], a["ffn2_w_down"][l])
    for l in range(DEPTH):
        if l == 0:
            w = a["ab_w_in_2"][0]
            at = {}
            n = 0
            for name, width in (("xr", 1024), ("gr", 1024), ("q", 1024), ("kc", 256), ("vc", 256), ("ks", 256),
                                ("vs", 256), ("kw", 256), ("vw", 256), ("gl", 48)):
                at[name] = w[:, n:n + width]
                n += width
            for name in ("kc", "vc", "xr", "q", "ks", "kw", "gr"):
                add(block_tiles(at[name]))
            add(token_tiles(at["vs"]))
            add(token_tiles(at["vw"]))
            gl = np.zeros((D_MODEL, P), w.dtype)
            gl[:, :3 * NSA_HEADS] = at["gl"]
            add(block_tiles(gl))
            for name in ("lru_w_r_2", "lru_w_i_2"):
                t = np.zeros((P, KT, P), w.dtype)
                pairs = a[name][0].reshape(KT, 2, HD, HD)
                for k in range(2):
                    t[k * HD:(k + 1) * HD, :, k * HD:(k + 1) * HD] = pairs[:, k].transpose(1, 0, 2)
                add(t)
            for name in ("cmp_wk1_2", "cmp_wv1_2"):
                add(a[name][0].reshape(2, KT, P, P).transpose(0, 2, 1, 3))
            o = a["ab_w_out_2"][0]
            add(block_tiles(o[:D_MODEL]))
            add(block_tiles(o[D_MODEL:]))
        else:
            w = block_tiles(a["sc_w_in_2"][0])
            for m in range(KT):
                add(w[KT + m]), add(w[2 * KT + m])
            add(w[:KT])
            add(block_tiles(a["sc_w_out_2"][0]))
        ffn(a["ffn_w_gate_2"][l], a["ffn_w_up_2"][l], a["ffn_w_down_2"][l])
    return np.concatenate(lots)


def vector_table(a):
    t = np.zeros((P, N_VEC), np.float32)

    def put(name, l, value):
        t[:, VEC[name, l]:VEC[name, l] + value.shape[1]] = value

    def columns(v):
        return v.reshape(-1, P).T

    def taps(w):
        k = w.shape[0]
        return w.reshape(k, -1, P).transpose(2, 1, 0).reshape(P, -1)

    for l in range(DEPTH):
        for name in ("ffn1_norm", "mix_norm", "ffn2_norm", "final_norm", "conv_b", "conv_ln_g", "conv_ln_b",
                     "b_conv_proj"):
            put(name, l, columns(a[name][l]))
        b = columns(a["b_in"][l])
        v1 = 3 * QT
        put("b_in", l, np.concatenate([b[:, v1:v1 + 2 * KT], b[:, :2 * QT], b[:, v1 + 2 * KT:]], 1))
        for name in ("q", "k"):
            g = a[name + "_norm"][l]
            swapped = g.reshape(GROUPS, 2, HD // 2)[:, ::-1].reshape(GROUPS, HD)
            put(name + "_gain", l, np.concatenate([g, g], 1).T)
            put(name + "_gain_swapped", l, np.concatenate([swapped, swapped], 1).T)
        put("conv_w", l, taps(a["conv_w"][l]))
        put("mod_b", l, columns(a["mod_b_2"][l]))
        for name, of in (("mix_pre", "norm_mix_pre_2"), ("mix_post", "norm_mix_post_2"),
                         ("ffn_pre", "norm_ffn_pre_2"), ("ffn_post", "norm_ffn_post_2")):
            put(name, l, columns(a[of][l]))
        put("ffn_conv_w", l, taps(a["ffn_conv_w_2"][l]))
        put("ffn_conv_b", l, columns(a["ffn_conv_b_2"][l]))
    put("c", 0, columns(a["c_2"][0]))
    put("rnn_conv_w", 0, taps(a["ab_conv_w_2"][0]))
    put("rnn_conv_b", 0, columns(a["ab_conv_b_2"][0]))
    put("b_r", 0, columns(a["lru_b_r_2"][0]))
    put("b_i", 0, columns(a["lru_b_i_2"][0]))
    put("lam", 0, columns(a["lru_lam_2"][0]))
    put("sc_conv_w", 0, taps(a["sc_conv_w_2"][0]))
    put("sc_conv_b", 0, columns(a["sc_conv_b_2"][0]))
    put("pe_k", 0, a["cmp_pe_k_2"][0].reshape(CMP_BLOCK // 2, P).T)
    put("pe_v", 0, a["cmp_pe_v_2"][0].reshape(CMP_BLOCK // 2, P).T)
    put("wk2", 0, np.concatenate([a["cmp_wk2_2"][0]] * 2, 1))
    put("wv2", 0, a["cmp_wv2_2"][0])
    return t


def kernel(**inputs):
    import concourse.bacc as bacc
    from concourse.bass_utils import run_bass_kernel_spmd

    a = {name: np.asarray(value) for name, value in inputs.items()}
    v0 = 2 * QT * P
    v_bias = a["b_in"][:, v0:v0 + QT * P]
    arrays = {
        "x_fm": a["x"][0].T[:, residue_order()].reshape(KT, P, SEQ).transpose(1, 0, 2),
        "weights": weight_tiles(a),
        "vectors": vector_table(a),
        "shape_tables": shape_tables(),
        "v_bias": np.broadcast_to(v_bias[:, None, :], (DEPTH, P, QT * P)),
        "mod_w": a["mod_w_2"].reshape(DEPTH, KT, P, MOD_PARTS, TILE).transpose(0, 3, 1, 2, 4).reshape(-1, P, TILE),
    }
    arrays = {name: np.ascontiguousarray(value) for name, value in arrays.items()}
    nc = bacc.Bacc("TRN2", target_bir_lowering=False, num_devices=1)
    args = [nc.dram_tensor(name, value.shape, F32, kind="ExternalInput").ap() for name, value in arrays.items()]
    out = nc.dram_tensor("out_fm", (P, KT, SEQ), F32, kind="ExternalOutput").ap()
    build(nc, *args, out)
    result = run_bass_kernel_spmd(nc, [arrays], core_ids=[0]).results[0]["out_fm"]
    return result.transpose(1, 0, 2).reshape(D_MODEL, SEQ).T.reshape(1, SEQ, D_MODEL)
```
